# Optimizing a Trainium2 kernel written in Bass

```python
import math
import jax, jax.numpy as jnp
from jax import lax
import numpy as np

D_MODEL = 1024
BATCH = 1
SEQ = 256
DEPTH = 2

CHUNK = 64
HEAD_DIM = 64
N_HEADS_ATTN = 8
N_IDX_HEADS = 4
IDX_DIM = 64
TOPK_MAX = 256
Q_BLOCK = 64
N_HEADS_RET = 4
N_HEADS_MLSTM = 4
CONV_WIDTH = 4
ROPE_THETA = 10000.0
N_EXPERTS = 16
N_GROUPS = 4
EXPERTS_PER_GROUP = N_EXPERTS // N_GROUPS
TOP_K_EXPERTS = 2
D_FF_EXPERT = 256
LN_EPS = 1e-5

MIX_ATTN = N_HEADS_ATTN * HEAD_DIM
MIX_RET = N_HEADS_RET * HEAD_DIM
MIX_MLSTM = N_HEADS_MLSTM * HEAD_DIM
D_MIX = MIX_ATTN + MIX_RET + MIX_MLSTM

DEEPNORM_ALPHA = (2.0 * DEPTH) ** 0.25
DEEPNORM_BETA = (8.0 * DEPTH) ** -0.25

SPLIT_SIZES = (
    MIX_ATTN, MIX_ATTN, MIX_ATTN,
    N_IDX_HEADS * IDX_DIM, IDX_DIM, N_IDX_HEADS,
    MIX_RET, MIX_RET, MIX_RET, MIX_RET,
    MIX_MLSTM, MIX_MLSTM, MIX_MLSTM, MIX_MLSTM,
    N_HEADS_MLSTM, N_HEADS_MLSTM,
)
IN_PROJ_WIDTH = sum(SPLIT_SIZES)
SPLIT_OFFSETS = tuple(int(v) for v in np.cumsum((0,) + SPLIT_SIZES)[:-1])
SPLIT_POINTS = SPLIT_OFFSETS[1:]


def layer_norm(x, g, b):
    xf = x.astype(jnp.float32)
    mu = jnp.mean(xf, axis=-1, keepdims=True)
    var = jnp.mean(jnp.square(xf - mu), axis=-1, keepdims=True)
    return ((xf - mu) * lax.rsqrt(var + LN_EPS) * g + b).astype(x.dtype)

def head_norm(x):
    xf = x.astype(jnp.float32)
    mu = jnp.mean(xf, axis=-1, keepdims=True)
    var = jnp.mean(jnp.square(xf - mu), axis=-1, keepdims=True)
    return ((xf - mu) * lax.rsqrt(var + LN_EPS)).astype(x.dtype)

def rope_tables(positions):
    half = HEAD_DIM // 2
    inv_freq = ROPE_THETA ** (-jnp.arange(half, dtype=jnp.float32) / half)
    ang = positions.astype(jnp.float32)[..., None] * inv_freq
    return jnp.cos(ang)[:, :, None, :], jnp.sin(ang)[:, :, None, :]

def apply_rope(x, cos, sin):
    half = x.shape[-1] // 2
    x1 = x[..., :half].astype(jnp.float32)
    x2 = x[..., half:].astype(jnp.float32)
    return jnp.concatenate([x1 * cos - x2 * sin, x2 * cos + x1 * sin], axis=-1).astype(x.dtype)

def causal_conv(x, w, b):
    seq = x.shape[1]
    xp = jnp.pad(x, ((0, 0), (CONV_WIDTH - 1, 0), (0, 0)))
    out = b
    for j in range(CONV_WIDTH):
        out = out + xp[:, j:j + seq] * w[j]
    return out

def dsa_attention(q, k, v, iq, ik, iw):
    bsz, seq, n_heads, hd = q.shape
    topk = min(TOPK_MAX, seq // 4)
    n_blocks = seq // Q_BLOCK
    key_pos = jnp.arange(seq)
    iw = iw.astype(jnp.float32) * (N_IDX_HEADS ** -0.5) * (IDX_DIM ** -0.5)
    gather = jax.vmap(lambda arr, ids: arr[ids])

    def one_block(blk):
        start = blk * Q_BLOCK
        qb = lax.dynamic_slice_in_dim(q, start, Q_BLOCK, axis=1)
        iqb = lax.dynamic_slice_in_dim(iq, start, Q_BLOCK, axis=1)
        iwb = lax.dynamic_slice_in_dim(iw, start, Q_BLOCK, axis=1)
        q_pos = start + jnp.arange(Q_BLOCK)
        limit = (q_pos // CHUNK + 1) * CHUNK
        visible = key_pos[None, :] < limit[:, None]
        rel = jax.nn.relu(jnp.einsum('bqhd,bsd->bqhs', iqb, ik).astype(jnp.float32))
        score = jnp.einsum('bqhs,bqh->bqs', rel, iwb)
        score = jnp.where(visible[None], score, -jnp.inf)
        _, idx = lax.top_k(score, topk)
        valid = idx < limit[None, :, None]
        k_sel = gather(k, idx)
        v_sel = gather(v, idx)
        s = jnp.einsum('bqhd,bqkhd->bqhk', qb, k_sel).astype(jnp.float32) * (hd ** -0.5)
        s = jnp.where(valid[:, :, None, :], s, -jnp.inf)
        p = jax.nn.softmax(s, axis=-1).astype(v.dtype)
        return jnp.einsum('bqhk,bqkhd->bqhd', p, v_sel)

    out = lax.map(one_block, jnp.arange(n_blocks))
    return out.transpose(1, 0, 2, 3, 4).reshape(bsz, seq, n_heads, hd)

def retention_chunkwise(q, k, v):
    bsz, seq, nh, hd = q.shape
    dv = v.shape[-1]
    n_chunks = seq // CHUNK
    f32 = jnp.float32
    log_gamma = jnp.log1p(-(2.0 ** (-5.0 - jnp.arange(nh, dtype=f32))))

    def to_chunks(a):
        return a.astype(f32).reshape(bsz, n_chunks, CHUNK, nh, -1)

    qc = to_chunks(q)
    kc = to_chunks(k) * (hd ** -0.5)
    vc = to_chunks(v)
    pos = jnp.arange(CHUNK, dtype=f32)
    diff = pos[:, None] - pos[None, :]
    decay_in = jnp.where(diff >= 0, jnp.exp(diff[None] * log_gamma[:, None, None]), 0.0)
    scores = jnp.einsum('bnihd,bnjhd->bnhij', qc, kc) * decay_in
    inner = jnp.einsum('bnhij,bnjhe->bnihe', scores, vc)
    k_decay = jnp.exp((CHUNK - 1.0 - pos)[None, :] * log_gamma[:, None])
    chunk_kv = jnp.einsum('bnjhd,hj,bnjhe->nbhde', kc, k_decay, vc)
    chunk_decay = jnp.exp(CHUNK * log_gamma)[None, :, None, None]

    def step(state, kv):
        return state * chunk_decay + kv, state

    _, prev = lax.scan(step, jnp.zeros((bsz, nh, hd, dv), f32), chunk_kv)
    q_decay = jnp.exp((pos + 1.0)[None, :] * log_gamma[:, None])
    cross = jnp.einsum('bnihd,hi,nbhde->bnihe', qc, q_decay, prev)
    return (inner + cross).reshape(bsz, seq, nh, dv)

def mlstm_chunkwise(q, k, v, i_pre, f_pre):
    bsz, seq, nh, hd = q.shape
    n_chunks = seq // CHUNK
    f32 = jnp.float32

    def to_chunks(a):
        return a.astype(f32).reshape(bsz, n_chunks, CHUNK, nh, -1).transpose(1, 0, 3, 2, 4)

    qc = to_chunks(q)
    kc = to_chunks(k) * (hd ** -0.5)
    vc = to_chunks(v)
    ic = to_chunks(i_pre[..., None])[..., 0]
    lfc = to_chunks(jax.nn.log_sigmoid(f_pre.astype(f32))[..., None])[..., 0]
    causal = jnp.tril(jnp.ones((CHUNK, CHUNK), dtype=bool))

    def step(carry, xs):
        c_mem, n_mem, m_mem = carry
        q_, k_, v_, i_, lf_ = xs
        b = jnp.cumsum(lf_, axis=-1)
        log_w = jnp.where(causal, b[..., :, None] - b[..., None, :] + i_[..., None, :], -jnp.inf)
        log_inter = b + m_mem[..., None]
        m_q = jnp.maximum(log_inter, jnp.max(log_w, axis=-1))
        w = jnp.exp(log_w - m_q[..., None])
        inter = jnp.exp(log_inter - m_q)
        s = jnp.einsum('bhjd,bhld->bhjl', q_, k_) * w
        num = jnp.einsum('bhjl,bhle->bhje', s, v_) + inter[..., None] * jnp.einsum('bhjd,bhde->bhje', q_, c_mem)
        den = jnp.sum(s, axis=-1) + inter * jnp.einsum('bhjd,bhd->bhj', q_, n_mem)
        h = num / jnp.maximum(jnp.abs(den), jnp.exp(-m_q))[..., None]
        b_last = b[..., -1]
        log_k = b_last[..., None] - b + i_
        m_new = jnp.maximum(b_last + m_mem, jnp.max(log_k, axis=-1))
        kw = jnp.exp(log_k - m_new[..., None])
        decay = jnp.exp(b_last + m_mem - m_new)
        c_new = decay[..., None, None] * c_mem + jnp.einsum('bhl,bhld,bhle->bhde', kw, k_, v_)
        n_new = decay[..., None] * n_mem + jnp.einsum('bhl,bhld->bhd', kw, k_)
        return (c_new, n_new, m_new), h

    init = (jnp.zeros((bsz, nh, hd, hd), f32), jnp.zeros((bsz, nh, hd), f32), jnp.zeros((bsz, nh), f32))
    _, hs = lax.scan(step, init, (qc, kc, vc, ic, lfc))
    return hs.transpose(1, 0, 3, 2, 4).reshape(bsz, seq, nh, hd)

def token_mixers(h, w_in, w_out, i_bias, f_bias, conv_w, conv_b, cos, sin):
    bsz, seq, _ = h.shape
    (aq, ak, av, iq, ik, iw, rq, rk, rv, rg,
     mq, mk, mv, mo, mi, mf) = jnp.split(h @ w_in, SPLIT_POINTS, axis=-1)

    def heads(a, n):
        return a.reshape(bsz, seq, n, -1)

    o_a = dsa_attention(apply_rope(heads(aq, N_HEADS_ATTN), cos, sin),
                        apply_rope(heads(ak, N_HEADS_ATTN), cos, sin),
                        heads(av, N_HEADS_ATTN),
                        apply_rope(heads(iq, N_IDX_HEADS), cos, sin),
                        apply_rope(heads(ik, 1), cos, sin)[:, :, 0],
                        iw).reshape(bsz, seq, MIX_ATTN)
    y_r = retention_chunkwise(apply_rope(heads(rq, N_HEADS_RET), cos, sin),
                              apply_rope(heads(rk, N_HEADS_RET), cos, sin),
                              heads(rv, N_HEADS_RET))
    o_b = (head_norm(y_r).reshape(bsz, seq, MIX_RET) * jax.nn.silu(rg)).astype(h.dtype)
    qk = jax.nn.silu(causal_conv(jnp.concatenate([mq, mk], axis=-1), conv_w, conv_b))
    mq_c, mk_c = jnp.split(qk, 2, axis=-1)
    h_tilde = mlstm_chunkwise(heads(mq_c, N_HEADS_MLSTM), heads(mk_c, N_HEADS_MLSTM),
                              heads(mv, N_HEADS_MLSTM), mi + i_bias, mf + f_bias)
    h_t = jax.nn.sigmoid(heads(mo, N_HEADS_MLSTM).astype(jnp.float32)) * h_tilde
    o_c = head_norm(h_t).reshape(bsz, seq, MIX_MLSTM).astype(h.dtype)
    return jnp.concatenate([o_a, o_b, o_c], axis=-1) @ w_out

def moe_ffn(h, w_router, b_router, w_gate, w_up, w_down):
    n_tok = h.shape[0]
    scores = jax.nn.sigmoid((h @ w_router).astype(jnp.float32))
    biased = scores + b_router.astype(jnp.float32)
    grouped = biased.reshape(n_tok, N_GROUPS, EXPERTS_PER_GROUP)
    group_score = jnp.sum(lax.top_k(grouped, TOP_K_EXPERTS)[0], axis=-1)
    best_group = jnp.argmax(group_score, axis=-1)
    in_group = jnp.take_along_axis(grouped, best_group[:, None, None], axis=1)[:, 0]
    _, local = lax.top_k(in_group, TOP_K_EXPERTS)
    expert_idx = best_group[:, None] * EXPERTS_PER_GROUP + local
    wts = jnp.take_along_axis(scores, expert_idx, axis=1)
    wts = wts / jnp.sum(wts, axis=-1, keepdims=True)
    gate = jnp.einsum('tk,tke->te', wts, jax.nn.one_hot(expert_idx, N_EXPERTS, dtype=jnp.float32))
    hid = jax.nn.silu(jnp.einsum('td,edf->tef', h, w_gate)) * jnp.einsum('td,edf->tef', h, w_up)
    hid = hid * gate[:, :, None].astype(hid.dtype)
    return jnp.einsum('tef,efd->td', hid, w_down)

def first_inputs(seed: int = 0) -> dict:
    key = jax.random.key(seed)
    ks = jax.random.split(key, 20)
    f32 = jnp.float32

    def nrm(k, shape, scale):
        return jax.random.normal(k, shape, f32) * scale

    x = nrm(ks[0], (BATCH, SEQ, D_MODEL), 1.0)
    c = nrm(ks[1], (BATCH, D_MODEL), 1.0)
    offset = jax.random.randint(ks[2], (BATCH, 1), 0, 1024, dtype=jnp.int32)
    positions = offset + jnp.arange(SEQ, dtype=jnp.int32)[None, :]
    w_ada = nrm(ks[3], (DEPTH, D_MODEL, 6 * D_MODEL), 0.1 * D_MODEL ** -0.5)
    b_ada = nrm(ks[4], (DEPTH, 6 * D_MODEL), 0.02)
    col_scale = np.ones(IN_PROJ_WIDTH, np.float32)
    for part in (2, 8, 12):
        col_scale[SPLIT_OFFSETS[part]:SPLIT_OFFSETS[part] + SPLIT_SIZES[part]] = DEEPNORM_BETA
    w_in = nrm(ks[5], (DEPTH, D_MODEL, IN_PROJ_WIDTH), D_MODEL ** -0.5) * jnp.asarray(col_scale)
    i_bias = nrm(ks[6], (DEPTH, N_HEADS_MLSTM), 0.1)
    f_bias = jnp.linspace(3.0, 6.0, N_HEADS_MLSTM, dtype=f32)[None, :] + nrm(ks[7], (DEPTH, N_HEADS_MLSTM), 0.01)
    conv_w = nrm(ks[8], (DEPTH, CONV_WIDTH, 2 * MIX_MLSTM), CONV_WIDTH ** -0.5)
    conv_b = nrm(ks[9], (DEPTH, 2 * MIX_MLSTM), 0.01)
    w_out = nrm(ks[10], (DEPTH, D_MIX, D_MODEL), DEEPNORM_BETA * D_MIX ** -0.5)
    ln_mix_g = 1.0 + nrm(ks[11], (DEPTH, D_MODEL), 0.01)
    ln_mix_b = nrm(ks[12], (DEPTH, D_MODEL), 0.01)
    w_router = nrm(ks[13], (D_MODEL, N_EXPERTS), D_MODEL ** -0.5)
    b_router = nrm(ks[14], (N_EXPERTS,), 0.01)
    w_gate = nrm(ks[15], (DEPTH, N_EXPERTS, D_MODEL, D_FF_EXPERT), D_MODEL ** -0.5)
    w_up = nrm(ks[16], (DEPTH, N_EXPERTS, D_MODEL, D_FF_EXPERT), DEEPNORM_BETA * D_MODEL ** -0.5)
    w_down = nrm(ks[17], (DEPTH, N_EXPERTS, D_FF_EXPERT, D_MODEL), DEEPNORM_BETA * D_FF_EXPERT ** -0.5)
    ln_ffn_g = 1.0 + nrm(ks[18], (DEPTH, D_MODEL), 0.01)
    ln_ffn_b = nrm(ks[19], (DEPTH, D_MODEL), 0.01)
    return {'x': x, 'c': c, 'positions': positions, 'w_ada': w_ada, 'b_ada': b_ada,
            'w_in': w_in, 'i_bias': i_bias, 'f_bias': f_bias, 'conv_w': conv_w, 'conv_b': conv_b,
            'w_out': w_out, 'ln_mix_g': ln_mix_g, 'ln_mix_b': ln_mix_b,
            'w_router': w_router, 'b_router': b_router, 'w_gate': w_gate, 'w_up': w_up,
            'w_down': w_down, 'ln_ffn_g': ln_ffn_g, 'ln_ffn_b': ln_ffn_b}

def first_block(x, c, positions, w_ada, b_ada, w_in, i_bias, f_bias, conv_w, conv_b,
              w_out, ln_mix_g, ln_mix_b, w_router, b_router, w_gate, w_up, w_down,
              ln_ffn_g, ln_ffn_b):
    bsz, seq, d = x.shape
    cos, sin = rope_tables(positions)
    c_act = jax.nn.silu(c)
    for l in range(DEPTH):
        mod = (c_act @ w_ada[l] + b_ada[l])[:, None, :]
        sh_m, sc_m, g_m, sh_f, sc_f, g_f = jnp.split(mod, 6, axis=-1)
        h = x * (1.0 + sc_m) + sh_m
        mix = token_mixers(h, w_in[l], w_out[l], i_bias[l], f_bias[l], conv_w[l], conv_b[l], cos, sin)
        x = layer_norm(DEEPNORM_ALPHA * x + (1.0 + g_m) * mix, ln_mix_g[l], ln_mix_b[l])
        h = x * (1.0 + sc_f) + sh_f
        y = moe_ffn(h.reshape(bsz * seq, d), w_router, b_router, w_gate[l], w_up[l], w_down[l])
        x = layer_norm(DEEPNORM_ALPHA * x + (1.0 + g_f) * y.reshape(bsz, seq, d), ln_ffn_g[l], ln_ffn_b[l])
    return x


BLOCK = 128
DIFF_HEADS = 6
DIFF_QK_DIM = HEAD_DIM // 2
DIFF_V_DIM = HEAD_DIM
DIFF_WIDTH = DIFF_HEADS * DIFF_V_DIM
GMLP_GROUPS = 4
GMLP_GROUP_DIM = 64
GMLP_WIDTH = GMLP_GROUPS * GMLP_GROUP_DIM
CHUNK_2 = 128
SWA_HEADS = 6
SWA_KV_HEADS = 2
SWA_GROUP = SWA_HEADS // SWA_KV_HEADS
SWA_WIDTH = SWA_HEADS * HEAD_DIM
WINDOW = 128
MIX_WIDTH = DIFF_WIDTH + GMLP_WIDTH + SWA_WIDTH
IN_SIZES = (DIFF_HEADS * 2 * DIFF_QK_DIM, DIFF_HEADS * 2 * DIFF_QK_DIM, DIFF_WIDTH,
            GMLP_WIDTH, GMLP_WIDTH,
            SWA_WIDTH, SWA_KV_HEADS * HEAD_DIM, SWA_KV_HEADS * HEAD_DIM)
IN_WIDTH = 384 + 384 + 384 + 256 + 256 + 384 + 128 + 128
D_FF = ((-(-8 * D_MODEL // 3) + 255) // 256) * 256
PLE_DIM = 256
N_ATTN_HEADS = DIFF_HEADS + SWA_HEADS
ALIBI_MAX_EXP = 8.0
EPS = 1e-6
NEG_INF = -1e30


def rmsnorm(x, g):
    x32 = x.astype(jnp.float32)
    y = x32 * lax.rsqrt(jnp.mean(x32 * x32, axis=-1, keepdims=True) + EPS)
    return (y * g.astype(jnp.float32)).astype(x.dtype)

def alibi_slopes():
    k = jnp.arange(1, N_ATTN_HEADS + 1, dtype=jnp.float32)
    s = jnp.exp2(-ALIBI_MAX_EXP * k / N_ATTN_HEADS)
    return s[SWA_HEADS:], s[:SWA_HEADS]

def diff_attention(q, k, v, lam, lam_init, g_sub, slopes):
    b, s_len = q.shape[0], q.shape[1]
    nb = s_len // BLOCK
    scale = DIFF_QK_DIM ** -0.5
    key_pos = jnp.arange(s_len)
    qb = q.reshape(b, nb, BLOCK, DIFF_HEADS, 2, DIFF_QK_DIM).transpose(1, 0, 2, 3, 4, 5)

    def one_block(args):
        q_blk, j = args
        sc = jnp.einsum('bqhcd,bkhcd->bhcqk', q_blk, k,
                        preferred_element_type=jnp.float32) * scale
        q_pos = j * BLOCK + jnp.arange(BLOCK)
        dist = jnp.abs(q_pos[:, None] - key_pos[None, :]).astype(jnp.float32)
        sc = sc - slopes[None, :, None, None, None] * dist
        pr = jax.nn.softmax(sc, axis=-1)
        attn = pr[:, :, 0] - lam * pr[:, :, 1]
        return jnp.einsum('bhqk,bkhd->bqhd', attn.astype(v.dtype), v)

    o = lax.map(one_block, (qb, jnp.arange(nb)))
    o = o.transpose(1, 0, 2, 3, 4).reshape(b, s_len, DIFF_HEADS, DIFF_V_DIM)
    o = rmsnorm(o, g_sub) * (1.0 - lam_init)
    return o.reshape(b, s_len, DIFF_WIDTH)

def spatial_gating(u, v, ln_g, ln_b, w_s, b_s):
    b, s_len = u.shape[0], u.shape[1]
    v32 = v.astype(jnp.float32)
    mu = jnp.mean(v32, axis=-1, keepdims=True)
    var = jnp.mean(jnp.square(v32 - mu), axis=-1, keepdims=True)
    vn = ((v32 - mu) * lax.rsqrt(var + EPS) * ln_g.astype(jnp.float32)
          + ln_b.astype(jnp.float32)).astype(v.dtype)
    nc = s_len // CHUNK_2
    vc = vn.reshape(b, nc, CHUNK_2, GMLP_GROUPS, GMLP_GROUP_DIM)
    mixed = jnp.einsum('gts,bnsgd->bntgd', w_s, vc) + b_s.T[:, :, None]
    return u * mixed.reshape(b, s_len, GMLP_WIDTH)

def window_gqa(q, k, v, sinks, slopes):
    b, s_len = q.shape[0], q.shape[1]
    nb = s_len // BLOCK
    k = k.reshape(b, s_len, SWA_KV_HEADS, HEAD_DIM)
    v = v.reshape(b, s_len, SWA_KV_HEADS, HEAD_DIM)
    pad = ((0, 0), (BLOCK, BLOCK), (0, 0), (0, 0))
    kp = jnp.pad(k, pad).reshape(b, nb + 2, BLOCK, SWA_KV_HEADS, HEAD_DIM)
    vp = jnp.pad(v, pad).reshape(b, nb + 2, BLOCK, SWA_KV_HEADS, HEAD_DIM)
    kb = jnp.concatenate([kp[:, :-2], kp[:, 1:-1], kp[:, 2:]], axis=2)
    vb = jnp.concatenate([vp[:, :-2], vp[:, 1:-1], vp[:, 2:]], axis=2)
    qb = q.reshape(b, nb, BLOCK, SWA_KV_HEADS, SWA_GROUP, HEAD_DIM)
    sc = jnp.einsum('bnqkgd,bnckd->bnkgqc', qb, kb,
                    preferred_element_type=jnp.float32) * (HEAD_DIM ** -0.5)
    rel = jnp.arange(3 * BLOCK)[None, :] - BLOCK - jnp.arange(BLOCK)[:, None]
    dist = jnp.abs(rel)
    key_pos = (jnp.arange(nb)[:, None] - 1) * BLOCK + jnp.arange(3 * BLOCK)[None, :]
    valid = (dist <= WINDOW)[None] & ((key_pos >= 0) & (key_pos < s_len))[:, None, :]
    sl = slopes.reshape(SWA_KV_HEADS, SWA_GROUP)
    sc = sc - sl[:, :, None, None] * dist.astype(jnp.float32)
    sc = jnp.where(valid[None, :, None, None], sc, NEG_INF)
    sink = sinks.astype(jnp.float32).reshape(SWA_KV_HEADS, SWA_GROUP)[:, :, None, None]
    m = jnp.maximum(jnp.max(sc, axis=-1, keepdims=True), sink)
    e = jnp.exp(sc - m)
    pr = e / (jnp.sum(e, axis=-1, keepdims=True) + jnp.exp(sink - m))
    o = jnp.einsum('bnkgqc,bnckd->bnqkgd', pr.astype(v.dtype), vb)
    return o.reshape(b, s_len, SWA_WIDTH)

def second_inputs(seed: int = 0) -> dict:
    key = jax.random.key(seed)
    ks = jax.random.split(key, 24)

    def nrm(k, shape, scale):
        return jax.random.normal(k, shape, jnp.float32) * scale

    def gain(k, shape):
        return 1.0 + 0.05 * jax.random.normal(k, shape, jnp.float32)

    L = DEPTH
    return {
        'x': nrm(ks[0], (BATCH, SEQ, D_MODEL), 1.0),
        'p': nrm(ks[1], (DEPTH, BATCH, SEQ, PLE_DIM), 1.0),
        'g_pre_mix': gain(ks[2], (L, D_MODEL)),
        'w_in': nrm(ks[3], (L, D_MODEL, IN_WIDTH), D_MODEL ** -0.5),
        'lam_q1': nrm(ks[4], (L, DIFF_QK_DIM), 0.1),
        'lam_k1': nrm(ks[5], (L, DIFF_QK_DIM), 0.1),
        'lam_q2': nrm(ks[6], (L, DIFF_QK_DIM), 0.1),
        'lam_k2': nrm(ks[7], (L, DIFF_QK_DIM), 0.1),
        'g_diff_sub': gain(ks[8], (L, DIFF_V_DIM)),
        'gmlp_ln_g': gain(ks[9], (L, GMLP_WIDTH)),
        'gmlp_ln_b': nrm(ks[10], (L, GMLP_WIDTH), 0.02),
        'w_spatial': nrm(ks[11], (L, GMLP_GROUPS, CHUNK_2, CHUNK_2), CHUNK_2 ** -0.5),
        'b_spatial': gain(ks[12], (L, GMLP_GROUPS, CHUNK_2)),
        'swa_sinks': nrm(ks[13], (L, SWA_HEADS), 0.5),
        'w_out': nrm(ks[14], (L, MIX_WIDTH, D_MODEL), MIX_WIDTH ** -0.5),
        'g_post_mix': gain(ks[15], (L, D_MODEL)),
        'g_pre_ffn': gain(ks[16], (L, D_MODEL)),
        'w_ffn_in': nrm(ks[17], (L, D_MODEL, 2 * D_FF), D_MODEL ** -0.5),
        'w_ffn_out': nrm(ks[18], (L, D_FF, D_MODEL), D_FF ** -0.5),
        'g_post_ffn': gain(ks[19], (L, D_MODEL)),
        'w_ple_up': nrm(ks[20], (L, PLE_DIM, D_MODEL), PLE_DIM ** -0.5),
        'w_ple_gate': nrm(ks[21], (L, D_MODEL, D_MODEL), D_MODEL ** -0.5),
        'g_ple_gate': gain(ks[22], (L, D_MODEL)),
        'g_ple_post': gain(ks[23], (L, D_MODEL)),
    }

def second_block(x, p, g_pre_mix, w_in, lam_q1, lam_k1, lam_q2, lam_k2, g_diff_sub,
              gmlp_ln_g, gmlp_ln_b, w_spatial, b_spatial, swa_sinks, w_out, g_post_mix,
              g_pre_ffn, w_ffn_in, w_ffn_out, g_post_ffn, w_ple_up, w_ple_gate,
              g_ple_gate, g_ple_post):
    b, s_len = x.shape[0], x.shape[1]
    diff_slopes, swa_slopes = alibi_slopes()
    split_at = np.cumsum(IN_SIZES)[:-1].tolist()
    for l in range(DEPTH):
        h = rmsnorm(x, g_pre_mix[l])
        proj = h @ w_in[l]
        a_q, a_k, a_v, b_u, b_v, c_q, c_k, c_v = jnp.split(proj, split_at, axis=-1)
        lam_init = 0.8 - 0.6 * math.exp(-0.3 * l)
        f32 = jnp.float32
        lam = (jnp.exp(jnp.sum(lam_q1[l].astype(f32) * lam_k1[l].astype(f32)))
               - jnp.exp(jnp.sum(lam_q2[l].astype(f32) * lam_k2[l].astype(f32)))
               + lam_init)
        y_a = diff_attention(
            a_q.reshape(b, s_len, DIFF_HEADS, 2, DIFF_QK_DIM),
            a_k.reshape(b, s_len, DIFF_HEADS, 2, DIFF_QK_DIM),
            a_v.reshape(b, s_len, DIFF_HEADS, DIFF_V_DIM),
            lam, lam_init, g_diff_sub[l], diff_slopes)
        y_b = spatial_gating(b_u, b_v, gmlp_ln_g[l], gmlp_ln_b[l], w_spatial[l], b_spatial[l])
        y_c = window_gqa(c_q, c_k, c_v, swa_sinks[l], swa_slopes)
        y = jnp.concatenate([y_a, y_b, y_c], axis=-1) @ w_out[l]
        x = x + rmsnorm(y, g_post_mix[l])
        h = rmsnorm(x, g_pre_ffn[l])
        gate, up = jnp.split(h @ w_ffn_in[l], 2, axis=-1)
        f = (jax.nn.silu(gate) * up) @ w_ffn_out[l]
        x = x + rmsnorm(f, g_post_ffn[l])
        e = p[l] @ w_ple_up[l]
        g = jax.nn.sigmoid(rmsnorm(x, g_ple_gate[l]) @ w_ple_gate[l])
        x = x + rmsnorm(e * g, g_ple_post[l])
    return x


def setup_inputs(seed=0):
    out = dict(first_inputs(seed))
    for name, value in second_inputs(seed + 1).items():
        if name != "x":
            out[name + "_2"] = value
    return out


def reference(
    x, c, positions, w_ada, b_ada, w_in, i_bias, f_bias, conv_w, conv_b, w_out, ln_mix_g,
    ln_mix_b, w_router, b_router, w_gate, w_up, w_down, ln_ffn_g, ln_ffn_b, p_2, g_pre_mix_2,
    w_in_2, lam_q1_2, lam_k1_2, lam_q2_2, lam_k2_2, g_diff_sub_2, gmlp_ln_g_2, gmlp_ln_b_2,
    w_spatial_2, b_spatial_2, swa_sinks_2, w_out_2, g_post_mix_2, g_pre_ffn_2, w_ffn_in_2,
    w_ffn_out_2, g_post_ffn_2, w_ple_up_2, w_ple_gate_2, g_ple_gate_2, g_ple_post_2,
):
    x = first_block(
        x, c, positions, w_ada, b_ada, w_in, i_bias, f_bias, conv_w, conv_b, w_out, ln_mix_g,
        ln_mix_b, w_router, b_router, w_gate, w_up, w_down, ln_ffn_g, ln_ffn_b,
    )
    return second_block(
        x, p_2, g_pre_mix_2, w_in_2, lam_q1_2, lam_k1_2, lam_q2_2, lam_k2_2, g_diff_sub_2,
        gmlp_ln_g_2, gmlp_ln_b_2, w_spatial_2, b_spatial_2, swa_sinks_2, w_out_2, g_post_mix_2,
        g_pre_ffn_2, w_ffn_in_2, w_ffn_out_2, g_post_ffn_2, w_ple_up_2, w_ple_gate_2,
        g_ple_gate_2, g_ple_post_2,
    )


_drawn_inputs = setup_inputs


def setup_inputs(seed=0):
    import zlib

    import numpy as np

    out = dict(_drawn_inputs(seed))
    spreads = {}
    factors = {'i_bias': 64.0,
     'conv_b': 4.193,
     'lam_k1_2': 5.04,
     'lam_q2_2': 3.417,
     'lam_k2_2': 3.135,
     'gmlp_ln_b_2': 5.255,
     'swa_sinks_2': 4.212,
     'g_ple_gate_2': 4.403}
    for name, (base, spread) in spreads.items():
        noise = np.random.default_rng([zlib.crc32(name.encode()), seed]).standard_normal(out[name].shape)
        drawn = base * np.exp(spread * noise) if base else spread * noise
        out[name] = __import__('jax').numpy.asarray(drawn.astype(out[name].dtype))
    for name, factor in factors.items():
        out[name] = (out[name] * factor).astype(out[name].dtype)
    return out
```

```python
from contextlib import ExitStack

import concourse.bass as bass
from concourse import mybir
import numpy as np

F32 = mybir.dt.float32
I32 = mybir.dt.int32
ALU = mybir.AluOpType
ACT = mybir.ActivationFunctionType
AX = mybir.AxisListType

P = 128
D = 1024
SEQ = 256
TT = SEQ // P
KT = D // P
DEPTH = 2
HD = 64
HALF = HD // 2
N = 512
BIG = 1.0e30
TAKEN = -3.0e38
TOPK = min(256, SEQ // 4)
LN_EPS = 1e-5
RMS_EPS = 1e-6
ALPHA = (2.0 * DEPTH) ** 0.25
TWO_PI = 2.0 * np.pi
ROUND = 12582912.0

AQ, AK, AV, IQ, IK, IW, RQ, RK, RV, RG, MQ, MK, MV, MO, MI, MF = (
    0, 512, 1024, 1536, 1792, 1856, 1860, 2116, 2372, 2628, 2884, 3140, 3396, 3652, 3908, 3912)
IN1 = 3916
CHUNKS1 = {"idx": (IQ, RQ), "aq": (AQ, AK), "ak": (AK, AV), "av": (AV, IQ), "rqk": (RQ, RV),
           "rvg": (RV, MQ), "mqk": (MQ, MV), "mvo": (MV, IN1)}
NA = 8
NI = 4
NR = 4
NE = 16
NG = 4
EG = NE // NG
FE = 256
ADA = 6 * D // N
CONV = 4
DH = 6
DQK = 32
GG = 4
GW = 256
WH = 6
WG = 3
DFF = 2816
NF = DFF // FE
PLE = 256
IN2 = 2304
SLOPES = [2.0 ** (-8.0 * k / (DH + WH)) for k in range(1, DH + WH + 1)]
DIFF_SLOPES, SWA_SLOPES = SLOPES[WH:], SLOPES[:WH]

GS = 4
GW_MAX = 520
ARENA = 15400
SMALL = 640
DS = 2
ORDER = (
    [f"ada{c}" for c in range(4)] + list(CHUNKS1) + ["ada4", "ada5", "wo0", "wo1"]
    + [f"ada{c}" for c in range(6, ADA)] + [f"gu{e}" for e in range(NE)],
    ["aq", "ak", "avcv", "buv", "cqk", "wo0", "wo1"] + [f"gu{e}" for e in range(NF)] + ["pg0", "pg1"],
)
ORDER_D = ([f"dn{e}" for e in range(NE)], [f"dn{e}" for e in range(NF)] + ["up"])
DMAS = ({f"ada{c}": 1 for c in range(ADA)} | {f"gu{e}": 2 for e in range(NE)},
        {f"gu{e}": 2 for e in range(NF)} | {"avcv": 2, "cqk": 7})
ROWS = (2, 1)
PARAMS = (10, 17)

CONST = {}
_at = 0
for _name, _w in (("ident", P), ("invf", HALF), ("first4", NG), ("first16", NE), ("shared", 0)):
    CONST[_name] = _at
    _at += _w
C_SHARED = _at
C1 = {"decay": 0, "causal": NR * 384, "vis": NR * 384 + 256}
C1_W = NR * 384 + 256 + TT * SEQ
C2 = {"dist": 0, "wdist": TT * SEQ}
C2_W = 2 * TT * SEQ


def constants():
    p = np.arange(P)[:, None]
    j = np.arange(SEQ)[None, :]
    shared = np.zeros((P, C_SHARED), np.float32)
    shared[:, CONST["ident"]:CONST["ident"] + P] = np.eye(P)
    shared[:, CONST["invf"]:CONST["invf"] + HALF] = np.float32(10000.0) ** (
        -np.arange(HALF, dtype=np.float32) / np.float32(HALF))
    shared[:, CONST["first4"]:CONST["first4"] + NG] = np.arange(NG, 0, -1)
    shared[:, CONST["first16"]:CONST["first16"] + NE] = np.arange(NE, 0, -1)
    c1 = np.zeros((P, C1_W), np.float32)
    for h in range(NR):
        log_gamma = np.log1p(-(2.0 ** (-5.0 - h)))
        decay = np.where(j >= p, np.exp(np.maximum(j - p, 0) * log_gamma), 0.0) * HD ** -0.5
        c1[:, h * 384:h * 384 + 256] = decay
        c1[:, h * 384 + 256:h * 384 + 384] = decay[:, :P]
    c1[:, C1["causal"]:C1["causal"] + SEQ] = np.where(j >= p, 0.0, -BIG)
    c2 = np.zeros((P, C2_W), np.float32)
    for t in range(TT):
        q = t * P + p
        c1[:, C1["vis"] + t * SEQ:C1["vis"] + (t + 1) * SEQ] = np.where(j < (q // 64 + 1) * 64, 0.0, -BIG)
        dist = np.abs(q - j)
        c2[:, t * SEQ:(t + 1) * SEQ] = dist
        c2[:, C2["wdist"] + t * SEQ:C2["wdist"] + (t + 1) * SEQ] = np.where(dist <= 128, dist, BIG)
    rows = np.zeros((ADA, 8, P), np.float32)
    for n, c in enumerate((4, 5, 10, 11)):
        rows[c, n, :] = 1.0
    for h in range(NR):
        rows[h, 4 + h, :] = -1.0
    lam = np.array([[0.8 - 0.6 * np.exp(-0.3 * l), 0.2 + 0.6 * np.exp(-0.3 * l)] for l in range(DEPTH)], np.float32)
    return {"c_shared": shared, "c_first": c1, "c_second": c2, "c_rows": rows, "c_lam": lam}


class Done:

    def __init__(self, sem, known):
        self.sem, self.known = sem, known
        self.block, self.l, self.n = None, None, 0
        self.marks, self.per, self.stride, self.first = {}, [0, 0], {}, 0
        self.inner, self.inner_n, self.inner_from = None, 0, 0

    def begin(self, block, l):
        if block == 0:
            self.first = self.n
        self.block, self.l, self.n = block, l, 0

    def end(self):
        self.per[self.block] = self.n

    def loop(self, name, n):
        self.inner, self.inner_n, self.inner_from = name, n, self.n

    def loop_end(self):
        step = self.n - self.inner_from
        self.stride[self.inner] = step
        self.n = self.inner_from + step * self.inner_n
        self.inner = None

    def step(self, name=None):
        self.n += 1
        if name is not None:
            self.also(name)
        return 1

    def also(self, name):
        assert (self.block, name) not in self.marks, name
        self.marks[self.block, name] = (self.n, self.inner)

    def base(self, block):
        k = self.known
        return k["first"] + (DEPTH * k["per"][0] if block else 0) if k else 1

    def before(self, by):
        return by.l * self.known["per"][by.block] + self.base(by.block) if self.known else 1

    def now(self):
        if self.block is None:
            return self.n
        return self.l * self.known["per"][self.block] + (self.base(self.block) + self.n) if self.known else 1

    def total(self):
        return self.base(1) + DEPTH * self.known["per"][1] if self.known else 1

    def at(self, by, name, i=None):
        if not self.known:
            return 1
        n, inner = self.known["marks"][by.block, name]
        if by.block is None:
            return n
        v = by.l * self.known["per"][by.block] + (self.base(by.block) + n)
        return v if inner is None else v + i * self.known["stride"][inner]

    def counted(self):
        return {"marks": self.marks, "per": self.per, "stride": self.stride, "first": self.first}


class Ring:

    def __init__(self, sems, slots, orders, dmas):
        self.sems, self.slot, self.count, self.per = sems, {}, {}, []
        for b, order in enumerate(orders):
            total = [0] * slots
            for c, name in enumerate(order):
                s = c % slots
                total[s] += 16 * dmas[b].get(name, 1)
                self.slot[b, name], self.count[b, name] = s, total[s]
            self.per.append(total)

    def sem(self, by, name):
        return self.sems[self.slot[by.block, name]]

    def level(self, by, name, more=0):
        b, s = by.block, self.slot[by.block, name]
        first = DEPTH * self.per[0][s] if b else 0
        return by.l * self.per[b][s] + (first + self.count[b, name]) + more


def program(nc, ins, out, known):
    ctx = ExitStack()
    with ctx:
        def sb(name, shape, dt=F32):
            return ctx.enter_context(nc.sbuf_tensor(name, shape, dt))

        def sem(name):
            return ctx.enter_context(nc.semaphore(name))

        pe, dve, act, sp = nc.tensor, nc.vector, nc.scalar, nc.sync

        gring = sb("gring", [P, GS, KT, GW_MAX])
        dring = sb("dring", [P, DS, FE // P, D])
        x = sb("x", [P, TT, D])
        hT = sb("hT", [P, KT, SEQ])
        o_cat = sb("o_cat", [P, TT, D])
        cshared = sb("cshared", [P, C_SHARED])
        cblock = sb("cblock", [P, C1_W])
        crows = sb("crows", [ADA, 8, P])
        rows = sb("rows", [P, 2, D])
        gb = sb("gb", [P, D])
        ones = sb("ones", [P, N])
        zeros = sb("zeros", [P, P])
        cosf = sb("cosf", [P, TT, HD])
        sinf = sb("sinf", [P, TT, HD])
        cact = sb("cact", [P, KT])
        wr = sb("wr", [P, KT, NE])
        br = sb("br", [P, NE])
        ex = sb("ex", [P, 3, TT * FE])
        sact = ex[:, 0, :].rearrange("p (t f) -> p t f", t=TT)
        hid = ex[:, 1, :].rearrange("p (t f) -> p t f", t=TT)
        hidT = ex[:, 2, :].rearrange("p (t f n) -> p t f n", t=TT, f=FE // P)
        small = sb("small", [P, SMALL])
        tmp = sb("tmp", [P, 2, N])
        arena = sb("arena", [P, ARENA])
        ident = cshared[:, 0:P]

        used = [0]

        def restart():
            used[0] = 0

        def buf(*shape):
            size = int(np.prod(shape))
            a = arena[:, used[0]:used[0] + size]
            used[0] += size
            assert used[0] <= ARENA, used[0]
            if len(shape) == 2:
                a = a.rearrange("p (a b) -> p a b", a=shape[0])
            elif len(shape) == 3:
                a = a.rearrange("p (a b c) -> p a b c", a=shape[0], b=shape[1])
            return a

        s_used = [0]

        def sc(n):
            a = small[:, s_used[0]:s_used[0] + n]
            s_used[0] += n
            assert s_used[0] <= SMALL
            return a

        psum = ctx.enter_context(nc.psum_tensor("psum", [P, 8, N], F32))

        tensor_done, vector_done, scalar_done = sem("tensor_done"), sem("vector_done"), sem("scalar_done")
        g_landed = [sem(f"g_landed{i}") for i in range(GS)]
        d_landed = [sem(f"d_landed{i}") for i in range(DS)]
        start_loaded, params_loaded, rows_loaded = sem("start_loaded"), sem("params_loaded"), sem("rows_loaded")
        const_loaded, stored, waited = sem("const_loaded"), sem("stored"), sem("waited")

        known = known or {}
        T = Done(tensor_done, known.get("T"))
        V = Done(vector_done, known.get("V"))
        A = Done(scalar_done, known.get("A"))
        S = Done(None, known.get("S"))
        G = Ring(g_landed, GS, ORDER, DMAS)
        DN = Ring(d_landed, DS, ORDER_D, ({}, {}))

        def gslot(block, name):
            return gring[:, G.slot[block, name]]

        def dslot(block, name):
            return dring[:, DN.slot[block, name]]

        def params_count(by):
            b = by.block
            return by.l * (16 * PARAMS[b]) + (16 * PARAMS[b] + (DEPTH * 16 * PARAMS[0] if b else 0))

        def rows_count(by):
            b = by.block
            return by.l * (16 * ROWS[b]) + (16 * ROWS[b] + (DEPTH * 16 * ROWS[0] if b else 0))

        bank_of, on_bank = {}, {}
        turn = [0]

        def take(name, reader, bank=None, pair=False):
            if bank is None:
                bank = turn[0] + (turn[0] % 2 if pair else 0)
                bank %= 6
                turn[0] = (bank + (2 if pair else 1)) % 6
            banks = (bank, bank + 1) if pair else (bank,)
            for last in dict.fromkeys(on_bank[b] for b in banks if b in on_bank):
                pe.wait_ge(last[0].sem, last[0].at(T, *last[1:]))
                if pair:
                    pe.sem_inc(waited)
            for b in banks:
                on_bank[b] = (reader, ("read", name))
            bank_of[T.block, name] = (bank, pair)
            return psum[:, bank:bank + 2, :] if pair else psum[:, bank, :]

        def bank(E, name):
            b, pair = bank_of[E.block, name]
            return psum[:, b:b + 2, :] if pair else psum[:, b, :]

        roped = buf(3, N)
        idxT, aqT, akT, rrT = buf(3, SEQ), buf(4, SEQ), buf(4, SEQ), buf(4, SEQ)
        av, rv, rg = buf(TT, N), buf(TT, 256), buf(TT, 256)
        cin, qkT = buf(4, SEQ + CONV - 1), buf(4, SEQ)
        mv, mo = buf(TT, NR, HD + 1), buf(TT, 256)
        rel, bias = buf(NI, SEQ), buf(TT, SEQ)
        score = buf(SEQ)
        sm, pT = buf(2, N), buf(2, N)
        brow = buf(N)
        convw = buf(4, CONV + 1)
        sT = roped.rearrange("p a n -> p (a n)")[:, 0:768].rearrange("p (a n) -> p a n", a=2)
        wT = roped.rearrange("p a n -> p (a n)")[:, 768:1536].rearrange("p (a n) -> p a n", a=2)
        hn = rel.rearrange("p a n -> p (a n)")[:, 0:N].rearrange("p (h d) -> p h d", h=8)
        sq = rel.rearrange("p a n -> p (a n)")[:, N:2 * N].rearrange("p (h d) -> p h d", h=8)
        acc = tmp
        grow = ex.rearrange("p a n -> p (a n)").rearrange("p (r n) -> p r n", r=6)
        restart()
        qT2, kT2, at2 = buf(3, SEQ), buf(3, SEQ), buf(2, SEQ)
        cT2 = buf(4, SEQ)
        avcv, buv, vn, wsT = buf(TT, N), buf(TT, N), buf(TT, GW), buf(GG, P)
        wsp = buf(GG, P)
        sm2, pT2 = buf(2, N), buf(2, N)
        hn2, sq2 = buf(DH, HD), buf(DH, HD)
        prow, pTT = buf(TT, PLE), buf(PLE // P, SEQ)
        grows, glnrow, subrow = buf(P), buf(2, GW), buf(HD)
        lamrow = buf(4, DQK)
        e2, e2b = gb[:, :], buf(D)
        y2 = arena[:, 0:TT * D].rearrange("p (t n) -> p t n", t=TT)
        junk = sm2.rearrange("p a n -> p (a n)")

        mod = [sc(KT) for _ in range(4)]
        iw, ngm, rsum = sc(TT * NI), sc(2 * 2), sc(TT * NA)
        rinv, top8 = sc(TT * NA), sc(8)
        st, agg, rstd = sc(12), sc(2 * TT), sc(2 * TT)
        hs, hv = sc(8), sc(8)
        gcol, den = sc(16), sc(NR)
        ibias, fbias = sc(1), sc(1)
        scores, biased, bmask, onehot, sel, gate = (sc(TT * NE) for _ in range(6))
        pairs, gsum, key4, t2 = sc(8 * 6), sc(8), sc(8), sc(TT)
        posf = sc(TT)
        gcols = sc(3 * KT + GG)
        lamc, lam, lsum = sc(2), sc(1), sc(2)
        r2, nm2, sinks, msink, dsum = sc(2), sc(2), sc(WH), sc(2), sc(TT * WH)
        lprod = sc(2 * DQK)
        c8 = ex[0:KT, 0, 0:P]
        posi = sb("posi", [P, TT], I32)

        block = ctx.enter_context(nc.Block())

        def token_major(ap):
            return ap.rearrange("(t p) n -> p t n", p=P)

        def by_row(ap):
            return ap.rearrange("(k p) n -> p k n", p=P)

        def layer(name, l):
            a = ins[name][bass.ds(l, 1)]
            return a.rearrange("a b c d -> (a b) c d") if len(a.shape) == 4 else a.rearrange(
                "a b c -> (a b) c") if len(a.shape) == 3 else a.rearrange("a b -> (a b)")

        NIT = {NE: (NE - 2) // 4, NF: (NF - 2) // 4}

        def transposed_x(tag, src, reader):
            for g in range(KT // 2):
                ps = take((tag, g), reader)
                for f in (2 * g, 2 * g + 1):
                    for t in range(TT):
                        last = nc.tensor.transpose(ps[:, (f % 2) * SEQ + t * P:(f % 2) * SEQ + (t + 1) * P],
                                                   src[:, t, f * P:(f + 1) * P], ident)
                last.then_inc(tensor_done, T.step((tag, g)))

        def token_product(ps, t, w, n):
            for k in range(KT):
                last = nc.tensor.matmul(ps[:, 0:n], hT[:, k, t * P:(t + 1) * P], w[:, k, 0:n],
                                        start=k == 0, stop=k == KT - 1)
            return last

        def feature_product(ps, w, c0, m, at):
            for k in range(KT):
                last = nc.tensor.matmul(ps[0:m, at:at + SEQ], w[:, k, c0:c0 + m], hT[:, k, :],
                                        start=k == 0, stop=k == KT - 1)
            return last

        def pe_experts(ne, start, block_no):
            n = NIT[ne]

            def gu(e, t, i, name, read):
                if t == 0:
                    pe.wait_ge(G.sem(T, f"gu{e}"), G.level(T, f"gu{e}", 0 if i is None else i * 32))
                if read is not None:
                    pe.wait_ge(vector_done, V.at(T, *read))
                token_product(psum[:, t, :], t, gslot(block_no, f"gu{e}"), N).then_inc(tensor_done, T.step(name))

            def tr(t, i, name, hid_name):
                pe.wait_ge(vector_done, V.at(T, hid_name, i))
                for f in range(FE // P):
                    last = nc.tensor.transpose(psum[:, 2 + t, f * P:(f + 1) * P], hid[:, t, f * P:(f + 1) * P], ident)
                last.then_inc(tensor_done, T.step(name))

            def dn(e, t, i, name, copied, more, first=False, final=False):
                pe.wait_ge(scalar_done, A.at(T, *copied))
                if t == 0:
                    pe.wait_ge(DN.sem(T, f"dn{e}"), DN.level(T, f"dn{e}", more))
                w = dslot(block_no, f"dn{e}")
                for f in range(FE // P):
                    for h in range(2):
                        last = nc.tensor.matmul(psum[:, 4 + 2 * t + h, :], hidT[:, t, f, :], w[:, f, h * N:(h + 1) * N],
                                                start=first and f == 0, stop=final and f == FE // P - 1)
                last.then_inc(tensor_done, T.step(name))

            for b in range(8):
                if b in on_bank:
                    pe.wait_ge(on_bank[b][0].sem, on_bank[b][0].at(T, *on_bank[b][1:]))
                    pe.sem_inc(waited)
                    del on_bank[b]
            pe.wait_ge(start[0].sem, start[0].at(T, *start[1:]))
            for h in range(2):
                nc.tensor.matmul(psum[:, 6 + h, :], zeros[0:1, :], ones[0:1, :], start=True, stop=False)
            gu(0, 0, None, ("gu0", 0), None)
            gu(0, 1, None, ("gu1", 0), None)
            tr(0, None, ("tr", 0, 0), ("hid", 0, 0))
            gu(1, 0, None, ("gu0", 1), (("hid", 0, 0), None))
            tr(1, None, ("tr", 0, 1), ("hid", 0, 1))
            dn(0, 0, None, ("dn0", 0), (("hidT", 0, 0), None), 0, first=True)
            with nc.tensor.Fori(0, n) as i:
                T.loop(f"pe{block_no}", n)
                for j in range(4):
                    e = 1 + j
                    before = (("hid", "loop", j - 1, 1), i) if j else (("hid", "loop", 3, 1), i - 1)
                    gu(e, 1, i, ("gu1", "loop", j), before)
                    tr(0, i, ("tr", "loop", j, 0), ("hid", "loop", j, 0))
                    copied = (("hidT", "loop", j - 1, 1), i) if j else (("hidT", "loop", 3, 1), i - 1)
                    dn(e - 1, 1, i, ("dn1", "loop", j), copied, i * 32)
                    gu(e + 1, 0, i, ("gu0", "loop", j), (("hid", "loop", j, 0), i))
                    tr(1, i, ("tr", "loop", j, 1), ("hid", "loop", j, 1))
                    dn(e, 0, i, ("dn0", "loop", j), (("hidT", "loop", j, 0), i), i * 32)
                T.loop_end()
            for e in range(1 + 4 * n, ne):
                prev = ("loop", 3) if e == 1 + 4 * n else (e - 1,)
                it = n - 1 if e == 1 + 4 * n else None
                gu(e, 1, None, ("gu1", e), (("hid", *prev, 1), it))
                tr(0, None, ("tr", e, 0), ("hid", e, 0))
                dn(e - 1, 1, None, ("dn1", e - 1), (("hidT", *prev, 1), it), 0)
                if e + 1 < ne:
                    gu(e + 1, 0, None, ("gu0", e + 1), (("hid", e, 0), None))
                tr(1, None, ("tr", e, 1), ("hid", e, 1))
                dn(e, 0, None, ("dn0", e), (("hidT", e, 0), None), 0, final=e == ne - 1)
            dn(ne - 1, 1, None, ("dn1", ne - 1), (("hidT", ne - 1, 1), None), 0, final=True)

        def pe_attention(tag, steps, scores_of, widths, values_of, probs_src, probs_T, outs):
            n = len(steps)

            def score_step(s):
                ps = take((tag, "S", s), V, pair=True)
                scores_of(ps, s).then_inc(tensor_done, T.step((tag, "S", s)))

            for s in range(min(2, n)):
                score_step(s)
            for s in range(n):
                pe.wait_ge(probs_src(s)[0].sem, probs_src(s)[0].at(T, *probs_src(s)[1:]))
                ps = take((tag, "PT", s), A)
                src, blocks = widths(s)
                for b in range(blocks):
                    last = nc.tensor.transpose(ps[:, b * P:(b + 1) * P], src[:, b * P:(b + 1) * P], ident)
                last.then_inc(tensor_done, T.step((tag, "PT", s)))
                if s + 2 < n:
                    score_step(s + 2)
                if s in outs:
                    name, reader, b = outs[s]
                    take(name, reader, b)
                pe.wait_ge(scalar_done, A.at(T, (tag, "pT", s)))
                values_of(s).then_inc(tensor_done, T.step((tag, "PV", s)))

        ATT = [(t, i) for t in range(TT) for i in range(NA // 2)]

        def pe_first(l):
            T.begin(0, l)
            on_bank.clear()
            turn[0] = 0
            pe.wait_ge(vector_done, V.before(T))
            pe.wait_ge(scalar_done, A.before(T))
            transposed_x("xT", x, V)

            def ada_columns(tag, chunks, bank_no):
                ps = take(tag, V, bank_no)
                for n, c in enumerate(chunks):
                    pe.wait_ge(vector_done, V.at(T, ("acc", c)))
                    if n == 0 and c == 0:
                        pe.wait_ge(params_loaded, params_count(T))
                    for j in range(N // P):
                        o = ps[:, 4 * n + j:4 * n + j + 1]
                        nc.tensor.matmul(o, acc[:, c % 2, j * P:(j + 1) * P], ones[:, 0:1], start=True, stop=False)
                        last = nc.tensor.matmul(o, brow[0:ADA, j * P:(j + 1) * P], ident[0:ADA, c:c + 1],
                                                start=False, stop=True)
                    last.then_inc(tensor_done, T.step(("acc_used", c)))

            def ada_rows(n, c):
                ps = take(("gate_row", c), V)
                pe.wait_ge(vector_done, V.at(T, ("acc", c)))
                nc.tensor.matmul(ps, ones[:, 0:P], acc[:, c % 2, :], start=True, stop=False)
                nc.tensor.matmul(ps, crows[:, n, :], brow[0:ADA, :], start=False, stop=True).then_inc(tensor_done, T.step(("acc_used", c)))

            ada_columns("modm", range(4), 7)
            pe.wait_ge(vector_done, V.at(T, ("hT", KT // 2 - 1)))

            def in_proj(name):
                pe.wait_ge(G.sem(T, name), G.level(T, name))
                c0, c1 = CHUNKS1[name]
                for t in range(TT):
                    ps = take((name, t), V if name in ("idx", "aq", "ak", "rqk") else A)
                    token_product(ps, t, gslot(0, name), min(N, c1 - c0)).then_inc(tensor_done, T.step((name, t)))

            rope_slot = {n: i for i, n in enumerate([(c, t) for c in ("idx", "aq", "ak", "rqk") for t in range(TT)])}

            def transposed_rope(name, t, blocks):
                pe.wait_ge(vector_done, V.at(T, ("rope", name, t)))
                ps = take((name, "T", t), A)
                src = roped[:, rope_slot[name, t] % 3, :]
                for b in range(blocks):
                    last = nc.tensor.transpose(ps[:, b * P:(b + 1) * P], src[:, b * P:(b + 1) * P], ident)
                last.then_inc(tensor_done, T.step((name, "T", t)))

            def index_scores(t):
                nk = (t + 1) * P
                ps = take(("idxS", t), A, pair=True)
                if t == 0:
                    pe.sem_inc(waited)
                    pe.wait_ge(scalar_done, A.at(T, ("idx", "Tc", 1)))
                for p in range(2):
                    for h in (0, 1):
                        last = nc.tensor.matmul(ps[:, h, p * SEQ:p * SEQ + nk],
                                                idxT[h * HD:(h + 1) * HD, p, t * P:(t + 1) * P],
                                                idxT[h * HD:(h + 1) * HD, 2, 0:nk], start=True, stop=True)
                last.then_inc(tensor_done, T.step(("idxS", t)))

            in_proj("idx")
            transposed_rope("idx", 0, 3)
            transposed_rope("idx", 1, 3)
            in_proj("aq")
            index_scores(0)
            index_scores(1)
            transposed_rope("aq", 0, 4)
            transposed_rope("aq", 1, 4)
            in_proj("ak")
            in_proj("av")
            transposed_rope("ak", 0, 4)
            transposed_rope("ak", 1, 4)
            in_proj("rqk")
            in_proj("rvg")
            transposed_rope("rqk", 0, 4)
            transposed_rope("rqk", 1, 4)
            pe.wait_ge(G.sem(T, "mqk"), G.level(T, "mqk"))
            for b in range(2):
                ps = take(("mqk", b), A)
                for f in range(2):
                    last = feature_product(ps, gslot(0, "mqk"), (2 * b + f) * P, P, f * SEQ)
                last.then_inc(tensor_done, T.step(("mqk", b)))
            in_proj("mvo")
            ps = take("gates", V)
            for f in range(2):
                last = feature_product(ps, gslot(0, "mvo"), N + NR * f, NR, f * SEQ)
            last.then_inc(tensor_done, T.step("gates"))

            def att_scores(ps, s):
                t, i = ATT[s]
                nk = (t + 1) * P
                if s == 0:
                    pe.wait_ge(scalar_done, A.at(T, ("aq", "Tc", 1)))
                    pe.wait_ge(scalar_done, A.at(T, ("ak", "Tc", 1)))
                for h in (0, 1):
                    last = nc.tensor.matmul(ps[:, h, 0:nk], aqT[h * HD:(h + 1) * HD, i, t * P:(t + 1) * P],
                                            akT[h * HD:(h + 1) * HD, i, 0:nk], start=True, stop=True)
                return last

            def att_values(s):
                t, i = ATT[s]
                if s == 0:
                    pe.wait_ge(scalar_done, A.at(T, ("av", 1)))
                for h in (0, 1):
                    c = (2 * i + h) * HD
                    for k in range(t + 1):
                        last = nc.tensor.matmul(psum[:, 6 + t, c:c + HD], pT[:, s % 2, (h * (t + 1) + k) * P:(h * (t + 1) + k + 1) * P],
                                                av[:, k, c:c + HD], start=k == 0, stop=k == t)
                return last

            pe_attention("att", ATT, att_scores, lambda s: (sm[:, s % 2, :], 2 * (ATT[s][0] + 1)), att_values,
                         lambda s: (A, ("att", "exp", s)), pT,
                         {0: (("att", "O", 0), V, 6), NA // 2: (("att", "O", 1), V, 7)})

            def transposed_scores(ps, qk, h):
                r, b = (h % 2) * HD, h // 2
                nc.tensor.matmul(ps[:, 0:SEQ], qk[r:r + HD, 2 + b, 0:P], qk[r:r + HD, b, :], start=True, stop=True)
                return nc.tensor.matmul(ps[:, SEQ:SEQ + P], qk[r:r + HD, 2 + b, P:SEQ], qk[r:r + HD, b, P:SEQ],
                                        start=True, stop=True)

            def ret_scores(h):
                ps = take(("ret", "S", h), V)
                if h == 0:
                    pe.wait_ge(scalar_done, A.at(T, ("rqk", "Tc", 1)))
                transposed_scores(ps, rrT, h).then_inc(tensor_done, T.step(("ret", "S", h)))

            ret_scores(0)
            ret_scores(1)
            ps = take(("ret", "O"), V, 6)
            for h in range(NR):
                pe.wait_ge(vector_done, V.at(T, ("ret", "sT", h)))
                if h == 0:
                    pe.wait_ge(scalar_done, A.at(T, ("rvg", 1)))
                c = h * HD
                nc.tensor.matmul(ps[:, c:c + HD], sT[:, h % 2, 0:P], rv[:, 0, c:c + HD], start=True, stop=True)
                nc.tensor.matmul(ps[:, 256 + c:256 + c + HD], sT[:, h % 2, P:SEQ], rv[:, 0, c:c + HD], start=True, stop=False)
                nc.tensor.matmul(ps[:, 256 + c:256 + c + HD], sT[:, h % 2, SEQ:384], rv[:, 1, c:c + HD], start=False, stop=True).then_inc(tensor_done, T.step(("ret", "PV", h)))
                if h + 2 < NR:
                    ret_scores(h + 2)

            ps = take("gcol", V)
            pe.wait_ge(scalar_done, A.at(T, "erow"))
            for t in range(TT):
                for n, r in ((0, 2), (1, 5)):
                    last = nc.tensor.matmul(ps[:, 8 * t + 4 * n:8 * t + 4 * n + NR], grow[0:NR, r, t * P:(t + 1) * P],
                                            ident[0:NR, 0:NR], start=True, stop=True)
            last.then_inc(tensor_done, T.step("gcol"))

            def ml_scores(h):
                ps = take(("ml", "M", h), V)
                if h == 0:
                    pe.wait_ge(scalar_done, A.at(T, "conv"))
                nc.tensor.matmul(ps[:, 0:SEQ], crows[0:NR, 4 + h, :], grow[0:NR, 3, :], start=True, stop=True).then_inc(tensor_done, T.step(("ml", "M", h)))
                ps = take(("ml", "S", h), V)
                transposed_scores(ps, qkT, h).then_inc(tensor_done, T.step(("ml", "S", h)))

            ml_scores(0)
            ml_scores(1)
            o0, o1 = take(("ml", "O", 0), V, 7), take(("ml", "O", 1), V, 6)
            for h in range(NR):
                pe.wait_ge(vector_done, V.at(T, ("ml", "sT", h)))
                if h == 0:
                    pe.wait_ge(scalar_done, A.at(T, ("mvo", 1)))
                c = h * (HD + 1)
                nc.tensor.matmul(o0[:, c:c + HD + 1], sT[:, h % 2, 0:P], mv[:, 0, h, :], start=True, stop=True)
                nc.tensor.matmul(o1[:, c:c + HD + 1], sT[:, h % 2, P:SEQ], mv[:, 0, h, :], start=True, stop=False)
                nc.tensor.matmul(o1[:, c:c + HD + 1], sT[:, h % 2, SEQ:384], mv[:, 1, h, :], start=False, stop=True).then_inc(tensor_done, T.step(("ml", "PV", h)))
                if h + 2 < NR:
                    ml_scores(h + 2)

            ada_rows(0, 4)
            ada_rows(1, 5)
            pe.wait_ge(vector_done, V.at(T, "o_cat"))
            transposed_x("oT", o_cat, A)
            pe.wait_ge(scalar_done, A.at(T, ("oTc", KT // 2 - 1)))
            for h in range(2):
                pe.wait_ge(G.sem(T, f"wo{h}"), G.level(T, f"wo{h}"))
                for t in range(TT):
                    ps = take(("wo", t, h), V)
                    token_product(ps, t, gslot(0, f"wo{h}"), N).then_inc(tensor_done, T.step(("wo", t, h)))

            ada_columns("modf", range(6, 10), 7)
            ada_rows(2, 10)
            ada_rows(3, 11)
            pe.wait_ge(vector_done, V.at(T, "ln1"))
            transposed_x("xT2", x, V)
            pe.wait_ge(vector_done, V.at(T, ("hT2", KT // 2 - 1)))
            ps = take("router", A)
            for t in range(TT):
                for k in range(KT):
                    last = nc.tensor.matmul(ps[:, t * NE:(t + 1) * NE], hT[:, k, t * P:(t + 1) * P], wr[:, k, :],
                                            start=k == 0, stop=k == KT - 1)
            last.then_inc(tensor_done, T.step("router"))
            pe_experts(NE, (V, ("hT2", KT // 2 - 1)), 0)
            T.end()

        DIFF = [(t, h) for t in range(TT) for h in range(DH)]
        WIN = [(t, g) for t in range(TT) for g in range(WG)]

        def pe_second(l):
            T.begin(1, l)
            on_bank.clear()
            turn[0] = 0
            pe.wait_ge(vector_done, V.before(T))
            pe.wait_ge(scalar_done, A.before(T))
            pe.wait_ge(params_loaded, params_count(T))
            ps = take("gains", V)
            pe.sem_inc(waited)
            nc.tensor.transpose(ps[:, 0:3 * KT + GG], grows[0:3 * KT + GG, :], ident[0:3 * KT + GG, 0:3 * KT + GG]).then_inc(tensor_done, T.step("gains"))
            ps = take("ws", A)
            for g in range(GG):
                last = nc.tensor.transpose(ps[:, g * P:(g + 1) * P], wsp[:, g, :], ident)
            last.then_inc(tensor_done, T.step("ws"))
            ps = take("p", A)
            for t in range(TT):
                for k in range(PLE // P):
                    last = nc.tensor.transpose(ps[:, k * SEQ + t * P:k * SEQ + (t + 1) * P], prow[:, t, k * P:(k + 1) * P], ident)
            last.then_inc(tensor_done, T.step("p"))
            pe.wait_ge(vector_done, V.at(T, ("xn", "mix")))
            transposed_x("xT", o_cat, V)
            pe.wait_ge(vector_done, V.at(T, ("hT", KT // 2 - 1)))

            def features(name, blocks):
                pe.wait_ge(G.sem(T, name), G.level(T, name))
                for b in range(0, blocks, 2):
                    ps = take((name, b // 2), A)
                    for f in range(min(2, blocks - b)):
                        last = feature_product(ps, gslot(1, name), (b + f) * P, P, f * SEQ)
                    last.then_inc(tensor_done, T.step((name, b // 2)))

            def tokens(name):
                pe.wait_ge(G.sem(T, name), G.level(T, name))
                for t in range(TT):
                    ps = take((name, t), A)
                    token_product(ps, t, gslot(1, name), N).then_inc(tensor_done, T.step((name, t)))

            features("aq", 3)
            features("ak", 3)
            tokens("avcv")
            tokens("buv")
            features("cqk", 4)

            def diff_scores(ps, s):
                t, h = DIFF[s]
                if s == 0:
                    pe.wait_ge(scalar_done, A.at(T, ("ak", "c", 1)))
                for c in range(2):
                    r = (h % 2) * HD + c * DQK
                    last = nc.tensor.matmul(ps[:, c, 0:SEQ], qT2[r:r + DQK, h // 2, t * P:(t + 1) * P],
                                            kT2[r:r + DQK, h // 2, :], start=True, stop=True)
                return last

            def diff_values(s):
                t, h = DIFF[s]
                if s == 0:
                    pe.wait_ge(scalar_done, A.at(T, ("avcv", "c", 1)))
                for k in range(TT):
                    last = nc.tensor.matmul(psum[:, 6 + t, h * HD:(h + 1) * HD], pT2[:, s % 2, k * P:(k + 1) * P],
                                            avcv[:, k, h * HD:(h + 1) * HD], start=k == 0, stop=k == TT - 1)
                return last

            pe_attention("diff", DIFF, diff_scores, lambda s: (at2[:, s % 2, :], TT), diff_values,
                         lambda s: (V, ("diff", "at", s)), pT2,
                         {0: (("diff", "O", 0), V, 6), DH: (("diff", "O", 1), V, 7)})

            pe.wait_ge(vector_done, V.at(T, ("vn", 1)))
            pe.wait_ge(scalar_done, A.at(T, "wsT"))
            pe.sem_inc(waited)
            ps = take("mix", V)
            for g in range(GG):
                last = nc.tensor.matmul(ps[:, g * P:(g + 1) * P], wsT[:, g, :], vn[:, :, g * HD:(g + 1) * HD],
                                        start=True, stop=True)
            last.then_inc(tensor_done, T.step("mix"))

            def win_scores(ps, s):
                t, g = WIN[s]
                if s == 0:
                    pe.wait_ge(scalar_done, A.at(T, ("cqk", "c", 1)))
                for h in range(2):
                    last = nc.tensor.matmul(ps[:, h, 0:SEQ], cT2[h * HD:(h + 1) * HD, g, t * P:(t + 1) * P],
                                            cT2[h * HD:(h + 1) * HD, WG, :], start=True, stop=True)
                return last

            def win_values(s):
                t, g = WIN[s]
                for h in range(2):
                    c = (h * WG + g) * HD
                    for k in range(TT):
                        last = nc.tensor.matmul(psum[:, 6 + t, c:c + HD], pT2[:, s % 2, (h * TT + k) * P:(h * TT + k + 1) * P],
                                                avcv[:, k, 384 + h * HD:384 + (h + 1) * HD], start=k == 0, stop=k == TT - 1)
                return last

            pe_attention("win", WIN, win_scores, lambda s: (sm2[:, s % 2, :], 2 * TT), win_values,
                         lambda s: (A, ("win", "exp", s)), pT2,
                         {0: (("win", "O", 0), V, 6), WG: (("win", "O", 1), V, 7)})

            pe.wait_ge(vector_done, V.at(T, "o_cat"))
            transposed_x("oT", o_cat, A)
            pe.wait_ge(scalar_done, A.at(T, ("oTc", KT // 2 - 1)))
            for h in range(2):
                pe.wait_ge(G.sem(T, f"wo{h}"), G.level(T, f"wo{h}"))
                for t in range(TT):
                    ps = take(("wo", t, h), A)
                    token_product(ps, t, gslot(1, f"wo{h}"), N).then_inc(tensor_done, T.step(("wo", t, h)))
            pe.wait_ge(vector_done, V.at(T, ("xn", "ffn")))
            transposed_x("xT2", o_cat, V)
            pe_experts(NF, (V, ("hT2", KT // 2 - 1)), 1)
            for b in range(4):
                on_bank[4 + b] = (A, ("read", ("acc", b)))
            for t in range(TT):
                on_bank[t], on_bank[2 + t] = (V, ("hid", NF - 1, t)), (A, ("hidT", NF - 1, t))
            pe.wait_ge(DN.sem(T, "up"), DN.level(T, "up"))
            pe.wait_ge(scalar_done, A.at(T, "pT"))
            for t in range(TT):
                for h in range(2):
                    ps = take(("e", t, h), A)
                    for k in range(PLE // P):
                        last = nc.tensor.matmul(ps, pTT[:, k, t * P:(t + 1) * P], dslot(1, "up")[:, k, h * N:(h + 1) * N],
                                                start=k == 0, stop=k == PLE // P - 1)
                    last.then_inc(tensor_done, T.step(("e", t, h)))
            pe.wait_ge(vector_done, V.at(T, ("xn", "ple")))
            transposed_x("xT3", o_cat, V)
            pe.wait_ge(vector_done, V.at(T, ("hT3", KT // 2 - 1)))
            for h in range(2):
                pe.wait_ge(G.sem(T, f"pg{h}"), G.level(T, f"pg{h}"))
                for t in range(TT):
                    ps = take(("pg", t, h), A)
                    token_product(ps, t, gslot(1, f"pg{h}"), N).then_inc(tensor_done, T.step(("pg", t, h)))
            T.end()

        @block.tensor
        def _(pe):
            pe.wait_ge(start_loaded, 16 * 8)
            nc.tensor.transpose(psum[:, 0, 0:KT], c8, ident[0:KT, 0:KT]).then_inc(tensor_done, T.step("c"))
            with pe.Fori(0, DEPTH) as l:
                pe_first(l)
            with pe.Fori(0, DEPTH) as l:
                pe_second(l)

        def ts(o, a, s1, s2, op0, op1=None):
            if op1 is None:
                return nc.vector.tensor_scalar(o, a, s1, None, op0)
            return nc.vector.tensor_scalar(o, a, s1, s2, op0, op1)

        def tt(o, a, b, op):
            return nc.vector.tensor_tensor(o, a, b, op)

        def stt(o, a, s, b, op0, op1):
            return nc.vector.scalar_tensor_tensor(o, a, s, b, op0, op1)

        def vmax(o, a):
            return nc.vector.tensor_reduce(o, a, AX.X, ALU.max)

        def vsum(o, a):
            return nc.vector.tensor_reduce(o, a, AX.X, ALU.add)

        def over(col, *shape):
            return col.unsqueeze(2).to_broadcast([P, *shape])

        def ada(c):
            dve.wait_ge(G.sem(V, f"ada{c}"), G.level(V, f"ada{c}"))
            if c >= 2:
                dve.wait_ge(tensor_done, T.at(V, ("acc_used", c - 2)))
            w, a = gslot(0, f"ada{c}"), acc[:, c % 2, :]
            ts(a, w[:, 0, 0:N], cact[:, 0:1], None, ALU.mult).then_inc(vector_done, V.step())
            dve.wait_ge(vector_done, V.now())
            for k in range(1, KT):
                stt(a, w[:, k, 0:N], cact[:, k:k + 1], a, ALU.mult, ALU.add).then_inc(vector_done, V.step(("acc", c) if k == KT - 1 else None))
                dve.wait_ge(vector_done, V.now())

        def rope(ps, nh, t, o, name, last_read):
            heads = ps[:, 0:nh * HD].rearrange("p (h d) -> p h d", h=nh)
            a = tmp[:, 0, 0:nh * HD].rearrange("p (h d) -> p h d", h=nh)
            b = tmp[:, 1, 0:nh * HD].rearrange("p (h d) -> p h d", h=nh)
            cs = cosf[:, t, :].unsqueeze(1).to_broadcast([P, nh, HD])
            tt(a, heads, cs, ALU.mult).then_inc(vector_done, V.step())
            dve.wait_ge(vector_done, V.now())
            for h, g in ((0, 1), (1, 0)):
                sn = sinf[:, t, h * HALF:(h + 1) * HALF].unsqueeze(1).to_broadcast([P, nh, HALF])
                tt(b[:, :, h * HALF:(h + 1) * HALF], heads[:, :, g * HALF:(g + 1) * HALF], sn, ALU.mult).then_inc(vector_done, V.step(last_read if h else None))
                dve.wait_ge(vector_done, V.now())
            tt(o.rearrange("p (h d) -> p h d", h=nh), a, b, ALU.add).then_inc(vector_done, V.step(name))
            dve.wait_ge(vector_done, V.now())

        def head_norm(name, nh, center):
            if center:
                vsum(hs[:, 0:nh], hn[:, 0:nh, :]).then_inc(vector_done, V.step())
                dve.wait_ge(vector_done, V.now())
                ts(hs[:, 0:nh], hs[:, 0:nh], 1.0 / HD, None, ALU.mult).then_inc(vector_done, V.step())
                dve.wait_ge(vector_done, V.now())
                tt(hn[:, 0:nh, :], hn[:, 0:nh, :], over(hs[:, 0:nh], nh, HD), ALU.subtract).then_inc(vector_done, V.step())
                dve.wait_ge(vector_done, V.now())
            tt(sq[:, 0:nh, :], hn[:, 0:nh, :], hn[:, 0:nh, :], ALU.mult).then_inc(vector_done, V.step())
            dve.wait_ge(vector_done, V.now())
            vsum(hv[:, 0:nh], sq[:, 0:nh, :]).then_inc(vector_done, V.step())
            dve.wait_ge(vector_done, V.now())
            ts(hv[:, 0:nh], hv[:, 0:nh], 1.0 / HD, LN_EPS if center else RMS_EPS, ALU.mult, ALU.add).then_inc(vector_done, V.step((name, "var")))
            dve.wait_ge(vector_done, V.now())
            dve.wait_ge(scalar_done, A.at(V, (name, "sqrt")))
            nc.vector.reciprocal(hs[:, 0:nh], hv[:, 0:nh]).then_inc(vector_done, V.step())
            dve.wait_ge(vector_done, V.now())
            tt(sq[:, 0:nh, :], hn[:, 0:nh, :], over(hs[:, 0:nh], nh, HD), ALU.mult).then_inc(vector_done, V.step())
            dve.wait_ge(vector_done, V.now())

        def layer_norm(name):
            for t in range(TT):
                for h in range(2):
                    nc.vector.bn_stats(st[:, 6 * h:6 * h + 6], x[:, t, h * N:(h + 1) * N]).then_inc(vector_done, V.step())
                    dve.wait_ge(vector_done, V.now())
                dve.sem_inc(waited)
                nc.vector.bn_aggr(agg[:, 2 * t:2 * t + 2], st).then_inc(vector_done, V.step())
                dve.wait_ge(vector_done, V.now())
                ts(rstd[:, t:t + 1], agg[:, 2 * t + 1:2 * t + 2], LN_EPS, None, ALU.add).then_inc(vector_done, V.step((name, "var") if t else None))
                dve.wait_ge(vector_done, V.now())
            dve.wait_ge(scalar_done, A.at(V, (name, "sqrt")))
            nc.vector.reciprocal(rstd[:, TT:2 * TT], rstd[:, 0:TT]).then_inc(vector_done, V.step())
            dve.wait_ge(vector_done, V.now())
            for t in range(TT):
                ts(x[:, t, :], x[:, t, :], agg[:, 2 * t:2 * t + 1], rstd[:, TT + t:TT + t + 1], ALU.subtract, ALU.mult).then_inc(vector_done, V.step())
                dve.wait_ge(vector_done, V.now())
                tt(x[:, t, :], x[:, t, :], rows[:, 0, :], ALU.mult).then_inc(vector_done, V.step())
                dve.wait_ge(vector_done, V.now())
                tt(x[:, t, :], x[:, t, :], rows[:, 1, :], ALU.add).then_inc(vector_done, V.step(name if t else None))
                dve.wait_ge(vector_done, V.now())

        def modulated(tag, name, shift, scale):
            for g in range(KT // 2):
                dve.wait_ge(tensor_done, T.at(V, (tag, g)))
                ps = bank(V, (tag, g))
                for f in range(2):
                    k = 2 * g + f
                    ts(hT[:, k, :], ps[:, f * SEQ:(f + 1) * SEQ], scale[:, k:k + 1], shift[:, k:k + 1], ALU.mult, ALU.add).then_inc(vector_done, V.step(("read", (tag, g)) if f else None))
                    dve.wait_ge(vector_done, V.now())
                V.also((name, g))

        def dve_experts(ne, gated):
            n = NIT[ne]

            def one(e, silu, i, name, column):
                for t in range(TT):
                    dve.wait_ge(scalar_done, A.at(V, (*silu, t), i))
                    up = psum[:, t, FE:2 * FE]
                    if gated:
                        stt(hid[:, t, :], up, column(t), sact[:, t, :], ALU.mult, ALU.mult).then_inc(vector_done, V.step((*name, t)))
                    else:
                        tt(hid[:, t, :], up, sact[:, t, :], ALU.mult).then_inc(vector_done, V.step((*name, t)))

            def static_column(e):
                return lambda t: gate[:, t * NE + e:t * NE + e + 1]

            one(0, ("silu", 0), None, ("hid", 0), static_column(0))
            with nc.vector.Fori(0, n) as i:
                V.loop(f"dve{V.block}", n)
                for j in range(4):
                    one(None, ("silu", "loop", j), i, ("hid", "loop", j),
                        lambda t, j=j: gate[:, bass.ds(i * 4 + (t * NE + 1 + j), 1)])
                V.loop_end()
            for e in range(1 + 4 * n, ne):
                one(e, ("silu", e), None, ("hid", e), static_column(e))

        def dve_first(l):
            V.begin(0, l)
            dve.wait_ge(scalar_done, A.before(V))
            dve.wait_ge(tensor_done, T.before(V))
            for c in range(4):
                ada(c)
            dve.wait_ge(tensor_done, T.at(V, ("acc_used", 3)))
            ps = bank(V, "modm")
            nc.vector.tensor_copy(mod[0], ps[:, 0:KT]).then_inc(vector_done, V.step())
            dve.wait_ge(vector_done, V.now())
            ts(mod[1], ps[:, KT:2 * KT], 1.0, None, ALU.add).then_inc(vector_done, V.step(("read", "modm")))
            dve.wait_ge(vector_done, V.now())
            modulated("xT", "hT", mod[0], mod[1])

            slots = {}

            def rope_chunk(name, t, nh):
                i = len(slots)
                slots[i] = (name, t)
                dve.wait_ge(tensor_done, T.at(V, (name, t)))
                ps = bank(V, (name, t))
                if i >= 3:
                    dve.wait_ge(tensor_done, T.at(V, (slots[i - 3][0], "T", slots[i - 3][1])))
                o = roped[:, i % 3, :]
                if name == "idx":
                    nc.vector.tensor_copy(iw[:, t * NI:(t + 1) * NI], ps[:, IW - IQ:RQ - IQ]).then_inc(vector_done, V.step())
                    dve.wait_ge(vector_done, V.now())
                    rope(ps, nh, t, o[:, 0:nh * HD], None, ("read", (name, t)))
                    nc.vector.tensor_copy(o[:, nh * HD:(nh + 1) * HD], o[:, (nh - 1) * HD:nh * HD]).then_inc(vector_done, V.step(("rope", name, t)))
                    dve.wait_ge(vector_done, V.now())
                else:
                    rope(ps, nh, t, o, ("rope", name, t), ("read", (name, t)))

            def top_k(t):
                nk = (t + 1) * P
                w = score[:, 0:nk]
                dve.wait_ge(scalar_done, A.at(V, ("rel", t)))
                for h in range(NI):
                    prev = cblock[:, C1["vis"] + t * SEQ:C1["vis"] + t * SEQ + nk] if h == 0 else w
                    stt(w, rel[:, (h % 2) * 2 + h // 2, 0:nk], iw[:, t * NI + h:t * NI + h + 1], prev, ALU.mult, ALU.add).then_inc(vector_done, V.step(("rel_read", t) if h == NI - 1 else None))
                    dve.wait_ge(vector_done, V.now())
                for r in range(TOPK // 8):
                    dve.sem_inc(waited)
                    nc.vector.max(top8, w).then_inc(vector_done, V.step())
                    dve.wait_ge(vector_done, V.now())
                    dve.sem_inc(waited)
                    nc.vector.match_replace(w, top8, w, TAKEN).then_inc(vector_done, V.step())
                    dve.wait_ge(vector_done, V.now())
                ts(bias[:, t, 0:nk], w, -2.0e38, -BIG, ALU.is_gt, ALU.mult).then_inc(vector_done, V.step())
                dve.wait_ge(vector_done, V.now())

            def scale_iw(t):
                ts(iw[:, t * NI:(t + 1) * NI], iw[:, t * NI:(t + 1) * NI], (NI * HD) ** -0.5, None, ALU.mult).then_inc(vector_done, V.step())
                dve.wait_ge(vector_done, V.now())

            for t in range(TT):
                rope_chunk("idx", t, NI + 1)
                scale_iw(t)
            for t in range(TT):
                rope_chunk("aq", t, NA)
            for t in range(TT):
                rope_chunk("ak", t, NA)
            top_k(0)
            for t in range(TT):
                rope_chunk("rqk", t, 2 * NR)
            top_k(1)

            dve.wait_ge(tensor_done, T.at(V, "gates"))
            ps = bank(V, "gates")
            g4 = grow[0:NR]
            dve.wait_ge(params_loaded, params_count(V))
            ts(g4[:, 0, :], ps[0:NR, 0:SEQ], ibias[0:NR], None, ALU.add).then_inc(vector_done, V.step())
            dve.wait_ge(vector_done, V.now())
            ts(g4[:, 1, :], ps[0:NR, SEQ:2 * SEQ], fbias[0:NR], None, ALU.add).then_inc(vector_done, V.step(("read", "gates")))
            dve.wait_ge(vector_done, V.now())
            stt(g4[:, 5, :], g4[:, 1, :], -1.0, g4[:, 1, :], ALU.mult, ALU.min).then_inc(vector_done, V.step("negabs"))
            dve.wait_ge(vector_done, V.now())
            ts(g4[:, 1, :], g4[:, 1, :], 0.0, None, ALU.min).then_inc(vector_done, V.step())
            dve.wait_ge(vector_done, V.now())
            for b in range(4):
                if b % 2 == 0:
                    dve.wait_ge(scalar_done, A.at(V, ("mqk", "c", b // 2)))
                o = qkT[:, b, :]
                ts(o, cin[:, b, 0:SEQ], convw[:, b, 0:1], convw[:, b, CONV:CONV + 1], ALU.mult, ALU.add).then_inc(vector_done, V.step())
                dve.wait_ge(vector_done, V.now())
                for j in range(1, CONV):
                    stt(o, cin[:, b, j:j + SEQ], convw[:, b, j:j + 1], o, ALU.mult, ALU.add).then_inc(vector_done, V.step("conv" if b == 3 and j == CONV - 1 else None))
                    dve.wait_ge(vector_done, V.now())
            dve.wait_ge(scalar_done, A.at(V, "softplus"))
            tt(g4[:, 4, :], g4[:, 1, :], g4[:, 5, :], ALU.subtract).then_inc(vector_done, V.step())
            dve.wait_ge(vector_done, V.now())
            nc.vector.tensor_tensor_scan(g4[:, 1, :], ones[0:NR, 0:SEQ], g4[:, 4, :], 0.0, ALU.mult, ALU.add).then_inc(vector_done, V.step())
            dve.wait_ge(vector_done, V.now())
            tt(g4[:, 2, :], g4[:, 0, :], g4[:, 1, :], ALU.subtract).then_inc(vector_done, V.step())
            dve.wait_ge(vector_done, V.now())
            nc.vector.tensor_tensor_scan(g4[:, 3, :], g4[:, 2, :], g4[:, 2, :], 0.0, ALU.max, ALU.max).then_inc(vector_done, V.step())
            dve.wait_ge(vector_done, V.now())
            tt(g4[:, 4, :], g4[:, 1, :], g4[:, 3, :], ALU.add).then_inc(vector_done, V.step("bm"))
            dve.wait_ge(vector_done, V.now())

            for s, (t, i) in enumerate(ATT):
                nk = (t + 1) * P
                dve.wait_ge(tensor_done, T.at(V, ("att", "S", s)))
                ps = bank(V, ("att", "S", s))
                if s >= 2:
                    dve.wait_ge(tensor_done, T.at(V, ("att", "PT", s - 2)))
                o = sm[:, s % 2, 0:2 * nk].rearrange("p (h k) -> p h k", h=2)
                bb = bias[:, t, 0:nk].unsqueeze(1).to_broadcast([P, 2, nk])
                stt(o, ps[:, :, 0:nk], HD ** -0.5, bb, ALU.mult, ALU.add).then_inc(vector_done, V.step(("read", ("att", "S", s))))
                dve.wait_ge(vector_done, V.now())
                nc.vector.tensor_reduce(ngm[:, 2 * (s % 2):2 * (s % 2) + 2], o, AX.X, ALU.max, negate=True).then_inc(vector_done, V.step(("att", "max", s)))
                dve.wait_ge(vector_done, V.now())

            def att_out(t):
                dve.wait_ge(scalar_done, A.at(V, ("att", "exp", (t + 1) * (NA // 2) - 1)))
                nc.vector.reciprocal(rinv[:, t * NA:(t + 1) * NA], rsum[:, t * NA:(t + 1) * NA]).then_inc(vector_done, V.step())
                dve.wait_ge(vector_done, V.now())
                dve.wait_ge(tensor_done, T.at(V, ("att", "PV", (t + 1) * (NA // 2) - 1)))
                tt(o_cat[:, t, 0:N].rearrange("p (h d) -> p h d", h=NA), bank(V, ("att", "O", t)).rearrange("p (h d) -> p h d", h=NA), over(rinv[:, t * NA:(t + 1) * NA], NA, HD), ALU.mult).then_inc(vector_done, V.step(("read", ("att", "O", t))))
                dve.wait_ge(vector_done, V.now())

            att_out(0)
            att_out(1)

            for h in range(NR):
                dve.wait_ge(tensor_done, T.at(V, ("ret", "S", h)))
                ps = bank(V, ("ret", "S", h))
                if h >= 2:
                    dve.wait_ge(tensor_done, T.at(V, ("ret", "PV", h - 2)))
                tt(sT[:, h % 2, :], ps[:, 0:384], cblock[:, h * 384:(h + 1) * 384], ALU.mult).then_inc(vector_done, V.step(("ret", "sT", h)))
                dve.wait_ge(vector_done, V.now())
                V.also(("read", ("ret", "S", h)))
            dve.wait_ge(tensor_done, T.at(V, ("ret", "PV", NR - 1)))
            nc.vector.tensor_copy(hn.rearrange("p h d -> p (h d)"), bank(V, ("ret", "O"))).then_inc(vector_done, V.step(("read", ("ret", "O"))))
            dve.wait_ge(vector_done, V.now())
            dve.wait_ge(tensor_done, T.at(V, "gcol"))
            ps = bank(V, "gcol")
            nc.vector.tensor_copy(gcol, ps[:, 0:16]).then_inc(vector_done, V.step(("read", "gcol")))
            dve.wait_ge(vector_done, V.now())
            head_norm("ret", 8, True)
            dve.wait_ge(scalar_done, A.at(V, ("rvg", "g", 1)))
            tt(o_cat[:, :, 512:768], sq.rearrange("p (t h) d -> p t (h d)", t=TT), rg, ALU.mult).then_inc(vector_done, V.step())
            dve.wait_ge(vector_done, V.now())

            for h in range(NR):
                dve.wait_ge(tensor_done, T.at(V, ("ml", "M", h)))
                ps = bank(V, ("ml", "M", h))
                if h >= 2:
                    dve.wait_ge(tensor_done, T.at(V, ("ml", "PV", h - 2)))
                ca = cblock[:, C1["causal"]:C1["causal"] + SEQ]
                stt(wT[:, h % 2, 0:SEQ], ps[:, 0:SEQ], gcol[:, h:h + 1], ca, ALU.add, ALU.add).then_inc(vector_done, V.step())
                dve.wait_ge(vector_done, V.now())
                stt(wT[:, h % 2, SEQ:384], ps[:, P:SEQ], gcol[:, 8 + h:9 + h], ca[:, 0:P], ALU.add, ALU.add).then_inc(vector_done, V.step(("ml", "arg", h)))
                dve.wait_ge(vector_done, V.now())
                V.also(("read", ("ml", "M", h)))
                dve.wait_ge(tensor_done, T.at(V, ("ml", "S", h)))
                ps = bank(V, ("ml", "S", h))
                dve.wait_ge(scalar_done, A.at(V, ("ml", "exp", h)))
                stt(sT[:, h % 2, :], ps[:, 0:384], HD ** -0.5, wT[:, h % 2, :], ALU.mult, ALU.mult).then_inc(vector_done, V.step(("ml", "sT", h)))
                dve.wait_ge(vector_done, V.now())
                V.also(("read", ("ml", "S", h)))
            dve.wait_ge(tensor_done, T.at(V, ("ml", "PV", NR - 1)))
            dve.wait_ge(scalar_done, A.at(V, ("mvo", "o", 1)))
            for t in range(TT):
                ps = bank(V, ("ml", "O", t))
                o = ps[:, 0:NR * (HD + 1)].rearrange("p (h d) -> p h d", h=NR)
                nc.vector.tensor_copy(den, o[:, :, HD:HD + 1]).then_inc(vector_done, V.step())
                dve.wait_ge(vector_done, V.now())
                stt(hv[:, 0:NR], den, -1.0, den, ALU.mult, ALU.max).then_inc(vector_done, V.step())
                dve.wait_ge(vector_done, V.now())
                tt(hv[:, 0:NR], hv[:, 0:NR], gcol[:, 8 * t + NR:8 * t + 2 * NR], ALU.max).then_inc(vector_done, V.step())
                dve.wait_ge(vector_done, V.now())
                nc.vector.reciprocal(hs[:, 0:NR], hv[:, 0:NR]).then_inc(vector_done, V.step())
                dve.wait_ge(vector_done, V.now())
                tt(hn[:, NR * t:NR * (t + 1), :], o[:, :, 0:HD], over(hs[:, 0:NR], NR, HD), ALU.mult).then_inc(vector_done, V.step(("read", ("ml", "O", t))))
                dve.wait_ge(vector_done, V.now())
            hflat = hn.rearrange("p (t h) d -> p t (h d)", t=TT)
            tt(hflat, hflat, mo, ALU.mult).then_inc(vector_done, V.step())
            dve.wait_ge(vector_done, V.now())
            head_norm("ml", 8, True)
            nc.vector.tensor_copy(o_cat[:, :, 768:1024], sq.rearrange("p (t h) d -> p t (h d)", t=TT)).then_inc(vector_done, V.step("o_cat"))
            dve.wait_ge(vector_done, V.now())

            def gate_row(c, h):
                ada(c)
                dve.wait_ge(tensor_done, T.at(V, ("acc_used", c)))
                ts(gb[:, h * N:(h + 1) * N], bank(V, ("gate_row", c)), 1.0, None, ALU.add).then_inc(vector_done, V.step(("read", ("gate_row", c))))
                dve.wait_ge(vector_done, V.now())

            gate_row(4, 0)
            gate_row(5, 1)

            def residual(ps, t, h, read):
                o = x[:, t, h * N:(h + 1) * N]
                tt(tmp[:, 0, :], ps, gb[:, h * N:(h + 1) * N], ALU.mult).then_inc(vector_done, V.step(read))
                dve.wait_ge(vector_done, V.now())
                stt(o, o, ALPHA, tmp[:, 0, :], ALU.mult, ALU.add).then_inc(vector_done, V.step())
                dve.wait_ge(vector_done, V.now())

            for h in range(2):
                for t in range(TT):
                    dve.wait_ge(tensor_done, T.at(V, ("wo", t, h)))
                    residual(bank(V, ("wo", t, h)), t, h, ("read", ("wo", t, h)))
            layer_norm("ln1")

            for c in range(6, 10):
                ada(c)
            dve.wait_ge(tensor_done, T.at(V, ("acc_used", 9)))
            ps = bank(V, "modf")
            nc.vector.tensor_copy(mod[2], ps[:, 0:KT]).then_inc(vector_done, V.step())
            dve.wait_ge(vector_done, V.now())
            ts(mod[3], ps[:, KT:2 * KT], 1.0, None, ALU.add).then_inc(vector_done, V.step(("read", "modf")))
            dve.wait_ge(vector_done, V.now())
            gate_row(10, 0)
            gate_row(11, 1)
            modulated("xT2", "hT2", mod[2], mod[3])

            dve.wait_ge(scalar_done, A.at(V, "router"))
            v3 = lambda a, n: a.rearrange("p (t n) -> p t n", n=n)
            tt(v3(biased, NE), v3(scores, NE), br[:, :].unsqueeze(1).to_broadcast([P, TT, NE]), ALU.add).then_inc(vector_done, V.step())
            dve.wait_ge(vector_done, V.now())
            b4, pr = v3(biased, EG), v3(pairs, 6)
            tt(pr[:, :, 0:2], b4[:, :, 0:2], b4[:, :, 2:4], ALU.add).then_inc(vector_done, V.step())
            dve.wait_ge(vector_done, V.now())
            tt(pr[:, :, 2:4], b4[:, :, 0:4:2], b4[:, :, 1:4:2], ALU.add).then_inc(vector_done, V.step())
            dve.wait_ge(vector_done, V.now())
            tt(pr[:, :, 4:5], b4[:, :, 0:1], b4[:, :, 3:4], ALU.add).then_inc(vector_done, V.step())
            dve.wait_ge(vector_done, V.now())
            tt(pr[:, :, 5:6], b4[:, :, 1:2], b4[:, :, 2:3], ALU.add).then_inc(vector_done, V.step())
            dve.wait_ge(vector_done, V.now())
            vmax(gsum, pr).then_inc(vector_done, V.step())
            dve.wait_ge(vector_done, V.now())

            def first_best(o, src, key, n, weights):
                vmax(t2, v3(src, n)).then_inc(vector_done, V.step())
                dve.wait_ge(vector_done, V.now())
                tt(v3(key, n), v3(src, n), over(t2, TT, n), ALU.is_equal).then_inc(vector_done, V.step())
                dve.wait_ge(vector_done, V.now())
                tt(v3(key, n), v3(key, n), weights.unsqueeze(1).to_broadcast([P, TT, n]), ALU.mult).then_inc(vector_done, V.step())
                dve.wait_ge(vector_done, V.now())
                vmax(t2, v3(key, n)).then_inc(vector_done, V.step())
                dve.wait_ge(vector_done, V.now())
                tt(v3(o, n), v3(key, n), over(t2, TT, n), ALU.is_equal).then_inc(vector_done, V.step())
                dve.wait_ge(vector_done, V.now())

            first4 = cshared[:, CONST["first4"]:CONST["first4"] + NG]
            first16 = cshared[:, CONST["first16"]:CONST["first16"] + NE]
            first_best(gsum, gsum, key4, NG, first4)
            ts(gsum, gsum, -1.0, BIG, ALU.add, ALU.mult).then_inc(vector_done, V.step())
            dve.wait_ge(vector_done, V.now())
            tt(v3(bmask, EG), b4, over(gsum, 8, EG), ALU.add).then_inc(vector_done, V.step())
            dve.wait_ge(vector_done, V.now())
            first_best(sel, bmask, onehot, NE, first16)
            stt(bmask, sel, -BIG, bmask, ALU.mult, ALU.add).then_inc(vector_done, V.step())
            dve.wait_ge(vector_done, V.now())
            first_best(biased, bmask, onehot, NE, first16)
            tt(sel, sel, biased, ALU.add).then_inc(vector_done, V.step())
            dve.wait_ge(vector_done, V.now())
            tt(gate, sel, scores, ALU.mult).then_inc(vector_done, V.step())
            dve.wait_ge(vector_done, V.now())
            vsum(t2, v3(gate, NE)).then_inc(vector_done, V.step())
            dve.wait_ge(vector_done, V.now())
            nc.vector.reciprocal(t2, t2).then_inc(vector_done, V.step())
            dve.wait_ge(vector_done, V.now())
            tt(v3(gate, NE), v3(gate, NE), over(t2, TT, NE), ALU.mult).then_inc(vector_done, V.step())
            dve.wait_ge(vector_done, V.now())
            dve_experts(NE, True)
            dve.wait_ge(vector_done, V.now())
            for t in range(TT):
                dve.wait_ge(tensor_done, T.at(V, ("dn0", NE - 1) if t == 0 else ("dn1", NE - 1)))
                for h in range(2):
                    residual(psum[:, 4 + 2 * t + h, :], t, h, None)
            dve.wait_ge(rows_loaded, rows_count(V))
            layer_norm("ln2")
            V.end()

        def rms(name):
            dve.wait_ge(scalar_done, A.at(V, (name, "ss")))
            ts(rstd[:, 0:TT], agg[:, 0:TT], 1.0 / D, RMS_EPS, ALU.mult, ALU.add).then_inc(vector_done, V.step((name, "var")))
            dve.wait_ge(vector_done, V.now())
            dve.wait_ge(scalar_done, A.at(V, (name, "sqrt")))
            nc.vector.reciprocal(rstd[:, TT:2 * TT], rstd[:, 0:TT]).then_inc(vector_done, V.step())
            dve.wait_ge(vector_done, V.now())

        def pre_norm(name):
            rms(("pre", name))
            for t in range(TT):
                ts(o_cat[:, t, :], x[:, t, :], rstd[:, TT + t:TT + t + 1], None, ALU.mult).then_inc(vector_done, V.step(("xn", name) if t else None))
                dve.wait_ge(vector_done, V.now())

        def gained(tag, name, gains):
            for g in range(KT // 2):
                dve.wait_ge(tensor_done, T.at(V, (tag, g)))
                ps = bank(V, (tag, g))
                for f in range(2):
                    k = 2 * g + f
                    ts(hT[:, k, :], ps[:, f * SEQ:(f + 1) * SEQ], gcols[:, gains + k:gains + k + 1], None, ALU.mult).then_inc(vector_done, V.step(("read", (tag, g)) if f else None))
                    dve.wait_ge(vector_done, V.now())
                V.also((name, g))

        def post_norm(name, row):
            rms(("post", name))
            for t in range(TT):
                stt(y2[:, t, :], y2[:, t, :], rstd[:, TT + t:TT + t + 1], rows[:, row, :], ALU.mult, ALU.mult).then_inc(vector_done, V.step())
                dve.wait_ge(vector_done, V.now())
                tt(x[:, t, :], x[:, t, :], y2[:, t, :], ALU.add).then_inc(vector_done, V.step(("x", name) if t else None))
                dve.wait_ge(vector_done, V.now())

        def dve_second(l):
            V.begin(1, l)
            dve.wait_ge(scalar_done, A.before(V))
            dve.wait_ge(tensor_done, T.before(V))
            dve.wait_ge(params_loaded, params_count(V))
            dve.wait_ge(const_loaded, 16)
            lq = lprod.rearrange("p (a d) -> p a d", a=2)
            tt(lq, lamrow[:, 0:2, :], lamrow[:, 2:4, :], ALU.mult).then_inc(vector_done, V.step())
            dve.wait_ge(vector_done, V.now())
            vsum(lsum, lq).then_inc(vector_done, V.step("lsum"))
            dve.wait_ge(vector_done, V.now())
            ts(subrow, subrow, lamc[:, 1:2], None, ALU.mult).then_inc(vector_done, V.step())
            dve.wait_ge(vector_done, V.now())
            dve.wait_ge(scalar_done, A.at(V, "lexp"))
            tt(lam, lsum[:, 0:1], lsum[:, 1:2], ALU.subtract).then_inc(vector_done, V.step())
            dve.wait_ge(vector_done, V.now())
            tt(lam, lam, lamc[:, 0:1], ALU.add).then_inc(vector_done, V.step())
            dve.wait_ge(vector_done, V.now())
            dve.wait_ge(tensor_done, T.at(V, "gains"))
            ps = bank(V, "gains")
            nc.vector.tensor_copy(gcols, ps[:, 0:3 * KT + GG]).then_inc(vector_done, V.step(("read", "gains")))
            dve.wait_ge(vector_done, V.now())
            pre_norm("mix")
            gained("xT", "hT", 0)

            for t in range(TT):
                dve.wait_ge(scalar_done, A.at(V, ("buv", "c", t)))
                nc.vector.bn_stats(st[:, 0:6], buv[:, t, GW:2 * GW]).then_inc(vector_done, V.step())
                dve.wait_ge(vector_done, V.now())
                dve.sem_inc(waited)
                nc.vector.bn_aggr(agg[:, 2 * t:2 * t + 2], st[:, 0:6]).then_inc(vector_done, V.step())
                dve.wait_ge(vector_done, V.now())
                ts(rstd[:, t:t + 1], agg[:, 2 * t + 1:2 * t + 2], RMS_EPS, None, ALU.add).then_inc(vector_done, V.step(("vn", "var") if t else None))
                dve.wait_ge(vector_done, V.now())
            dve.wait_ge(scalar_done, A.at(V, ("vn", "sqrt")))
            nc.vector.reciprocal(rstd[:, TT:2 * TT], rstd[:, 0:TT]).then_inc(vector_done, V.step())
            dve.wait_ge(vector_done, V.now())
            for t in range(TT):
                ts(vn[:, t, :], buv[:, t, GW:2 * GW], agg[:, 2 * t:2 * t + 1], rstd[:, TT + t:TT + t + 1], ALU.subtract, ALU.mult).then_inc(vector_done, V.step())
                dve.wait_ge(vector_done, V.now())
                tt(vn[:, t, :], vn[:, t, :], glnrow[:, 0, :], ALU.mult).then_inc(vector_done, V.step())
                dve.wait_ge(vector_done, V.now())
                tt(vn[:, t, :], vn[:, t, :], glnrow[:, 1, :], ALU.add).then_inc(vector_done, V.step(("vn", t)))
                dve.wait_ge(vector_done, V.now())

            scale = DQK ** -0.5

            def diff_in(s):
                t, h = DIFF[s]
                dve.wait_ge(tensor_done, T.at(V, ("diff", "S", s)))
                ps = bank(V, ("diff", "S", s))
                dist = cblock[:, t * SEQ:(t + 1) * SEQ].unsqueeze(1).to_broadcast([P, 2, SEQ])
                o = sm2[:, s % 2, :].rearrange("p (c k) -> p c k", c=2)
                stt(o, dist, -DIFF_SLOPES[h] / scale, ps[:, :, 0:SEQ], ALU.mult, ALU.add).then_inc(vector_done, V.step(("read", ("diff", "S", s))))
                dve.wait_ge(vector_done, V.now())
                n = ngm[:, 2 * (s % 2):2 * (s % 2) + 2]
                nc.vector.tensor_reduce(n, o, AX.X, ALU.max, negate=True).then_inc(vector_done, V.step())
                dve.wait_ge(vector_done, V.now())
                ts(n, n, scale, None, ALU.mult).then_inc(vector_done, V.step(("diff", "max", s)))
                dve.wait_ge(vector_done, V.now())

            def diff_out(s):
                dve.wait_ge(scalar_done, A.at(V, ("diff", "exp", s)))
                r = rsum[:, 2 * (s % 2):2 * (s % 2) + 2]
                nc.vector.reciprocal(r2, r).then_inc(vector_done, V.step())
                dve.wait_ge(vector_done, V.now())
                tt(r2[:, 1:2], r2[:, 1:2], lam, ALU.mult).then_inc(vector_done, V.step())
                dve.wait_ge(vector_done, V.now())
                p0, p1 = sm2[:, s % 2, 0:SEQ], sm2[:, s % 2, SEQ:2 * SEQ]
                ts(p1, p1, r2[:, 1:2], None, ALU.mult).then_inc(vector_done, V.step())
                dve.wait_ge(vector_done, V.now())
                if s >= 2:
                    dve.wait_ge(tensor_done, T.at(V, ("diff", "PT", s - 2)))
                stt(at2[:, s % 2, :], p0, r2[:, 0:1], p1, ALU.mult, ALU.subtract).then_inc(vector_done, V.step(("diff", "at", s)))
                dve.wait_ge(vector_done, V.now())

            diff_in(0)
            for s in range(len(DIFF)):
                if s + 1 < len(DIFF):
                    diff_in(s + 1)
                diff_out(s)

            def diff_norm(t):
                dve.wait_ge(tensor_done, T.at(V, ("diff", "PV", (t + 1) * DH - 1)))
                nc.vector.tensor_copy(hn2, bank(V, ("diff", "O", t))[:, 0:DH * HD].rearrange("p (h d) -> p h d", h=DH)).then_inc(vector_done, V.step(("read", ("diff", "O", t))))
                dve.wait_ge(vector_done, V.now())
                tt(sq2, hn2, hn2, ALU.mult).then_inc(vector_done, V.step())
                dve.wait_ge(vector_done, V.now())
                vsum(hv[:, 0:DH], sq2).then_inc(vector_done, V.step())
                dve.wait_ge(vector_done, V.now())
                ts(hv[:, 0:DH], hv[:, 0:DH], 1.0 / HD, RMS_EPS, ALU.mult, ALU.add).then_inc(vector_done, V.step(("diff", "var", t)))
                dve.wait_ge(vector_done, V.now())
                dve.wait_ge(scalar_done, A.at(V, ("diff", "sqrt", t)))
                nc.vector.reciprocal(hs[:, 0:DH], hv[:, 0:DH]).then_inc(vector_done, V.step())
                dve.wait_ge(vector_done, V.now())
                tt(hn2, hn2, over(hs[:, 0:DH], DH, HD), ALU.mult).then_inc(vector_done, V.step())
                dve.wait_ge(vector_done, V.now())
                tt(o_cat[:, t, 0:DH * HD].rearrange("p (h d) -> p h d", h=DH), hn2, subrow.unsqueeze(1).to_broadcast([P, DH, HD]), ALU.mult).then_inc(vector_done, V.step())
                dve.wait_ge(vector_done, V.now())

            diff_norm(0)
            diff_norm(1)

            dve.wait_ge(tensor_done, T.at(V, "mix"))
            ps = bank(V, "mix")
            for g in range(GG):
                stt(o_cat[:, :, 384 + g * HD:384 + (g + 1) * HD], ps[:, g * P:(g + 1) * P].rearrange("p (t d) -> p t d", t=TT), gcols[:, 3 * KT + g:3 * KT + g + 1], buv[:, :, g * HD:(g + 1) * HD], ALU.add, ALU.mult).then_inc(vector_done, V.step(("read", "mix") if g == GG - 1 else None))
                dve.wait_ge(vector_done, V.now())

            wscale = HD ** -0.5
            for s, (t, g) in enumerate(WIN):
                dve.wait_ge(tensor_done, T.at(V, ("win", "S", s)))
                ps = bank(V, ("win", "S", s))
                if s >= 2:
                    dve.wait_ge(tensor_done, T.at(V, ("win", "PT", s - 2)))
                wd = cblock[:, C2["wdist"] + t * SEQ:C2["wdist"] + (t + 1) * SEQ]
                for h in range(2):
                    stt(sm2[:, s % 2, h * SEQ:(h + 1) * SEQ], wd, -SWA_SLOPES[h * WG + g] / wscale, ps[:, h, 0:SEQ], ALU.mult, ALU.add).then_inc(vector_done, V.step(("read", ("win", "S", s)) if h else None))
                    dve.wait_ge(vector_done, V.now())
                vmax(nm2, sm2[:, s % 2, :].rearrange("p (h k) -> p h k", h=2)).then_inc(vector_done, V.step())
                dve.wait_ge(vector_done, V.now())
                sk = sinks[:, g:g + WG + 1:WG]
                stt(msink, nm2, wscale, sk, ALU.mult, ALU.max).then_inc(vector_done, V.step())
                dve.wait_ge(vector_done, V.now())
                c = t * WH + g
                tt(dsum[:, c:c + WG + 1:WG], sk, msink, ALU.subtract).then_inc(vector_done, V.step())
                dve.wait_ge(vector_done, V.now())
                ts(ngm[:, 2 * (s % 2):2 * (s % 2) + 2], msink, -1.0, None, ALU.mult).then_inc(vector_done, V.step(("win", "max", s)))
                dve.wait_ge(vector_done, V.now())

            def win_out(t):
                dve.wait_ge(scalar_done, A.at(V, ("win", "sink", t)))
                tt(rinv[:, 0:WH], dsum[:, t * WH:(t + 1) * WH], rsum[:, t * NA:t * NA + WH], ALU.add).then_inc(vector_done, V.step())
                dve.wait_ge(vector_done, V.now())
                nc.vector.reciprocal(rinv[:, WH:2 * WH], rinv[:, 0:WH]).then_inc(vector_done, V.step())
                dve.wait_ge(vector_done, V.now())
                dve.wait_ge(tensor_done, T.at(V, ("win", "PV", (t + 1) * WG - 1)))
                tt(o_cat[:, t, 640:1024].rearrange("p (h d) -> p h d", h=WH), bank(V, ("win", "O", t))[:, 0:WH * HD].rearrange("p (h d) -> p h d", h=WH), over(rinv[:, WH:2 * WH], WH, HD), ALU.mult).then_inc(vector_done, V.step(("read", ("win", "O", t))))
                dve.wait_ge(vector_done, V.now())

            win_out(0)
            win_out(1)
            V.also("o_cat")
            post_norm("mix", 0)
            pre_norm("ffn")
            gained("xT2", "hT2", KT)
            dve_experts(NF, False)
            dve.wait_ge(vector_done, V.now())
            post_norm("ffn", 1)
            pre_norm("ple")
            gained("xT3", "hT3", 2 * KT)
            for h in range(2):
                for t in range(TT):
                    dve.wait_ge(scalar_done, A.at(V, ("sig", t, h)))
                    o = y2[:, t, h * N:(h + 1) * N]
                    e = (e2 if t == 0 else e2b)[:, h * N:(h + 1) * N]
                    tt(o, o, e, ALU.mult).then_inc(vector_done, V.step("eg" if (h, t) == (1, 1) else None))
                    dve.wait_ge(vector_done, V.now())
            dve.wait_ge(rows_loaded, rows_count(V))
            post_norm("ple", 0)
            V.end()

        @block.vector
        def _(dve):
            nc.vector.memset(ones[:, :], 1.0).then_inc(vector_done, V.step())
            dve.wait_ge(vector_done, V.now())
            nc.vector.memset(zeros[:, :], 0.0).then_inc(vector_done, V.step())
            dve.wait_ge(vector_done, V.now())
            nc.vector.memset(cin, 0.0).then_inc(vector_done, V.step())
            dve.wait_ge(vector_done, V.now())
            nc.vector.memset(mv, 1.0).then_inc(vector_done, V.step())
            dve.wait_ge(vector_done, V.now())
            dve.wait_ge(start_loaded, 16 * 8)
            nc.vector.tensor_copy(posf, posi[:, :]).then_inc(vector_done, V.step())
            dve.wait_ge(vector_done, V.now())
            invf = cshared[:, CONST["invf"]:CONST["invf"] + HALF]
            c1 = 6.28125
            c2 = float(np.float32(np.float16(TWO_PI - c1)))
            c3 = TWO_PI - c1 - c2
            for t in range(TT):
                ang, k, r = tmp[:, 0, 0:HALF], tmp[:, 0, HALF:HD], tmp[:, 1, 0:HALF]
                ts(ang, invf, posf[:, t:t + 1], None, ALU.mult).then_inc(vector_done, V.step())
                dve.wait_ge(vector_done, V.now())
                for cos in (0, 1):
                    ts(k, ang, 1.0 / TWO_PI, 0.25 * cos, ALU.mult, ALU.add).then_inc(vector_done, V.step())
                    dve.wait_ge(vector_done, V.now())
                    ts(k, k, ROUND, None, ALU.add).then_inc(vector_done, V.step())
                    dve.wait_ge(vector_done, V.now())
                    ts(k, k, -ROUND, None, ALU.add).then_inc(vector_done, V.step())
                    dve.wait_ge(vector_done, V.now())
                    stt(r, k, -c1, ang, ALU.mult, ALU.add).then_inc(vector_done, V.step())
                    dve.wait_ge(vector_done, V.now())
                    for c in (c2, c3):
                        stt(r, k, -c, r, ALU.mult, ALU.add).then_inc(vector_done, V.step())
                        dve.wait_ge(vector_done, V.now())
                    ts(r, r, np.pi / 2 * cos, None, ALU.add).then_inc(vector_done, V.step())
                    dve.wait_ge(vector_done, V.now())
                    o = (cosf if cos else sinf)[:, t, HALF:HD]
                    ts(o, r, -3.141592, 3.141592, ALU.max, ALU.min).then_inc(vector_done, V.step(("angle", t, cos)))
                    dve.wait_ge(vector_done, V.now())
            dve.wait_ge(scalar_done, A.at(V, "sigc"))
            tt(cact[:, :], cact[:, :], psum[:, 0, 0:KT], ALU.mult).then_inc(vector_done, V.step())
            dve.wait_ge(vector_done, V.now())
            dve.wait_ge(scalar_done, A.at(V, "trig"))
            for t in range(TT):
                nc.vector.tensor_copy(cosf[:, t, 0:HALF], cosf[:, t, HALF:HD]).then_inc(vector_done, V.step())
                dve.wait_ge(vector_done, V.now())
                ts(sinf[:, t, 0:HALF], sinf[:, t, HALF:HD], -1.0, None, ALU.mult).then_inc(vector_done, V.step(("rope_tables") if t else None))
                dve.wait_ge(vector_done, V.now())
            with dve.Fori(0, DEPTH) as l:
                dve_first(l)
            with dve.Fori(0, DEPTH) as l:
                dve_second(l)

        def activate(o, a, f, **k):
            return nc.scalar.activation(o, a, f, **k)

        def copy(o, a):
            return nc.scalar.activation(o, a, ACT.Copy)

        def act_experts(ne):
            n = NIT[ne]

            def one(gu0, gu1, trs, i0, i, silu, copied):
                for t, (gu, it) in enumerate(((gu0, i0), (gu1, i))):
                    act.wait_ge(tensor_done, T.at(A, gu, it))
                    activate(sact[:, t, :], psum[:, t, 0:FE], ACT.Silu).then_inc(scalar_done, A.step((*silu, t)))
                for t in range(TT):
                    act.wait_ge(tensor_done, T.at(A, (*trs, t), i))
                    copy(hidT[:, t, :, :].rearrange("p f n -> p (f n)"), psum[:, 2 + t, 0:FE]).then_inc(scalar_done, A.step((*copied, t)))

            one(("gu0", 0), ("gu1", 0), ("tr", 0), None, None, ("silu", 0), ("hidT", 0))
            with nc.scalar.Fori(0, n) as i:
                A.loop(f"act{A.block}", n)
                for j in range(4):
                    first = (("gu0", "loop", j - 1), i) if j else (("gu0", "loop", 3), i - 1)
                    one(first[0], ("gu1", "loop", j), ("tr", "loop", j), first[1], i, ("silu", "loop", j), ("hidT", "loop", j))
                A.loop_end()
            for e in range(1 + 4 * n, ne):
                first = (("gu0", "loop", 3), n - 1) if e == 1 + 4 * n else (("gu0", e), None)
                one(first[0], ("gu1", e), ("tr", e), first[1], None, ("silu", e), ("hidT", e))

        def root_of(name, var, o=None):
            act.wait_ge(vector_done, V.at(A, (name, "var")))
            activate(var, var, ACT.Sqrt).then_inc(scalar_done, A.step((name, "sqrt")))
            act.wait_ge(scalar_done, A.now())

        def act_first(l):
            A.begin(0, l)
            act.wait_ge(vector_done, V.before(A))
            act.wait_ge(tensor_done, T.before(A))

            def rows_T(name, dst, blocks):
                for t in range(TT):
                    act.wait_ge(tensor_done, T.at(A, (name, "T", t)))
                    ps = bank(A, (name, "T", t))
                    copy(dst[:, 0:blocks, t * P:(t + 1) * P], ps[:, 0:blocks * P].rearrange("p (b n) -> p b n", b=blocks)).then_inc(scalar_done, A.step((name, "Tc", t)))
                    act.wait_ge(scalar_done, A.now())
                    A.also(("read", (name, "T", t)))

            rows_T("idx", idxT, 3)

            def relu(t):
                nk = (t + 1) * P
                if t:
                    act.wait_ge(vector_done, V.at(A, ("rel_read", t - 1)))
                act.wait_ge(tensor_done, T.at(A, ("idxS", t)))
                ps = bank(A, ("idxS", t))
                for h in range(2):
                    activate(rel[:, 2 * h:2 * h + 2, 0:nk], ps[:, h, :].rearrange("p (i k) -> p i k", i=2)[:, :, 0:nk], ACT.Relu).then_inc(scalar_done, A.step(("rel", t) if h else None))
                    act.wait_ge(scalar_done, A.now())
                A.also(("read", ("idxS", t)))

            relu(0)
            rows_T("aq", aqT, 4)
            relu(1)
            for t in range(TT):
                act.wait_ge(tensor_done, T.at(A, ("av", t)))
                ps = bank(A, ("av", t))
                copy(av[:, t, :], ps).then_inc(scalar_done, A.step(("av", t)))
                act.wait_ge(scalar_done, A.now())
                A.also(("read", ("av", t)))
            rows_T("ak", akT, 4)
            for t in range(TT):
                act.wait_ge(tensor_done, T.at(A, ("rvg", t)))
                ps = bank(A, ("rvg", t))
                copy(rv[:, t, :], ps[:, 0:256]).then_inc(scalar_done, A.step(("rvg", t)))
                act.wait_ge(scalar_done, A.now())
                activate(rg[:, t, :], ps[:, 256:512], ACT.Silu).then_inc(scalar_done, A.step(("rvg", "g", t)))
                act.wait_ge(scalar_done, A.now())
                A.also(("read", ("rvg", t)))
            rows_T("rqk", rrT, 4)
            for b in range(2):
                act.wait_ge(tensor_done, T.at(A, ("mqk", b)))
                ps = bank(A, ("mqk", b))
                copy(cin[:, 2 * b:2 * b + 2, CONV - 1:CONV - 1 + SEQ], ps.rearrange("p (b n) -> p b n", b=2)).then_inc(scalar_done, A.step(("mqk", "c", b)))
                act.wait_ge(scalar_done, A.now())
                A.also(("read", ("mqk", b)))
            for t in range(TT):
                act.wait_ge(tensor_done, T.at(A, ("mvo", t)))
                ps = bank(A, ("mvo", t))
                copy(mv[:, t, :, 0:HD], ps[:, 0:256].rearrange("p (h d) -> p h d", h=NR)).then_inc(scalar_done, A.step(("mvo", t)))
                act.wait_ge(scalar_done, A.now())
                activate(mo[:, t, :], ps[:, 256:512], ACT.Sigmoid).then_inc(scalar_done, A.step(("mvo", "o", t)))
                act.wait_ge(scalar_done, A.now())
                A.also(("read", ("mvo", t)))
            act.wait_ge(vector_done, V.at(A, "negabs"))
            activate(grow[0:NR, 5, :], grow[0:NR, 5, :], ACT.Exp).then_inc(scalar_done, A.step())
            act.wait_ge(scalar_done, A.now())
            activate(grow[0:NR, 5, :], grow[0:NR, 5, :], ACT.Ln, bias=ones[0:NR, 0:1]).then_inc(scalar_done, A.step("softplus"))
            act.wait_ge(scalar_done, A.now())
            act.wait_ge(vector_done, V.at(A, "conv"))
            activate(qkT, qkT, ACT.Silu).then_inc(scalar_done, A.step("conv"))
            act.wait_ge(scalar_done, A.now())
            act.wait_ge(vector_done, V.at(A, "bm"))
            activate(grow[0:NR, 5, :], grow[0:NR, 4, :], ACT.Exp, scale=-1.0).then_inc(scalar_done, A.step("erow"))
            act.wait_ge(scalar_done, A.now())
            for s, (t, i) in enumerate(ATT):
                nk = (t + 1) * P
                act.wait_ge(vector_done, V.at(A, ("att", "max", s)))
                for h in range(2):
                    o = sm[:, s % 2, h * nk:(h + 1) * nk]
                    c = t * NA + 2 * i + h
                    activate(o, o, ACT.Exp, bias=ngm[:, 2 * (s % 2) + h:2 * (s % 2) + h + 1], accum_out=rsum[:, c:c + 1]).then_inc(scalar_done, A.step(("att", "exp", s) if h else None))
                    act.wait_ge(scalar_done, A.now())
                act.wait_ge(tensor_done, T.at(A, ("att", "PT", s)))
                ps = bank(A, ("att", "PT", s))
                if s >= 2:
                    act.wait_ge(tensor_done, T.at(A, ("att", "PV", s - 2)))
                n = 2 * (t + 1) * P
                copy(pT[:, s % 2, 0:n], ps[:, 0:n]).then_inc(scalar_done, A.step(("att", "pT", s)))
                act.wait_ge(scalar_done, A.now())
                A.also(("read", ("att", "PT", s)))
            root_of("ret", hv)
            for h in range(NR):
                act.wait_ge(vector_done, V.at(A, ("ml", "arg", h)))
                activate(wT[:, h % 2, :], wT[:, h % 2, :], ACT.Exp).then_inc(scalar_done, A.step(("ml", "exp", h)))
                act.wait_ge(scalar_done, A.now())
            root_of("ml", hv)
            for g in range(KT // 2):
                act.wait_ge(tensor_done, T.at(A, ("oT", g)))
                ps = bank(A, ("oT", g))
                copy(hT[:, 2 * g:2 * g + 2, :].rearrange("p f n -> p (f n)"), ps).then_inc(scalar_done, A.step(("oTc", g)))
                act.wait_ge(scalar_done, A.now())
                A.also(("read", ("oT", g)))
            root_of("ln1", rstd[:, 0:TT])
            act.wait_ge(tensor_done, T.at(A, "router"))
            ps = bank(A, "router")
            activate(scores, ps[:, 0:TT * NE], ACT.Sigmoid).then_inc(scalar_done, A.step("router"))
            act.wait_ge(scalar_done, A.now())
            A.also(("read", "router"))
            act_experts(NE)
            act.wait_ge(scalar_done, A.now())
            root_of("ln2", rstd[:, 0:TT])
            A.end()

        def sum_squares(name, src):
            for t in range(TT):
                activate(junk, src[:, t, :], ACT.Square, accum_out=agg[:, t:t + 1]).then_inc(scalar_done, A.step((name, "ss") if t else None))
                act.wait_ge(scalar_done, A.now())
            root_of(name, rstd[:, 0:TT])

        def act_second(l):
            A.begin(1, l)
            act.wait_ge(vector_done, V.before(A))
            act.wait_ge(tensor_done, T.before(A))
            act.wait_ge(vector_done, V.at(A, "lsum"))
            activate(lsum, lsum, ACT.Exp).then_inc(scalar_done, A.step("lexp"))
            act.wait_ge(scalar_done, A.now())
            sum_squares(("pre", "mix"), x)
            act.wait_ge(tensor_done, T.at(A, "ws"))
            ps = bank(A, "ws")
            copy(wsT.rearrange("p g n -> p (g n)"), ps).then_inc(scalar_done, A.step("wsT"))
            act.wait_ge(scalar_done, A.now())
            A.also(("read", "ws"))
            act.wait_ge(tensor_done, T.at(A, "p"))
            ps = bank(A, "p")
            copy(pTT.rearrange("p k n -> p (k n)"), ps).then_inc(scalar_done, A.step("pT"))
            act.wait_ge(scalar_done, A.now())
            A.also(("read", "p"))

            def features(name, dst, blocks):
                for b in range(0, blocks, 2):
                    n = min(2, blocks - b)
                    act.wait_ge(tensor_done, T.at(A, (name, b // 2)))
                    ps = bank(A, (name, b // 2))
                    copy(dst[:, b:b + n, :].rearrange("p f n -> p (f n)"), ps[:, 0:n * SEQ]).then_inc(scalar_done, A.step((name, "c", b // 2)))
                    act.wait_ge(scalar_done, A.now())
                    A.also(("read", (name, b // 2)))

            def tokens(name, dst):
                for t in range(TT):
                    act.wait_ge(tensor_done, T.at(A, (name, t)))
                    ps = bank(A, (name, t))
                    copy(dst[:, t, :], ps).then_inc(scalar_done, A.step((name, "c", t)))
                    act.wait_ge(scalar_done, A.now())
                    A.also(("read", (name, t)))

            features("aq", qT2, 3)
            features("ak", kT2, 3)
            tokens("avcv", avcv)
            tokens("buv", buv)
            root_of("vn", rstd[:, 0:TT])
            features("cqk", cT2, 4)

            def probs_T(tag, s, n):
                act.wait_ge(tensor_done, T.at(A, (tag, "PT", s)))
                ps = bank(A, (tag, "PT", s))
                if s >= 2:
                    act.wait_ge(tensor_done, T.at(A, (tag, "PV", s - 2)))
                copy(pT2[:, s % 2, 0:n], ps[:, 0:n]).then_inc(scalar_done, A.step((tag, "pT", s)))
                act.wait_ge(scalar_done, A.now())
                A.also(("read", (tag, "PT", s)))

            def diff_exp(s):
                act.wait_ge(vector_done, V.at(A, ("diff", "max", s)))
                for c in range(2):
                    o = sm2[:, s % 2, c * SEQ:(c + 1) * SEQ]
                    k = 2 * (s % 2) + c
                    activate(o, o, ACT.Exp, bias=ngm[:, k:k + 1], scale=DQK ** -0.5, accum_out=rsum[:, k:k + 1]).then_inc(scalar_done, A.step(("diff", "exp", s) if c else None))
                    act.wait_ge(scalar_done, A.now())

            diff_exp(0)
            for s in range(len(DIFF)):
                if s + 1 < len(DIFF):
                    diff_exp(s + 1)
                probs_T("diff", s, SEQ)
            for t in range(TT):
                act.wait_ge(vector_done, V.at(A, ("diff", "var", t)))
                activate(hv[:, 0:DH], hv[:, 0:DH], ACT.Sqrt).then_inc(scalar_done, A.step(("diff", "sqrt", t)))
                act.wait_ge(scalar_done, A.now())
            for s, (t, g) in enumerate(WIN):
                act.wait_ge(vector_done, V.at(A, ("win", "max", s)))
                for h in range(2):
                    o = sm2[:, s % 2, h * SEQ:(h + 1) * SEQ]
                    k, c = 2 * (s % 2) + h, t * NA + h * WG + g
                    activate(o, o, ACT.Exp, bias=ngm[:, k:k + 1], scale=HD ** -0.5, accum_out=rsum[:, c:c + 1]).then_inc(scalar_done, A.step(("win", "exp", s) if h else None))
                    act.wait_ge(scalar_done, A.now())
                if g == WG - 1:
                    d = dsum[:, t * WH:(t + 1) * WH]
                    activate(d, d, ACT.Exp).then_inc(scalar_done, A.step(("win", "sink", t)))
                    act.wait_ge(scalar_done, A.now())
                probs_T("win", s, 2 * SEQ)
            for g in range(KT // 2):
                act.wait_ge(tensor_done, T.at(A, ("oT", g)))
                ps = bank(A, ("oT", g))
                copy(hT[:, 2 * g:2 * g + 2, :].rearrange("p f n -> p (f n)"), ps).then_inc(scalar_done, A.step(("oTc", g)))
                act.wait_ge(scalar_done, A.now())
                A.also(("read", ("oT", g)))
            for h in range(2):
                for t in range(TT):
                    act.wait_ge(tensor_done, T.at(A, ("wo", t, h)))
                    ps = bank(A, ("wo", t, h))
                    copy(y2[:, t, h * N:(h + 1) * N], ps).then_inc(scalar_done, A.step(("read", ("wo", t, h))))
                    act.wait_ge(scalar_done, A.now())
            sum_squares(("post", "mix"), y2)
            act.wait_ge(vector_done, V.at(A, ("x", "mix")))
            sum_squares(("pre", "ffn"), x)
            act_experts(NF)
            act.wait_ge(scalar_done, A.now())
            for t in range(TT):
                act.wait_ge(tensor_done, T.at(A, ("dn0", NF - 1) if t == 0 else ("dn1", NF - 1)))
                for h in range(2):
                    copy(y2[:, t, h * N:(h + 1) * N], psum[:, 4 + 2 * t + h, :]).then_inc(scalar_done, A.step(("read", ("acc", 2 * t + h))))
                    act.wait_ge(scalar_done, A.now())
            sum_squares(("post", "ffn"), y2)
            for t in range(TT):
                for h in range(2):
                    act.wait_ge(tensor_done, T.at(A, ("e", t, h)))
                    ps = bank(A, ("e", t, h))
                    copy((e2 if t == 0 else e2b)[:, h * N:(h + 1) * N], ps).then_inc(scalar_done, A.step(("read", ("e", t, h))))
                    act.wait_ge(scalar_done, A.now())
            act.wait_ge(vector_done, V.at(A, ("x", "ffn")))
            sum_squares(("pre", "ple"), x)
            for h in range(2):
                for t in range(TT):
                    act.wait_ge(tensor_done, T.at(A, ("pg", t, h)))
                    ps = bank(A, ("pg", t, h))
                    activate(y2[:, t, h * N:(h + 1) * N], ps, ACT.Sigmoid).then_inc(scalar_done, A.step(("sig", t, h)))
                    act.wait_ge(scalar_done, A.now())
                    A.also(("read", ("pg", t, h)))
            act.wait_ge(vector_done, V.at(A, "eg"))
            sum_squares(("post", "ple"), y2)
            A.end()

        @block.scalar
        def _(a):
            act.wait_ge(tensor_done, T.at(A, "c"))
            activate(cact[:, :], psum[:, 0, 0:KT], ACT.Sigmoid).then_inc(scalar_done, A.step("sigc"))
            act.wait_ge(scalar_done, A.now())
            for t in range(TT):
                for cos in (0, 1):
                    o = (cosf if cos else sinf)[:, t, HALF:HD]
                    act.wait_ge(vector_done, V.at(A, ("angle", t, cos)))
                    activate(o, o, ACT.Sin).then_inc(scalar_done, A.step("trig" if (t, cos) == (TT - 1, 1) else None))
                    act.wait_ge(scalar_done, A.now())
            with a.Fori(0, DEPTH) as l:
                act_first(l)
            with a.Fori(0, DEPTH) as l:
                act_second(l)

        def load(dst, src, s):
            nc.sync.dma_start(dst, src).then_inc(s, 16)

        def experts_load(ne, gu_src, dn_src, freed_g, freed_d):
            n = NIT[ne]
            b = S.block

            def one(e, number, wait_g, wait_d):
                if wait_g is not None:
                    sp.wait_ge(wait_g[0].sem, wait_g[0].at(S, *wait_g[1:]))
                gate_w, up_w = gu_src(number)
                g = gslot(b, f"gu{e}")
                s = g_landed[G.slot[b, f"gu{e}"]]
                load(g[:, :, 0:FE], gate_w, s)
                load(g[:, :, FE:2 * FE], up_w, s)
                if wait_d is not None:
                    sp.wait_ge(wait_d[0].sem, wait_d[0].at(S, *wait_d[1:]))
                load(dslot(b, f"dn{e}"), dn_src(number), d_landed[DN.slot[b, f"dn{e}"]])

            def used_g(e):
                if e == 0:
                    return (T, ("gu1", 0))
                i, j = divmod(e - 1, 4)
                return (T, ("gu1", "loop", j), i) if i < n else (T, ("gu1", e))

            def used_d(e):
                i, j = divmod(e, 4)
                return (T, ("dn1", "loop", j), i) if i < n else (T, ("dn1", e))

            for e in range(5):
                one(e, e, freed_g(e) if e < 4 else used_g(e - 4), freed_d(e) if e < 2 else used_d(e - 2))
            with nc.sync.Fori(0, n - 1) as i:
                for j in range(4):
                    e = 5 + j
                    one(e, i * 4 + e, (T, ("gu1", "loop", j), i),
                        (T, ("dn1", "loop", 3), i) if j == 0 else (T, ("dn1", "loop", j - 1), i + 1))
            for e in range(1 + 4 * n, ne):
                one(e, e, used_g(e - 4), used_d(e - 2))

        def used_first(name):
            if name.startswith("ada"):
                return (V, ("acc", int(name[3:])))
            if name == "mqk":
                return (T, ("mqk", 1))
            if name == "mvo":
                return (T, "gates")
            if name.startswith("wo"):
                return (T, ("wo", 1, int(name[2:])))
            return (T, (name, 1))

        def used_second(name):
            if name in ("aq", "ak", "cqk", "avcv", "buv"):
                return (T, (name, 1))
            if name.startswith("wo"):
                return (T, ("wo", 1, int(name[2:])))
            e = int(name[2:])
            n = NIT[NF]
            if e == 0:
                return (T, ("gu1", 0))
            i, j = divmod(e - 1, 4)
            return (T, ("gu1", "loop", j), i) if i < n else (T, ("gu1", e))

        def free_slot(b, name):
            c = ORDER[b].index(name)
            if c >= GS:
                sp.wait_ge((used_second if b else used_first)(ORDER[b][c - GS])[0].sem, (used_second if b else used_first)(ORDER[b][c - GS])[0].at(S, *(used_second if b else used_first)(ORDER[b][c - GS])[1:]))
                sp.sem_inc(waited)

        def sp_first(l):
            S.begin(0, l)
            sp.wait_ge(tensor_done, T.before(S))
            sp.wait_ge(vector_done, V.before(S))
            sp.wait_ge(scalar_done, A.before(S))
            load(brow[0:ADA, :], layer("b_ada", l).rearrange("(c n) -> c n", n=N), params_loaded)
            w = layer("w_ada", l)

            def load_ada(c):
                free_slot(0, f"ada{c}")
                load(gslot(0, f"ada{c}")[:, :, 0:N], by_row(w[:, c * N:(c + 1) * N]), g_landed[G.slot[0, f"ada{c}"]])

            for c in range(4):
                load_ada(c)
            load(ibias[0:NR], layer("i_bias", l).rearrange("(h a) -> h a", a=1), params_loaded)
            load(fbias[0:NR], layer("f_bias", l).rearrange("(h a) -> h a", a=1), params_loaded)
            cw = layer("conv_w", l).rearrange("j (b p) -> p b j", p=P)
            with nc.allow_non_contiguous_dma("one column of taps per channel"):
                for b in range(4):
                    load(convw[:, b, 0:CONV], cw[:, b, :], params_loaded)
                load(convw[:, :, CONV:CONV + 1], layer("conv_b", l).rearrange("(b p a) -> p b a", p=P, a=1), params_loaded)
            load(rows[:, 0, :], layer("ln_mix_g", l).partition_broadcast(P), params_loaded)
            load(rows[:, 1, :], layer("ln_mix_b", l).partition_broadcast(P), params_loaded)
            wi = layer("w_in", l)
            for name, (c0, c1) in CHUNKS1.items():
                free_slot(0, name)
                load(gslot(0, name)[:, :, 0:c1 - c0], by_row(wi[:, c0:c1]), g_landed[G.slot[0, name]])
            load_ada(4)
            load_ada(5)
            wo = layer("w_out", l)
            for h in range(2):
                free_slot(0, f"wo{h}")
                load(gslot(0, f"wo{h}")[:, :, 0:N], by_row(wo[:, h * N:(h + 1) * N]), g_landed[G.slot[0, f"wo{h}"]])
            for c in range(6, 10):
                load_ada(c)
            sp.wait_ge(vector_done, V.at(S, "ln1"))
            load(rows[:, 0, :], layer("ln_ffn_g", l).partition_broadcast(P), rows_loaded)
            load(rows[:, 1, :], layer("ln_ffn_b", l).partition_broadcast(P), rows_loaded)
            for c in range(10, ADA):
                load_ada(c)

            def expert(name, e):
                a = ins[name][bass.ds(l, 1), bass.ds(e, 1)]
                return by_row(a.rearrange("a b c d -> (a b c) d"))

            experts_load(NE, lambda e: (expert("w_gate", e), expert("w_up", e)), lambda e: expert("w_down", e),
                         lambda e: used_first(ORDER[0][ORDER[0].index(f"gu{e}") - GS]), lambda e: None)
            S.end()

        def sp_second(l):
            S.begin(1, l)
            sp.wait_ge(tensor_done, T.before(S))
            sp.wait_ge(vector_done, V.before(S))
            sp.wait_ge(scalar_done, A.before(S))
            for n, name in enumerate(("g_pre_mix_2", "g_pre_ffn_2", "g_ple_gate_2")):
                load(grows[KT * n:KT * (n + 1), :], layer(name, l).rearrange("(k p) -> k p", p=P), params_loaded)
            load(grows[3 * KT:3 * KT + GG, :], layer("b_spatial_2", l), params_loaded)
            for n, name in enumerate(("lam_q1_2", "lam_q2_2", "lam_k1_2", "lam_k2_2")):
                load(lamrow[:, n, :], layer(name, l).partition_broadcast(P), params_loaded)
            load(lamc, layer("c_lam", l).partition_broadcast(P), params_loaded)
            load(subrow, layer("g_diff_sub_2", l).partition_broadcast(P), params_loaded)
            load(wsp, layer("w_spatial_2", l).rearrange("g t s -> t g s"), params_loaded)
            load(prow, token_major(layer("p_2", l).rearrange("a b c -> (a b) c")), params_loaded)
            load(rows[:, 0, :], layer("g_post_mix_2", l).partition_broadcast(P), params_loaded)
            load(rows[:, 1, :], layer("g_post_ffn_2", l).partition_broadcast(P), params_loaded)
            load(glnrow[:, 0, :], layer("gmlp_ln_g_2", l).partition_broadcast(P), params_loaded)
            load(glnrow[:, 1, :], layer("gmlp_ln_b_2", l).partition_broadcast(P), params_loaded)
            load(sinks, layer("swa_sinks_2", l).partition_broadcast(P), params_loaded)
            wi = layer("w_in_2", l)

            def load_g(name, parts):
                free_slot(1, name)
                for a, c0, n in parts:
                    load(gslot(1, name)[:, :, a:a + n], by_row(wi[:, c0:c0 + n]), g_landed[G.slot[1, name]])

            load_g("aq", [(0, 0, 384)])
            load_g("ak", [(0, 384, 384)])
            load_g("avcv", [(0, 768, 384), (384, IN2 - P, P)])
            load_g("buv", [(0, 1152, 512)])
            free_slot(1, "cqk")
            cq = gslot(1, "cqk")
            for g in range(WG):
                for h in range(2):
                    c0 = 1664 + (h * WG + g) * HD
                    load(cq[:, :, (2 * g + h) * HD:(2 * g + h + 1) * HD], by_row(wi[:, c0:c0 + HD]), g_landed[G.slot[1, "cqk"]])
            load(cq[:, :, 384:512], by_row(wi[:, 2048:2176]), g_landed[G.slot[1, "cqk"]])
            wo = layer("w_out_2", l)
            for h in range(2):
                free_slot(1, f"wo{h}")
                load(gslot(1, f"wo{h}")[:, :, 0:N], by_row(wo[:, h * N:(h + 1) * N]), g_landed[G.slot[1, f"wo{h}"]])
            wf, wd = layer("w_ffn_in_2", l), layer("w_ffn_out_2", l)

            def ffn(e):
                if isinstance(e, int):
                    return by_row(wf[:, e * FE:(e + 1) * FE]), by_row(wf[:, DFF + e * FE:DFF + (e + 1) * FE])
                return by_row(wf[:, bass.ds(e * FE, FE)]), by_row(wf[:, bass.ds(e * FE + DFF, FE)])

            def ffn_out(e):
                return by_row(wd[e * FE:(e + 1) * FE, :] if isinstance(e, int) else wd[bass.ds(e * FE, FE), :])

            experts_load(NF, ffn, ffn_out, lambda e: used_second(ORDER[1][ORDER[1].index(f"gu{e}") - GS]), lambda e: None)
            sp.wait_ge(tensor_done, T.at(S, ("dn1", NF - 2)))
            load(dslot(1, "up"), by_row(layer("w_ple_up_2", l)), d_landed[DN.slot[1, "up"]])
            wg = layer("w_ple_gate_2", l)
            for h in range(2):
                free_slot(1, f"pg{h}")
                load(gslot(1, f"pg{h}")[:, :, 0:N], by_row(wg[:, h * N:(h + 1) * N]), g_landed[G.slot[1, f"pg{h}"]])
            sp.wait_ge(vector_done, V.at(S, ("x", "mix")))
            load(rows[:, 0, :], layer("g_ple_post_2", l).partition_broadcast(P), rows_loaded)
            S.end()

        @block.sync
        def _(sp):
            load(c8, ins["c"].rearrange("a (k p) -> (a k) p", p=P), start_loaded)
            load(cshared[:, :], ins["c_shared"], start_loaded)
            with nc.allow_non_contiguous_dma("one position per partition"):
                load(posi[:, :], ins["positions"].rearrange("a (t p) -> p (a t)", p=P), start_loaded)
            load(x[:, :, :], token_major(ins["x"].rearrange("a b c -> (a b) c")), start_loaded)
            load(cblock[:, :], ins["c_first"], start_loaded)
            load(crows[:, :, :], ins["c_rows"], start_loaded)
            load(wr[:, :, :], by_row(ins["w_router"]), start_loaded)
            load(br[:, :], ins["b_router"].partition_broadcast(P), start_loaded)
            with sp.Fori(0, DEPTH) as l:
                sp_first(l)
            sp.wait_ge(vector_done, V.base(1))
            load(cblock[:, 0:C2_W], ins["c_second"], const_loaded)
            with sp.Fori(0, DEPTH) as l:
                sp_second(l)
            sp.wait_ge(vector_done, V.total())
            sp.dma_start(token_major(out), x[:, :, :]).then_inc(stored, 16)
            sp.wait_ge(stored, 16)

    return {"T": T.counted(), "V": V.counted(), "A": A.counted()}


_INS = ["x", "c", "positions", "w_ada", "b_ada", "w_in", "i_bias", "f_bias", "conv_w", "conv_b", "w_out", "ln_mix_g",
        "ln_mix_b", "w_router", "b_router", "w_gate", "w_up", "w_down", "ln_ffn_g", "ln_ffn_b", "p_2", "g_pre_mix_2",
        "w_in_2", "lam_q1_2", "lam_k1_2", "lam_q2_2", "lam_k2_2", "g_diff_sub_2", "gmlp_ln_g_2", "gmlp_ln_b_2",
        "w_spatial_2", "b_spatial_2", "swa_sinks_2", "w_out_2", "g_post_mix_2", "g_pre_ffn_2", "w_ffn_in_2",
        "w_ffn_out_2", "g_post_ffn_2", "w_ple_up_2", "w_ple_gate_2", "g_ple_gate_2", "g_ple_post_2"]


def kernel(**inputs):
    import concourse.bacc as _bacc
    from concourse.bass_utils import run_bass_kernel_spmd as _run

    arrays = {f"in_{n}": np.ascontiguousarray(inputs[n]) for n in _INS}
    arrays |= {f"in_{n}": a for n, a in constants().items()}

    def build(known):
        nc = _bacc.Bacc("TRN2", target_bir_lowering=False, num_devices=1)
        ins = {n[3:]: nc.dram_tensor(n, a.shape, mybir.dt.from_np(a.dtype), kind="ExternalInput").ap()
               for n, a in arrays.items()}
        out = nc.dram_tensor("out_x", (SEQ, D), F32, kind="ExternalOutput").ap()
        return nc, program(nc, ins, out, known)

    _, known = build(None)
    nc, _ = build(known)
    r = _run(nc, [arrays], core_ids=[0])
    return r.results[0]["out_x"].reshape(1, SEQ, D)
```

```python
from contextlib import ExitStack

import concourse.bass as bass
from concourse import mybir
import numpy as np

F32 = mybir.dt.float32
F32R = mybir.dt.float32r
I32 = mybir.dt.int32
ALU = mybir.AluOpType
ACT = mybir.ActivationFunctionType
AX = mybir.AxisListType

P = 128
D = 1024
SEQ = 256
TT = SEQ // P
KT = D // P
DEPTH = 2
HD = 64
HALF = HD // 2
N = 512
BIG = 1.0e30
TAKEN = -3.0e38
TOPK = min(256, SEQ // 4)
LN_EPS = 1e-5
RMS_EPS = 1e-6
ALPHA = (2.0 * DEPTH) ** 0.25
TWO_PI = 2.0 * np.pi
ROUND = 12582912.0

AQ, AK, AV, IQ, IK, IW, RQ, RK, RV, RG, MQ, MK, MV, MO, MI, MF = (
    0, 512, 1024, 1536, 1792, 1856, 1860, 2116, 2372, 2628, 2884, 3140, 3396, 3652, 3908, 3912)
IN1 = 3916
CHUNKS1 = {"idx": (IQ, RQ), "aq": (AQ, AK), "ak": (AK, AV), "av": (AV, IQ), "rqk": (RQ, RV),
           "rvg": (RV, MQ), "mvo": (MV, IN1), "mqk": (MQ, MV)}
NA = 8
NI = 4
NR = 4
NE = 16
NG = 4
EG = NE // NG
FE = 256
ADA = 6 * D // N
CONV = 4
DH = 6
DQK = 32
GG = 4
GW = 256
WH = 6
WG = 3
DFF = 2816
NF = DFF // FE
PLE = 256
IN2 = 2304
SLOPES = [2.0 ** (-8.0 * k / (DH + WH)) for k in range(1, DH + WH + 1)]
DIFF_SLOPES, SWA_SLOPES = SLOPES[WH:], SLOPES[:WH]

GS = 4
GW_MAX = 520
ARENA = 15400
SMALL = 640
DS = 2
ORDER = (
    [f"ada{c}" for c in range(4)] + list(CHUNKS1) + [f"ada{c}" for c in range(4, 10)] + ["wo0", "wo1"]
    + [f"ada{c}" for c in range(10, ADA)] + [f"gu{e}" for e in range(NE)],
    ["aq", "ak", "avcv", "buv", "cqk", "wo0", "wo1"] + [f"gu{e}" for e in range(NF)] + ["pg0", "pg1"],
)
ORDER_D = ([f"dn{e}" for e in range(NE)], [f"dn{e}" for e in range(NF)] + ["up"])
DMAS = ({f"ada{c}": 1 for c in range(ADA)} | {f"gu{e}": 2 for e in range(NE)},
        {f"gu{e}": 2 for e in range(NF)} | {"avcv": 2, "cqk": 7})
ROWS = (2, 1)
GAINS = (2, 2)
PARAMS = (7, 15)
ADA_PAIRS = (2, 0, 4, 6, 8, 10)
AHEAD = 32

CONST = {}
_at = 0
for _name, _w in (("ident", P), ("invf", HALF), ("first4", NG), ("first16", NE), ("shared", 0)):
    CONST[_name] = _at
    _at += _w
C_SHARED = _at
C1 = {"decay": 0, "causal": NR * 384, "vis": NR * 384 + 256}
C1_W = NR * 384 + 256 + TT * SEQ
C2 = {"dist": 0, "wdist": TT * SEQ}
C2_W = 2 * TT * SEQ


def constants():
    p = np.arange(P)[:, None]
    j = np.arange(SEQ)[None, :]
    shared = np.zeros((P, C_SHARED), np.float32)
    shared[:, CONST["ident"]:CONST["ident"] + P] = np.eye(P)
    shared[:, CONST["invf"]:CONST["invf"] + HALF] = np.float32(10000.0) ** (
        -np.arange(HALF, dtype=np.float32) / np.float32(HALF))
    shared[:, CONST["first4"]:CONST["first4"] + NG] = np.arange(NG, 0, -1)
    shared[:, CONST["first16"]:CONST["first16"] + NE] = np.arange(NE, 0, -1)
    c1 = np.zeros((P, C1_W), np.float32)
    for h in range(NR):
        log_gamma = np.log1p(-(2.0 ** (-5.0 - h)))
        decay = np.where(j >= p, np.exp(np.maximum(j - p, 0) * log_gamma), 0.0) * HD ** -0.5
        c1[:, h * 384:h * 384 + 256] = decay
        c1[:, h * 384 + 256:h * 384 + 384] = decay[:, :P]
    c1[:, C1["causal"]:C1["causal"] + SEQ] = np.where(j >= p, 0.0, -BIG)
    c2 = np.zeros((P, C2_W), np.float32)
    for t in range(TT):
        q = t * P + p
        c1[:, C1["vis"] + t * SEQ:C1["vis"] + (t + 1) * SEQ] = np.where(j < (q // 64 + 1) * 64, 0.0, -BIG)
        dist = np.abs(q - j)
        c2[:, t * SEQ:(t + 1) * SEQ] = dist
        c2[:, C2["wdist"] + t * SEQ:C2["wdist"] + (t + 1) * SEQ] = np.where(dist <= 128, dist, BIG)
    rows = np.zeros((NR, NR, P), np.float32)
    for h in range(NR):
        rows[h, h, :] = -1.0
    lam = np.array([[0.8 - 0.6 * np.exp(-0.3 * l), 0.2 + 0.6 * np.exp(-0.3 * l)] for l in range(DEPTH)], np.float32)
    return {"c_shared": shared, "c_first": c1, "c_second": c2, "c_rows": rows, "c_lam": lam}


class Done:

    def __init__(self, sem, known):
        self.sem, self.known = sem, known
        self.block, self.l, self.n = None, None, 0
        self.marks, self.per, self.stride, self.first = {}, [0, 0], {}, 0
        self.inner, self.inner_n, self.inner_from = None, 0, 0

    def begin(self, block, l):
        if block == 0:
            self.first = self.n
        self.block, self.l, self.n = block, l, 0

    def end(self):
        self.per[self.block] = self.n

    def loop(self, name, n):
        self.inner, self.inner_n, self.inner_from = name, n, self.n

    def loop_end(self):
        step = self.n - self.inner_from
        self.stride[self.inner] = step
        self.n = self.inner_from + step * self.inner_n
        self.inner = None

    def step(self, name=None, by=1):
        self.n += by
        if name is not None:
            self.also(name)
        return by

    def also(self, name):
        assert (self.block, name) not in self.marks, name
        self.marks[self.block, name] = (self.n, self.inner)

    def base(self, block):
        k = self.known
        return k["first"] + (DEPTH * k["per"][0] if block else 0) if k else 1

    def before(self, by):
        return by.l * self.known["per"][by.block] + self.base(by.block) if self.known else 1

    def last_pass(self, by, name, i=None):
        if not self.known:
            return 1
        n, inner = self.known["marks"][0, name]
        n += i * self.known["stride"][inner] if inner else 0
        return by.l * self.known["per"][by.block] + (self.base(by.block) + n - self.known["per"][0])

    def now(self):
        if self.block is None:
            return self.n
        return self.l * self.known["per"][self.block] + (self.base(self.block) + self.n) if self.known else 1

    def total(self):
        return self.base(1) + DEPTH * self.known["per"][1] if self.known else 1

    def at(self, by, name, i=None):
        if not self.known:
            return 1
        n, inner = self.known["marks"][by.block, name]
        if by.block is None:
            return n
        v = by.l * self.known["per"][by.block] + (self.base(by.block) + n)
        return v if inner is None else v + i * self.known["stride"][inner]

    def counted(self):
        return {"marks": self.marks, "per": self.per, "stride": self.stride, "first": self.first}


class Ring:

    def __init__(self, sems, slots, orders, dmas):
        self.sems, self.slot, self.count, self.per = sems, {}, {}, []
        for b, order in enumerate(orders):
            total = [0] * slots
            for c, name in enumerate(order):
                s = c % slots
                total[s] += 16 * dmas[b].get(name, 1)
                self.slot[b, name], self.count[b, name] = s, total[s]
            self.per.append(total)

    def sem(self, by, name):
        return self.sems[self.slot[by.block, name]]

    def level(self, by, name, more=0):
        b, s = by.block, self.slot[by.block, name]
        first = DEPTH * self.per[0][s] if b else 0
        return by.l * self.per[b][s] + (first + self.count[b, name]) + more


def program(nc, ins, out, known):
    ctx = ExitStack()
    with ctx:
        def sb(name, shape, dt=F32):
            return ctx.enter_context(nc.sbuf_tensor(name, shape, dt))

        def sb_parts(name, shape):
            with nc.sbuf_tensor(name, shape, F32) as whole:
                pass
            return whole, ctx.enter_context(nc.sbuf_tensor(f"{name}_parts", shape, F32R))

        def sem(name):
            return ctx.enter_context(nc.semaphore(name))

        pe, dve, act, sp = nc.tensor, nc.vector, nc.scalar, nc.sync

        gring, gring_rest = sb_parts("gring", [P, GS, KT, GW_MAX])
        dring, dring_rest = sb_parts("dring", [P, DS, FE // P, D])
        x = sb("x", [P, TT, D])
        hT, hT_parts = sb_parts("hT", [P, KT, SEQ])
        o_cat, o_cat_parts = sb_parts("o_cat", [P, TT, D])
        cshared = sb("cshared", [P, C_SHARED])
        cblock = sb("cblock", [P, C1_W])
        crows = sb("crows", [NR, NR, P])
        rows = sb("rows", [P, 2, D])
        gb = sb("gb", [P, D])
        ones = sb("ones", [P, SEQ])
        zeros = sb("zeros", [P, P])
        cosf = sb("cosf", [P, TT, HD])
        sinf = sb("sinf", [P, TT, HD])
        cact = sb("cact", [P, KT])
        wr = sb("wr", [P, KT, NE])
        br = sb("br", [P, NE])
        ex, ex_parts = sb_parts("ex", [P, 3, TT * FE])
        sact = ex[:, 0, :].rearrange("p (t f) -> p t f", t=TT)
        hid = ex[:, 1, :].rearrange("p (t f) -> p t f", t=TT)
        hidT = ex_parts[:, 2, :].rearrange("p (t f n) -> p t f n", t=TT, f=FE // P)
        small = sb("small", [P, SMALL])
        tmp = sb("tmp", [P, 2, N])
        arena, arena_parts = sb_parts("arena", [P, ARENA])
        ident = cshared[:, 0:P]

        used = [0]

        def restart():
            used[0] = 0

        def buf(*shape, of=arena):
            size = int(np.prod(shape))
            a = of[:, used[0]:used[0] + size]
            used[0] += size
            assert used[0] <= ARENA, used[0]
            if len(shape) == 2:
                a = a.rearrange("p (a b) -> p a b", a=shape[0])
            elif len(shape) == 3:
                a = a.rearrange("p (a b c) -> p a b c", a=shape[0], b=shape[1])
            return a

        s_used = [0]

        def sc(n):
            a = small[:, s_used[0]:s_used[0] + n]
            s_used[0] += n
            assert s_used[0] <= SMALL
            return a

        psum = ctx.enter_context(nc.psum_tensor("psum", [P, 8, N], F32))

        tensor_done, vector_done, scalar_done = sem("tensor_done"), sem("vector_done"), sem("scalar_done")
        g_landed = [sem(f"g_landed{i}") for i in range(GS)]
        d_landed = [sem(f"d_landed{i}") for i in range(DS)]
        start_loaded, x_loaded, tables_loaded = sem("start_loaded"), sem("x_loaded"), sem("tables_loaded")
        bias_loaded, params_loaded = sem("bias_loaded"), sem("params_loaded")
        gains_loaded, rows_loaded = sem("gains_loaded"), sem("rows_loaded")
        const_loaded, stored, waited = sem("const_loaded"), sem("stored"), sem("waited")

        known = known or {}
        T = Done(tensor_done, known.get("T"))
        V = Done(vector_done, known.get("V"))
        A = Done(scalar_done, known.get("A"))
        S = Done(None, known.get("S"))
        G = Ring(g_landed, GS, ORDER, DMAS)
        DN = Ring(d_landed, DS, ORDER_D, ({}, {}))

        def gslot(block, name):
            return gring[:, G.slot[block, name]]

        def dslot(block, name):
            return dring[:, DN.slot[block, name]]

        def g_rest(block, name):
            return gring_rest[:, G.slot[block, name]]

        def d_rest(block, name):
            return dring_rest[:, DN.slot[block, name]]

        def params_count(by):
            b = by.block
            return by.l * (16 * PARAMS[b]) + (16 * PARAMS[b] + (DEPTH * 16 * PARAMS[0] if b else 0))

        def bias_count(by):
            return by.l * 16 + 16

        def gains_count(by):
            b = by.block
            return by.l * (16 * GAINS[b]) + (16 * GAINS[b] + (DEPTH * 16 * GAINS[0] if b else 0))

        def rows_count(by):
            b = by.block
            return by.l * (16 * ROWS[b]) + (16 * ROWS[b] + (DEPTH * 16 * ROWS[0] if b else 0))

        bank_of, on_bank = {}, {}
        turn = [0]

        def take(name, reader, bank=None, pair=False):
            if bank is None:
                bank = turn[0] + (turn[0] % 2 if pair else 0)
                bank %= 6
                turn[0] = (bank + (2 if pair else 1)) % 6
            banks = (bank, bank + 1) if pair else (bank,)
            for last in dict.fromkeys(on_bank[b] for b in banks if b in on_bank):
                pe.wait_ge(last[0].sem, last[0].at(T, *last[1:]))
                if pair:
                    pe.sem_inc(waited)
            for b in banks:
                on_bank[b] = (reader, ("read", name))
            bank_of[T.block, name] = (bank, pair)
            return psum[:, bank:bank + 2, :] if pair else psum[:, bank, :]

        def bank(E, name):
            b, pair = bank_of[E.block, name]
            return psum[:, b:b + 2, :] if pair else psum[:, b, :]

        roped = buf(3, N)
        idxT, aqT, akT, rrT = buf(3, SEQ), buf(4, SEQ), buf(4, SEQ), buf(4, SEQ)
        av, rvg = buf(TT, N), buf(TT, N)
        rv, rg = rvg[:, :, 0:256], rvg[:, :, 256:512]
        qkT, mo = buf(4, SEQ), buf(TT, 256)
        rel, bias = buf(NI, SEQ), buf(TT, SEQ)
        score = buf(SEQ)
        sm, pT = buf(2, N), buf(2, N)
        tail = used[0]
        cin, mv = buf(4, SEQ + CONV - 1), buf(TT, NR, HD + 1)
        brow = buf(N)
        arow = [buf(N)[0:1, :], sb("arow_odd", [1, N])[:, :]]
        convw = buf(4, CONV + 1)
        sT = roped.rearrange("p a n -> p (a n)")[:, 0:768].rearrange("p (a n) -> p a n", a=2)
        wT = roped.rearrange("p a n -> p (a n)")[:, 768:1536].rearrange("p (a n) -> p a n", a=2)
        hn = rel.rearrange("p a n -> p (a n)")[:, 0:N].rearrange("p (h d) -> p h d", h=8)
        sq = rel.rearrange("p a n -> p (a n)")[:, N:2 * N].rearrange("p (h d) -> p h d", h=8)
        grow = ex.rearrange("p a n -> p (a n)").rearrange("p (r n) -> p r n", r=6)
        restart()
        qT2, kT2, at2 = buf(3, SEQ), buf(3, SEQ), buf(2, SEQ)
        cT2 = buf(4, SEQ)
        avcv, buv, vn, wsT = buf(TT, N), buf(TT, N), buf(TT, GW), buf(GG, P)
        wsp = buf(GG, P)
        pT2 = buf(2, N)
        hn2, sq2 = buf(DH, HD), buf(DH, HD)
        sm2 = buf(2, N)
        prow = buf(TT, PLE)
        grows, glnrow, subrow = buf(P), buf(2, GW), buf(HD)
        lamrow = buf(4, DQK)
        e2, e2b = gb[:, :], buf(D)
        junk = sm2.rearrange("p a n -> p (a n)")
        restart()
        w_hi = [buf(KT, N, of=arena_parts) for _ in range(2)]
        d_hi = [buf(FE // P, D, of=arena_parts) for _ in range(2)]
        hidT_lo = buf(TT, FE // P, P, of=arena_parts)
        assert used[0] <= tail, (used[0], tail)
        used[0] = tail
        y2, pTT = buf(TT, D), buf(PLE // P, SEQ)
        used[0] = tail
        h_hi = (o_cat_parts[:, :, :].rearrange("p t n -> p (t n)").rearrange("p (k n) -> p k n", k=KT),
                buf(KT, SEQ, of=arena_parts))
        h_lo = hT_parts

        mod = [sc(KT) for _ in range(4)]
        iw, ngm, rsum = sc(TT * NI), sc(2 * 2), sc(TT * NA)
        rinv, top8 = sc(TT * NA), sc(8)
        st, agg, rstd = sc(12), sc(2 * TT), sc(2 * TT)
        hs, hv = sc(8), sc(8)
        gcol, den = sc(16), sc(NR)
        ibias, fbias = sc(1), sc(1)
        scores, biased, bmask, onehot, sel, gate = (sc(TT * NE) for _ in range(6))
        pairs, gsum, key4, t2 = sc(8 * 6), sc(8), sc(8), sc(TT)
        posf = sc(TT)
        gcols = sc(3 * KT + GG)
        lamc, lam, lsum = sc(2), sc(1), sc(2)
        r2, nm2, sinks, msink, dsum = sc(2), sc(2), sc(WH), sc(2), sc(TT * WH)
        lprod = sc(2 * DQK)
        c8 = ex[0:KT, 0, 0:P]
        posi = sb("posi", [P, TT], I32)

        block = ctx.enter_context(nc.Block())

        def token_major(ap):
            return ap.rearrange("(t p) n -> p t n", p=P)

        def by_row(ap):
            return ap.rearrange("(k p) n -> p k n", p=P)

        def layer(name, l):
            a = ins[name][bass.ds(l, 1)]
            return a.rearrange("a b c d -> (a b) c d") if len(a.shape) == 4 else a.rearrange(
                "a b c -> (a b) c") if len(a.shape) == 3 else a.rearrange("a b -> (a b)")

        NIT = {NE: (NE - 2) // 4, NF: (NF - 2) // 4}

        def transposed_x(tag, src, reader):
            for g in range(KT // 2):
                ps = take((tag, g), reader)
                for f in (2 * g, 2 * g + 1):
                    for t in range(TT):
                        last = nc.tensor.transpose(ps[:, (f % 2) * SEQ + t * P:(f % 2) * SEQ + (t + 1) * P],
                                                   src[:, t, f * P:(f + 1) * P], ident)
                last.then_inc(tensor_done, T.step((tag, g)))

        def token_product(ps, t, w, n):
            for k in range(KT):
                last = nc.tensor.matmul(ps[:, 0:n], hT[:, k, t * P:(t + 1) * P], w[:, k, 0:n],
                                        start=k == 0, stop=k == KT - 1)
            return last

        def split_product(ps, hi, lo, w, w_rest, start, stop):
            nc.tensor.matmul(ps, hi, w, start=start, stop=False)
            nc.tensor.matmul(ps, hi, w_rest, start=False, stop=False)
            return nc.tensor.matmul(ps, lo, w, start=False, stop=stop)

        def feature_product(ps, w, c0, m, at):
            for k in range(KT):
                last = nc.tensor.matmul(ps[0:m, at:at + SEQ], w[:, k, c0:c0 + m], hT[:, k, :],
                                        start=k == 0, stop=k == KT - 1)
            return last

        def pe_experts(ne, start, block_no, routed=None):
            n = NIT[ne]

            def gu(e, t, i, name, before):
                if before is not None:
                    pe.wait_ge(vector_done, V.at(T, *before))
                w, w_rest = w_hi[e % 2], g_rest(block_no, f"gu{e}")
                for k in range(KT):
                    last = split_product(psum[:, t, :], h_hi[block_no][:, k, t * P:(t + 1) * P], h_lo[:, k, t * P:(t + 1) * P],
                                         w[:, k, :], w_rest[:, k, 0:N], k == 0, k == KT - 1)
                last.then_inc(tensor_done, T.step(name))

            def tr(t, i, name, hid_name):
                pe.wait_ge(vector_done, V.at(T, hid_name, i))
                for f in range(FE // P):
                    last = nc.tensor.transpose(psum[:, 2 + t, f * P:(f + 1) * P], hid[:, t, f * P:(f + 1) * P], ident)
                last.then_inc(tensor_done, T.step(name))

            def dn(e, t, i, name, copied, first=False, final=False):
                pe.wait_ge(vector_done, V.at(T, *copied))
                w, w_rest = d_hi[e % 2], d_rest(block_no, f"dn{e}")
                for f in range(FE // P):
                    for h in range(2):
                        last = split_product(psum[:, 4 + 2 * t + h, :], hidT[:, t, f, :], hidT_lo[:, t, f, :],
                                             w[:, f, h * N:(h + 1) * N], w_rest[:, f, h * N:(h + 1) * N],
                                             first and f == 0, final and f == FE // P - 1)
                last.then_inc(tensor_done, T.step(name))

            for b in range(8):
                if b in on_bank:
                    pe.wait_ge(on_bank[b][0].sem, on_bank[b][0].at(T, *on_bank[b][1:]))
                    pe.sem_inc(waited)
                    del on_bank[b]
            pe.wait_ge(start[0].sem, start[0].at(T, *start[1:]))
            for h in range(2):
                nc.tensor.matmul(psum[:, 6 + h, :], zeros[0:1, :], crows[0:1, :, :].rearrange("r h p -> r (h p)"), start=True, stop=False)
            gu(0, 0, None, ("gu0", 0), (("parts", 0), None))
            if routed is not None:
                routed()
            gu(0, 1, None, ("gu1", 0), None)
            tr(0, None, ("tr", 0, 0), ("hid", 0, 0))
            gu(1, 0, None, ("gu0", 1), (("parts", 1), None))
            tr(1, None, ("tr", 0, 1), ("hid", 0, 1))
            dn(0, 0, None, ("dn0", 0), (("hidT", 0, 0), None), first=True)
            with nc.tensor.Fori(0, n) as i:
                T.loop(f"pe{block_no}", n)
                for j in range(4):
                    e = 1 + j
                    before = (("hid", "loop", j - 1, 1), i) if j else (("hid", "loop", 3, 1), i - 1)
                    gu(e, 1, i, ("gu1", "loop", j), before)
                    tr(0, i, ("tr", "loop", j, 0), ("hid", "loop", j, 0))
                    copied = (("hidT", "loop", j - 1, 1), i) if j else (("hidT", "loop", 3, 1), i - 1)
                    dn(e - 1, 1, i, ("dn1", "loop", j), copied)
                    gu(e + 1, 0, i, ("gu0", "loop", j), (("parts", "loop", j), i))
                    tr(1, i, ("tr", "loop", j, 1), ("hid", "loop", j, 1))
                    dn(e, 0, i, ("dn0", "loop", j), (("hidT", "loop", j, 0), i))
                T.loop_end()
            for e in range(1 + 4 * n, ne):
                prev = ("loop", 3) if e == 1 + 4 * n else (e - 1,)
                it = n - 1 if e == 1 + 4 * n else None
                gu(e, 1, None, ("gu1", e), (("hid", *prev, 1), it))
                tr(0, None, ("tr", e, 0), ("hid", e, 0))
                dn(e - 1, 1, None, ("dn1", e - 1), (("hidT", *prev, 1), it))
                if e + 1 < ne:
                    gu(e + 1, 0, None, ("gu0", e + 1), (("parts", e + 1), None))
                tr(1, None, ("tr", e, 1), ("hid", e, 1))
                dn(e, 0, None, ("dn0", e), (("hidT", e, 0), None), final=e == ne - 1)
            dn(ne - 1, 1, None, ("dn1", ne - 1), (("hidT", ne - 1, 1), None), final=True)

        def pe_attention(tag, steps, ahead, scores_of, widths, values_of, probs_src, probs_T, outs, between):
            n = len(steps)

            def score_step(s):
                ps = take((tag, "S", s), V, pair=True)
                scores_of(ps, s).then_inc(tensor_done, T.step((tag, "S", s)))

            for s in range(ahead):
                score_step(s)
            for s in range(n):
                between(s)
                pe.wait_ge(probs_src(s)[0].sem, probs_src(s)[0].at(T, *probs_src(s)[1:]))
                ps = take((tag, "PT", s), A)
                src, blocks = widths(s)
                for b in range(blocks):
                    last = nc.tensor.transpose(ps[:, b * P:(b + 1) * P], src[:, b * P:(b + 1) * P], ident)
                last.then_inc(tensor_done, T.step((tag, "PT", s)))
                if s + ahead < n:
                    score_step(s + ahead)
                if s in outs:
                    name, reader, b = outs[s]
                    take(name, reader, b)
                pe.wait_ge(scalar_done, A.at(T, (tag, "pT", s)))
                values_of(s).then_inc(tensor_done, T.step((tag, "PV", s)))

        ATT = [(t, i) for t in range(TT) for i in range(NA // 2)]

        def pe_first(l):
            T.begin(0, l)
            on_bank.clear()
            turn[0] = 0

            def ada_row(c, bank_no=None):
                ps = take(("ada", c), A, bank_no)
                pe.wait_ge(G.sem(T, f"ada{c}"), G.level(T, f"ada{c}"))
                if c == ADA_PAIRS[0]:
                    pe.wait_ge(bias_loaded, bias_count(T))
                for k in range(KT):
                    nc.tensor.matmul(ps[0:1, :], cact[:, k:k + 1], gslot(0, f"ada{c}")[:, k, 0:N], start=k == 0, stop=False)
                nc.tensor.matmul(ps[0:1, :], ident[0:ADA, c:c + 1], brow[0:ADA, :], start=False, stop=True).then_inc(tensor_done, T.step(("ada", c)))

            def ada_columns(c, bank_no=None):
                ps = take(("columns", c), V, bank_no)
                pe.wait_ge(scalar_done, A.at(T, ("arow", c + 1)))
                pe.sem_inc(waited)
                for n in range(2):
                    for j in range(N // P):
                        last = nc.tensor.matmul(ps[:, 4 * n + j:4 * n + j + 1], arow[n][:, j * P:(j + 1) * P], ones[0:1, 0:1],
                                                start=True, stop=True)
                last.then_inc(tensor_done, T.step(("arows_used", c)))

            def ada_gates(c):
                for n in range(2):
                    ps = take(("gate", c + n), V)
                    pe.wait_ge(scalar_done, A.at(T, ("arow", c + n)))
                    pe.sem_inc(waited)
                    nc.tensor.matmul(ps, ones[0:1, 0:P], arow[n], start=True, stop=True).then_inc(tensor_done, T.step(("gate", c + n)))
                T.also(("arows_used", c))

            ada_row(2, 0)
            ada_row(3, 1)
            ada_row(0, 0)
            ada_columns(2, 2)
            ada_row(1, 1)
            ada_columns(0, 3)
            pe.wait_ge(vector_done, V.before(T))
            pe.wait_ge(scalar_done, A.before(T))
            pe.wait_ge(x_loaded, 16)
            transposed_x("xT", x, V)
            pe.wait_ge(vector_done, V.at(T, ("hT", KT // 2 - 1)))

            def in_proj(name, t):
                if t == 0:
                    pe.wait_ge(G.sem(T, name), G.level(T, name))
                c0, c1 = CHUNKS1[name]
                ps = take((name, t), V if name in ("idx", "aq", "ak", "rqk") else A)
                token_product(ps, t, gslot(0, name), min(N, c1 - c0)).then_inc(tensor_done, T.step((name, t)))

            rope_slot = {n: i for i, n in enumerate([(c, t) for c in ("idx", "aq", "ak", "rqk") for t in range(TT)])}

            def transposed_rope(name, t, blocks):
                pe.wait_ge(vector_done, V.at(T, ("rope", name, t)))
                ps = take((name, "T", t), A)
                src = roped[:, rope_slot[name, t] % 3, :]
                for b in range(blocks):
                    last = nc.tensor.transpose(ps[:, b * P:(b + 1) * P], src[:, b * P:(b + 1) * P], ident)
                last.then_inc(tensor_done, T.step((name, "T", t)))

            def index_scores(t):
                nk = (t + 1) * P
                ps = take(("idxS", t), A, pair=True)
                if t == 0:
                    pe.sem_inc(waited)
                    pe.wait_ge(scalar_done, A.at(T, ("idx", "Tc", 1)))
                for p in range(2):
                    for h in (0, 1):
                        last = nc.tensor.matmul(ps[:, h, p * SEQ:p * SEQ + nk],
                                                idxT[h * HD:(h + 1) * HD, p, t * P:(t + 1) * P],
                                                idxT[h * HD:(h + 1) * HD, 2, 0:nk], start=True, stop=True)
                last.then_inc(tensor_done, T.step(("idxS", t)))

            def mqk(b):
                if b == 0:
                    pe.wait_ge(G.sem(T, "mqk"), G.level(T, "mqk"))
                ps = take(("mqk", b), A)
                for f in range(2):
                    last = feature_product(ps, gslot(0, "mqk"), (2 * b + f) * P, P, f * SEQ)
                last.then_inc(tensor_done, T.step(("mqk", b)))

            def gates():
                ps = take("gates", V)
                for f in range(2):
                    last = feature_product(ps, gslot(0, "mvo"), N + NR * f, NR, f * SEQ)
                last.then_inc(tensor_done, T.step("gates"))

            in_proj("idx", 0)
            in_proj("idx", 1)
            in_proj("aq", 0)
            transposed_rope("idx", 0, 3)
            transposed_rope("idx", 1, 3)
            in_proj("aq", 1)
            index_scores(0)
            index_scores(1)
            in_proj("ak", 0)
            transposed_rope("aq", 0, 4)
            transposed_rope("aq", 1, 4)
            in_proj("ak", 1)
            in_proj("av", 0)
            in_proj("av", 1)
            transposed_rope("ak", 0, 4)
            transposed_rope("ak", 1, 4)
            in_proj("rqk", 0)

            def att_scores(ps, s):
                t, i = ATT[s]
                nk = (t + 1) * P
                if s == 0:
                    pe.wait_ge(scalar_done, A.at(T, ("aq", "Tc", 1)))
                    pe.wait_ge(scalar_done, A.at(T, ("ak", "Tc", 1)))
                for h in (0, 1):
                    last = nc.tensor.matmul(ps[:, h, 0:nk], aqT[h * HD:(h + 1) * HD, i, t * P:(t + 1) * P],
                                            akT[h * HD:(h + 1) * HD, i, 0:nk], start=True, stop=True)
                return last

            def att_values(s):
                t, i = ATT[s]
                if s == 0:
                    pe.wait_ge(scalar_done, A.at(T, ("av", 1)))
                for h in (0, 1):
                    c = (2 * i + h) * HD
                    for k in range(t + 1):
                        last = nc.tensor.matmul(psum[:, 6 + t, c:c + HD], pT[:, s % 2, (h * (t + 1) + k) * P:(h * (t + 1) + k + 1) * P],
                                                av[:, k, c:c + HD], start=k == 0, stop=k == t)
                return last

            def transposed_scores(ps, qk, h):
                r, b = (h % 2) * HD, h // 2
                nc.tensor.matmul(ps[:, 0:SEQ], qk[r:r + HD, 2 + b, 0:P], qk[r:r + HD, b, :], start=True, stop=True)
                return nc.tensor.matmul(ps[:, SEQ:SEQ + P], qk[r:r + HD, 2 + b, P:SEQ], qk[r:r + HD, b, P:SEQ],
                                        start=True, stop=True)

            def ret_scores(h):
                ps = take(("ret", "S", h), V)
                if h == 0:
                    pe.wait_ge(scalar_done, A.at(T, ("rqk", "Tc", 1)))
                transposed_scores(ps, rrT, h).then_inc(tensor_done, T.step(("ret", "S", h)))

            def ret_values(h):
                if h == 0:
                    take(("ret", "O"), V, 6)
                    pe.wait_ge(scalar_done, A.at(T, ("rvg", 1)))
                ps = bank(T, ("ret", "O"))
                pe.wait_ge(vector_done, V.at(T, ("ret", "sT", h)))
                c = h * HD
                nc.tensor.matmul(ps[:, c:c + HD], sT[:, h % 2, 0:P], rv[:, 0, c:c + HD], start=True, stop=True)
                nc.tensor.matmul(ps[:, 256 + c:256 + c + HD], sT[:, h % 2, P:SEQ], rv[:, 0, c:c + HD], start=True, stop=False)
                nc.tensor.matmul(ps[:, 256 + c:256 + c + HD], sT[:, h % 2, SEQ:384], rv[:, 1, c:c + HD], start=False, stop=True).then_inc(tensor_done, T.step(("ret", "PV", h)))

            def between(s):
                if s == 0:
                    in_proj("rqk", 1)
                    in_proj("rvg", 0)
                if s == 1:
                    in_proj("rvg", 1)
                    transposed_rope("rqk", 0, 4)
                    transposed_rope("rqk", 1, 4)
                if s == 2:
                    in_proj("mvo", 0)
                if s == 3:
                    in_proj("mvo", 1)
                    gates()
                if s == 4:
                    ret_scores(0)
                    ret_scores(1)
                    mqk(0)
                if s == 5:
                    ret_values(0)
                    ret_values(1)
                    ret_scores(2)
                    ret_scores(3)
                    mqk(1)
                if s == 6:
                    ret_values(2)
                    ret_values(3)
                    ada_row(4)
                if s == 7:
                    ada_row(5)

            pe_attention("att", ATT, 2, att_scores, lambda s: (sm[:, s % 2, :], 2 * (ATT[s][0] + 1)), att_values,
                         lambda s: (A, ("att", "exp", s)), pT,
                         {0: (("att", "O", 0), V, 6), NA // 2: (("att", "O", 1), V, 7)}, between)
            ada_gates(4)

            ps = take("gcol", V)
            pe.wait_ge(scalar_done, A.at(T, "erow"))
            for t in range(TT):
                for n, r in ((0, 2), (1, 5)):
                    last = nc.tensor.matmul(ps[:, 8 * t + 4 * n:8 * t + 4 * n + NR], grow[0:NR, r, t * P:(t + 1) * P],
                                            ident[0:NR, 0:NR], start=True, stop=True)
            last.then_inc(tensor_done, T.step("gcol"))

            def ml_scores(h):
                ps = take(("ml", "M", h), V)
                if h == 0:
                    pe.wait_ge(tables_loaded, 16 * 4)
                    pe.wait_ge(scalar_done, A.at(T, "conv"))
                nc.tensor.matmul(ps[:, 0:SEQ], crows[0:NR, h, :], grow[0:NR, 3, :], start=True, stop=True).then_inc(tensor_done, T.step(("ml", "M", h)))
                ps = take(("ml", "S", h), V)
                transposed_scores(ps, qkT, h).then_inc(tensor_done, T.step(("ml", "S", h)))

            ml_scores(0)
            ml_scores(1)
            ada_row(6)
            o0, o1 = take(("ml", "O", 0), V, 7), take(("ml", "O", 1), V, 6)
            for h in range(NR):
                pe.wait_ge(vector_done, V.at(T, ("ml", "sT", h)))
                if h == 0:
                    pe.wait_ge(scalar_done, A.at(T, ("mvo", 1)))
                c = h * (HD + 1)
                nc.tensor.matmul(o0[:, c:c + HD + 1], sT[:, h % 2, 0:P], mv[:, 0, h, :], start=True, stop=True)
                nc.tensor.matmul(o1[:, c:c + HD + 1], sT[:, h % 2, P:SEQ], mv[:, 0, h, :], start=True, stop=False)
                nc.tensor.matmul(o1[:, c:c + HD + 1], sT[:, h % 2, SEQ:384], mv[:, 1, h, :], start=False, stop=True).then_inc(tensor_done, T.step(("ml", "PV", h)))
                if h + 2 < NR:
                    ml_scores(h + 2)
                if h == 1:
                    ada_row(7)

            ada_columns(6)
            ada_row(8)
            ada_row(9)
            ada_columns(8)
            pe.wait_ge(vector_done, V.at(T, "o_cat"))
            transposed_x("oT", o_cat, A)
            pe.wait_ge(scalar_done, A.at(T, ("oTc", KT // 2 - 1)))
            for t in range(TT):
                for h in range(2):
                    if t == 0:
                        pe.wait_ge(G.sem(T, f"wo{h}"), G.level(T, f"wo{h}"))
                    ps = take(("wo", t, h), V)
                    token_product(ps, t, gslot(0, f"wo{h}"), N).then_inc(tensor_done, T.step(("wo", t, h)))

            ada_row(10)
            ada_row(11)
            ada_gates(10)
            pe.wait_ge(vector_done, V.at(T, "ln1"))
            transposed_x("xT2", x, V)

            def router():
                ps = psum[:, 3, :]
                for t in range(TT):
                    for k in range(KT):
                        for n, part in enumerate((h_hi[0].bitcast(F32), h_lo[:, :, :].bitcast(F32))):
                            last = nc.tensor.matmul(ps[:, t * NE:(t + 1) * NE], part[:, k, t * P:(t + 1) * P], wr[:, k, :],
                                                    start=k == 0 and n == 0, stop=k == KT - 1 and n == 1)
                last.then_inc(tensor_done, T.step("router"))

            pe_experts(NE, (V, ("hT2", "parts")), 0, router)
            T.end()

        DIFF = [(t, h) for t in range(TT) for h in range(DH)]
        WIN = [(t, g) for t in range(TT) for g in range(WG)]

        def pe_second(l):
            T.begin(1, l)
            on_bank.clear()
            turn[0] = 0
            pe.wait_ge(vector_done, V.before(T))
            pe.wait_ge(scalar_done, A.before(T))
            pe.wait_ge(params_loaded, params_count(T))
            ps = take("gains", V)
            pe.sem_inc(waited)
            nc.tensor.transpose(ps[:, 0:3 * KT + GG], grows[0:3 * KT + GG, :], ident[0:3 * KT + GG, 0:3 * KT + GG]).then_inc(tensor_done, T.step("gains"))
            ps = take("ws", A)
            for g in range(GG):
                last = nc.tensor.transpose(ps[:, g * P:(g + 1) * P], wsp[:, g, :], ident)
            last.then_inc(tensor_done, T.step("ws"))
            ps = take("p", A)
            for t in range(TT):
                for k in range(PLE // P):
                    last = nc.tensor.transpose(ps[:, k * SEQ + t * P:k * SEQ + (t + 1) * P], prow[:, t, k * P:(k + 1) * P], ident)
            last.then_inc(tensor_done, T.step("p"))
            pe.wait_ge(vector_done, V.at(T, ("xn", "mix")))
            transposed_x("xT", o_cat, V)
            pe.wait_ge(vector_done, V.at(T, ("hT", KT // 2 - 1)))

            def features(name, blocks):
                pe.wait_ge(G.sem(T, name), G.level(T, name))
                for b in range(0, blocks, 2):
                    ps = take((name, b // 2), A)
                    for f in range(min(2, blocks - b)):
                        last = feature_product(ps, gslot(1, name), (b + f) * P, P, f * SEQ)
                    last.then_inc(tensor_done, T.step((name, b // 2)))

            def tokens(name):
                pe.wait_ge(G.sem(T, name), G.level(T, name))
                for t in range(TT):
                    ps = take((name, t), A)
                    token_product(ps, t, gslot(1, name), N).then_inc(tensor_done, T.step((name, t)))

            features("aq", 3)
            features("ak", 3)
            tokens("avcv")
            tokens("buv")
            features("cqk", 4)

            def diff_scores(ps, s):
                t, h = DIFF[s]
                if s == 0:
                    pe.wait_ge(scalar_done, A.at(T, ("ak", "c", 1)))
                for c in range(2):
                    r = (h % 2) * HD + c * DQK
                    last = nc.tensor.matmul(ps[:, c, 0:SEQ], qT2[r:r + DQK, h // 2, t * P:(t + 1) * P],
                                            kT2[r:r + DQK, h // 2, :], start=True, stop=True)
                return last

            def diff_values(s):
                t, h = DIFF[s]
                if s == 0:
                    pe.wait_ge(scalar_done, A.at(T, ("avcv", "c", 1)))
                for k in range(TT):
                    last = nc.tensor.matmul(psum[:, 6 + t, h * HD:(h + 1) * HD], pT2[:, s % 2, k * P:(k + 1) * P],
                                            avcv[:, k, h * HD:(h + 1) * HD], start=k == 0, stop=k == TT - 1)
                return last

            pe_attention("diff", DIFF, 2, diff_scores, lambda s: (at2[:, s % 2, :], TT), diff_values,
                         lambda s: (V, ("diff", "at", s)), pT2,
                         {0: (("diff", "O", 0), V, 6), DH: (("diff", "O", 1), V, 7)}, lambda s: None)

            pe.wait_ge(vector_done, V.at(T, ("vn", 1)))
            pe.wait_ge(scalar_done, A.at(T, "wsT"))
            pe.sem_inc(waited)
            ps = take("mix", V)
            for g in range(GG):
                last = nc.tensor.matmul(ps[:, g * P:(g + 1) * P], wsT[:, g, :], vn[:, :, g * HD:(g + 1) * HD],
                                        start=True, stop=True)
            last.then_inc(tensor_done, T.step("mix"))

            def win_scores(ps, s):
                t, g = WIN[s]
                if s == 0:
                    pe.wait_ge(scalar_done, A.at(T, ("cqk", "c", 1)))
                for h in range(2):
                    last = nc.tensor.matmul(ps[:, h, 0:SEQ], cT2[h * HD:(h + 1) * HD, g, t * P:(t + 1) * P],
                                            cT2[h * HD:(h + 1) * HD, WG, :], start=True, stop=True)
                return last

            def win_values(s):
                t, g = WIN[s]
                for h in range(2):
                    c = (h * WG + g) * HD
                    for k in range(TT):
                        last = nc.tensor.matmul(psum[:, 6 + t, c:c + HD], pT2[:, s % 2, (h * TT + k) * P:(h * TT + k + 1) * P],
                                                avcv[:, k, 384 + h * HD:384 + (h + 1) * HD], start=k == 0, stop=k == TT - 1)
                return last

            pe_attention("win", WIN, 2, win_scores, lambda s: (sm2[:, s % 2, :], 2 * TT), win_values,
                         lambda s: (A, ("win", "exp", s)), pT2,
                         {0: (("win", "O", 0), V, 6), WG: (("win", "O", 1), V, 7)}, lambda s: None)

            pe.wait_ge(vector_done, V.at(T, "o_cat"))
            transposed_x("oT", o_cat, A)
            pe.wait_ge(scalar_done, A.at(T, ("oTc", KT // 2 - 1)))
            for h in range(2):
                pe.wait_ge(G.sem(T, f"wo{h}"), G.level(T, f"wo{h}"))
                for t in range(TT):
                    ps = take(("wo", t, h), A)
                    token_product(ps, t, gslot(1, f"wo{h}"), N).then_inc(tensor_done, T.step(("wo", t, h)))
            pe.wait_ge(vector_done, V.at(T, ("xn", "ffn")))
            transposed_x("xT2", o_cat, V)
            pe_experts(NF, (V, ("hT2", "parts")), 1)
            for b in range(4):
                on_bank[4 + b] = (A, ("read", ("acc", b)))
            for t in range(TT):
                on_bank[t], on_bank[2 + t] = (V, ("hid", NF - 1, t)), (V, ("hidT", NF - 1, t))
            pe.wait_ge(DN.sem(T, "up"), DN.level(T, "up"))
            pe.wait_ge(scalar_done, A.at(T, "pT"))
            for t in range(TT):
                for h in range(2):
                    ps = take(("e", t, h), A)
                    for k in range(PLE // P):
                        last = nc.tensor.matmul(ps, pTT[:, k, t * P:(t + 1) * P], dslot(1, "up")[:, k, h * N:(h + 1) * N],
                                                start=k == 0, stop=k == PLE // P - 1)
                    last.then_inc(tensor_done, T.step(("e", t, h)))
            pe.wait_ge(vector_done, V.at(T, ("xn", "ple")))
            transposed_x("xT3", o_cat, V)
            pe.wait_ge(vector_done, V.at(T, ("hT3", KT // 2 - 1)))
            for h in range(2):
                pe.wait_ge(G.sem(T, f"pg{h}"), G.level(T, f"pg{h}"))
                for t in range(TT):
                    ps = take(("pg", t, h), A)
                    token_product(ps, t, gslot(1, f"pg{h}"), N).then_inc(tensor_done, T.step(("pg", t, h)))
            T.end()

        @block.tensor
        def _(pe):
            pe.sem_inc(tensor_done, T.step(by=AHEAD))
            pe.wait_ge(start_loaded, 16 * 3)
            nc.tensor.transpose(psum[:, 0, 0:KT], c8, ident[0:KT, 0:KT]).then_inc(tensor_done, T.step("c"))
            pe.wait_ge(vector_done, V.at(T, "cact"))
            with pe.Fori(0, DEPTH) as l:
                pe_first(l)
            with pe.Fori(0, DEPTH) as l:
                pe_second(l)

        def ts(o, a, s1, s2, op0, op1=None):
            if op1 is None:
                return nc.vector.tensor_scalar(o, a, s1, None, op0)
            return nc.vector.tensor_scalar(o, a, s1, s2, op0, op1)

        def tt(o, a, b, op):
            return nc.vector.tensor_tensor(o, a, b, op)

        def stt(o, a, s, b, op0, op1):
            return nc.vector.scalar_tensor_tensor(o, a, s, b, op0, op1)

        def vmax(o, a):
            return nc.vector.tensor_reduce(o, a, AX.X, ALU.max)

        def vsum(o, a):
            return nc.vector.tensor_reduce(o, a, AX.X, ALU.add)

        def over(col, *shape):
            return col.unsqueeze(2).to_broadcast([P, *shape])

        def rope(ps, nh, t, o, name, last_read):
            heads = ps[:, 0:nh * HD].rearrange("p (h d) -> p h d", h=nh)
            a = tmp[:, 0, 0:nh * HD].rearrange("p (h d) -> p h d", h=nh)
            b = tmp[:, 1, 0:nh * HD].rearrange("p (h d) -> p h d", h=nh)
            cs = cosf[:, t, :].unsqueeze(1).to_broadcast([P, nh, HD])
            tt(a, heads, cs, ALU.mult).then_inc(vector_done, V.step())
            dve.wait_ge(vector_done, V.now())
            for h, g in ((0, 1), (1, 0)):
                sn = sinf[:, t, h * HALF:(h + 1) * HALF].unsqueeze(1).to_broadcast([P, nh, HALF])
                tt(b[:, :, h * HALF:(h + 1) * HALF], heads[:, :, g * HALF:(g + 1) * HALF], sn, ALU.mult).then_inc(vector_done, V.step(last_read if h else None))
                dve.wait_ge(vector_done, V.now())
            tt(o.rearrange("p (h d) -> p h d", h=nh), a, b, ALU.add).then_inc(vector_done, V.step(name))
            dve.wait_ge(vector_done, V.now())

        def head_variance(name):
            vsum(hs, hn).then_inc(vector_done, V.step())
            dve.wait_ge(vector_done, V.now())
            ts(hs, hs, 1.0 / HD, None, ALU.mult).then_inc(vector_done, V.step())
            dve.wait_ge(vector_done, V.now())
            tt(hn, hn, over(hs, 8, HD), ALU.subtract).then_inc(vector_done, V.step())
            dve.wait_ge(vector_done, V.now())
            tt(sq, hn, hn, ALU.mult).then_inc(vector_done, V.step())
            dve.wait_ge(vector_done, V.now())
            vsum(hv, sq).then_inc(vector_done, V.step())
            dve.wait_ge(vector_done, V.now())
            ts(hv, hv, 1.0 / HD, LN_EPS, ALU.mult, ALU.add).then_inc(vector_done, V.step((name, "var")))
            dve.wait_ge(vector_done, V.now())

        def head_normed(name):
            dve.wait_ge(scalar_done, A.at(V, (name, "sqrt")))
            nc.vector.reciprocal(hs, hv).then_inc(vector_done, V.step())
            dve.wait_ge(vector_done, V.now())
            tt(sq, hn, over(hs, 8, HD), ALU.mult).then_inc(vector_done, V.step())
            dve.wait_ge(vector_done, V.now())

        def moments(name, t):
            for h in range(2):
                nc.vector.bn_stats(st[:, 6 * h:6 * h + 6], x[:, t, h * N:(h + 1) * N]).then_inc(vector_done, V.step())
                dve.wait_ge(vector_done, V.now())
            dve.sem_inc(waited)
            nc.vector.bn_aggr(agg[:, 2 * t:2 * t + 2], st).then_inc(vector_done, V.step())
            dve.wait_ge(vector_done, V.now())
            ts(rstd[:, t:t + 1], agg[:, 2 * t + 1:2 * t + 2], LN_EPS, None, ALU.add).then_inc(vector_done, V.step((name, "var", t)))
            dve.wait_ge(vector_done, V.now())

        def layer_norm(name, t):
            dve.wait_ge(scalar_done, A.at(V, (name, "sqrt", t)))
            nc.vector.reciprocal(rstd[:, TT + t:TT + t + 1], rstd[:, t:t + 1]).then_inc(vector_done, V.step())
            dve.wait_ge(vector_done, V.now())
            ts(x[:, t, :], x[:, t, :], agg[:, 2 * t:2 * t + 1], rstd[:, TT + t:TT + t + 1], ALU.subtract, ALU.mult).then_inc(vector_done, V.step())
            dve.wait_ge(vector_done, V.now())
            tt(x[:, t, :], x[:, t, :], rows[:, 0, :], ALU.mult).then_inc(vector_done, V.step())
            dve.wait_ge(vector_done, V.now())
            tt(x[:, t, :], x[:, t, :], rows[:, 1, :], ALU.add).then_inc(vector_done, V.step((name, t)))
            dve.wait_ge(vector_done, V.now())

        def modulated(tag, name, shift, scale):
            for g in range(KT // 2):
                dve.wait_ge(tensor_done, T.at(V, (tag, g)))
                ps = bank(V, (tag, g))
                for f in range(2):
                    k = 2 * g + f
                    ts(hT[:, k, :], ps[:, f * SEQ:(f + 1) * SEQ], scale[:, k:k + 1], shift[:, k:k + 1], ALU.mult, ALU.add).then_inc(vector_done, V.step(("read", (tag, g)) if f else None))
                    dve.wait_ge(vector_done, V.now())
                V.also((name, g))

        def input_rest(name):
            for g in range(KT // 2):
                dve.wait_ge(scalar_done, A.at(V, (name, "hi", g)))
                tt(h_lo[:, 2 * g:2 * g + 2, :], hT[:, 2 * g:2 * g + 2, :], h_hi[V.block][:, 2 * g:2 * g + 2, :], ALU.subtract).then_inc(vector_done, V.step((name, "parts") if g == KT // 2 - 1 else None))

        def weights_rest(e, i, rounded, name):
            w, w_rest, hi = gslot(V.block, f"gu{e}"), g_rest(V.block, f"gu{e}"), w_hi[e % 2]
            for q in range(2):
                k = slice(q * KT // 2, (q + 1) * KT // 2)
                dve.wait_ge(scalar_done, A.at(V, (*rounded, q), i))
                tt(w_rest[:, k, 0:N], w[:, k, 0:N], hi[:, k, :], ALU.subtract).then_inc(vector_done, V.step(name if q else None))

        def dve_experts(ne, gated):
            n = NIT[ne]

            def one(e, i, step, name, column, following):
                for t in range(TT):
                    dve.wait_ge(scalar_done, A.at(V, ("silu", *step, t), i))
                    up = psum[:, t, FE:2 * FE]
                    if gated:
                        stt(hid[:, t, :], up, column(t), sact[:, t, :], ALU.mult, ALU.mult).then_inc(vector_done, V.step((*name, t)))
                    else:
                        tt(hid[:, t, :], up, sact[:, t, :], ALU.mult).then_inc(vector_done, V.step((*name, t)))
                    if t == 0:
                        if following is not None:
                            weights_rest(e + 1, i, ("w_hi", *following), ("parts", *following))
                        dve.wait_ge(scalar_done, A.at(V, ("d_hi", *step), i))
                        d = dslot(V.block, f"dn{e}")
                        tt(d_rest(V.block, f"dn{e}"), d, d_hi[e % 2], ALU.subtract).then_inc(vector_done, V.step())
                for t in range(TT):
                    dve.wait_ge(scalar_done, A.at(V, ("hidT", *step, t), i))
                    tt(hidT_lo[:, t, :, :].rearrange("p f n -> p (f n)"), psum[:, 2 + t, 0:FE],
                       hidT[:, t, :, :].rearrange("p f n -> p (f n)"), ALU.subtract).then_inc(vector_done, V.step(("hidT", *step, t)))

            def static_column(e):
                return lambda t: gate[:, t * NE + e:t * NE + e + 1]

            one(0, None, (0,), ("hid", 0), static_column(0), (1,))
            with nc.vector.Fori(0, n) as i:
                V.loop(f"dve{V.block}", n)
                for j in range(4):
                    one(1 + j, i, ("loop", j), ("hid", "loop", j),
                        lambda t, j=j: gate[:, bass.ds(i * 4 + (t * NE + 1 + j), 1)], ("loop", j))
                V.loop_end()
            for e in range(1 + 4 * n, ne):
                one(e, None, (e,), ("hid", e), static_column(e), (e + 1,) if e + 1 < ne else None)

        def dve_first(l):
            V.begin(0, l)
            dve.wait_ge(scalar_done, A.before(V))
            dve.wait_ge(tensor_done, T.before(V))

            def shift_columns(c, i):
                dve.wait_ge(tensor_done, T.at(V, ("arows_used", c)))
                ts(mod[i], bank(V, ("columns", c))[:, 0:KT], float(i % 2), None, ALU.add).then_inc(vector_done, V.step(("read", ("columns", c))))
                dve.wait_ge(vector_done, V.now())

            shift_columns(2, 1)
            shift_columns(0, 0)
            modulated("xT", "hT", mod[0], mod[1])

            slots = {}

            def rope_chunk(name, t, nh):
                i = len(slots)
                slots[i] = (name, t)
                dve.wait_ge(tensor_done, T.at(V, (name, t)))
                ps = bank(V, (name, t))
                if i >= 3:
                    dve.wait_ge(tensor_done, T.at(V, (slots[i - 3][0], "T", slots[i - 3][1])))
                o = roped[:, i % 3, :]
                if name == "idx":
                    nc.vector.tensor_copy(iw[:, t * NI:(t + 1) * NI], ps[:, IW - IQ:RQ - IQ]).then_inc(vector_done, V.step())
                    dve.wait_ge(vector_done, V.now())
                    rope(ps, nh, t, o[:, 0:nh * HD], None, ("read", (name, t)))
                    nc.vector.tensor_copy(o[:, nh * HD:(nh + 1) * HD], o[:, (nh - 1) * HD:nh * HD]).then_inc(vector_done, V.step(("rope", name, t)))
                    dve.wait_ge(vector_done, V.now())
                else:
                    rope(ps, nh, t, o, ("rope", name, t), ("read", (name, t)))

            def top_k(t):
                nk = (t + 1) * P
                w = score[:, 0:nk]
                dve.wait_ge(scalar_done, A.at(V, ("rel", t)))
                for h in range(NI):
                    prev = cblock[:, C1["vis"] + t * SEQ:C1["vis"] + t * SEQ + nk] if h == 0 else w
                    stt(w, rel[:, (h % 2) * 2 + h // 2, 0:nk], iw[:, t * NI + h:t * NI + h + 1], prev, ALU.mult, ALU.add).then_inc(vector_done, V.step(("rel_read", t) if h == NI - 1 else None))
                    dve.wait_ge(vector_done, V.now())
                for r in range(TOPK // 8):
                    dve.sem_inc(waited)
                    nc.vector.max(top8, w).then_inc(vector_done, V.step())
                    dve.wait_ge(vector_done, V.now())
                    dve.sem_inc(waited)
                    nc.vector.match_replace(w, top8, w, TAKEN).then_inc(vector_done, V.step())
                    dve.wait_ge(vector_done, V.now())
                ts(bias[:, t, 0:nk], w, -2.0e38, -BIG, ALU.is_gt, ALU.mult).then_inc(vector_done, V.step())
                dve.wait_ge(vector_done, V.now())

            def scale_iw(t):
                ts(iw[:, t * NI:(t + 1) * NI], iw[:, t * NI:(t + 1) * NI], (NI * HD) ** -0.5, None, ALU.mult).then_inc(vector_done, V.step())
                dve.wait_ge(vector_done, V.now())

            def att_in(s):
                t, i = ATT[s]
                nk = (t + 1) * P
                dve.wait_ge(tensor_done, T.at(V, ("att", "S", s)))
                ps = bank(V, ("att", "S", s))
                if s >= 2:
                    dve.wait_ge(tensor_done, T.at(V, ("att", "PT", s - 2)))
                o = sm[:, s % 2, 0:2 * nk].rearrange("p (h k) -> p h k", h=2)
                bb = bias[:, t, 0:nk].unsqueeze(1).to_broadcast([P, 2, nk])
                stt(o, ps[:, :, 0:nk], HD ** -0.5, bb, ALU.mult, ALU.add).then_inc(vector_done, V.step(("read", ("att", "S", s))))
                dve.wait_ge(vector_done, V.now())
                nc.vector.tensor_reduce(ngm[:, 2 * (s % 2):2 * (s % 2) + 2], o, AX.X, ALU.max, negate=True).then_inc(vector_done, V.step(("att", "max", s)))
                dve.wait_ge(vector_done, V.now())

            def att_out(t):
                dve.wait_ge(scalar_done, A.at(V, ("att", "exp", (t + 1) * (NA // 2) - 1)))
                nc.vector.reciprocal(rinv[:, t * NA:(t + 1) * NA], rsum[:, t * NA:(t + 1) * NA]).then_inc(vector_done, V.step())
                dve.wait_ge(vector_done, V.now())
                dve.wait_ge(tensor_done, T.at(V, ("att", "PV", (t + 1) * (NA // 2) - 1)))
                tt(o_cat[:, t, 0:N].rearrange("p (h d) -> p h d", h=NA), bank(V, ("att", "O", t)).rearrange("p (h d) -> p h d", h=NA), over(rinv[:, t * NA:(t + 1) * NA], NA, HD), ALU.mult).then_inc(vector_done, V.step(("read", ("att", "O", t))))
                dve.wait_ge(vector_done, V.now())

            def ret_weights(h):
                dve.wait_ge(tensor_done, T.at(V, ("ret", "S", h)))
                ps = bank(V, ("ret", "S", h))
                if h >= 2:
                    dve.wait_ge(tensor_done, T.at(V, ("ret", "PV", h - 2)))
                tt(sT[:, h % 2, :], ps[:, 0:384], cblock[:, h * 384:(h + 1) * 384], ALU.mult).then_inc(vector_done, V.step(("ret", "sT", h)))
                dve.wait_ge(vector_done, V.now())
                V.also(("read", ("ret", "S", h)))

            g4 = grow[0:NR]

            def gate_rows():
                dve.wait_ge(tensor_done, T.at(V, "gates"))
                ps = bank(V, "gates")
                dve.wait_ge(params_loaded, params_count(V))
                ts(g4[:, 0, :], ps[0:NR, 0:SEQ], ibias[0:NR], None, ALU.add).then_inc(vector_done, V.step())
                dve.wait_ge(vector_done, V.now())
                ts(g4[:, 1, :], ps[0:NR, SEQ:2 * SEQ], fbias[0:NR], None, ALU.add).then_inc(vector_done, V.step(("read", "gates")))
                dve.wait_ge(vector_done, V.now())
                stt(g4[:, 5, :], g4[:, 1, :], -1.0, g4[:, 1, :], ALU.mult, ALU.min).then_inc(vector_done, V.step("negabs"))
                dve.wait_ge(vector_done, V.now())
                ts(g4[:, 1, :], g4[:, 1, :], 0.0, None, ALU.min).then_inc(vector_done, V.step())
                dve.wait_ge(vector_done, V.now())

            def conv(b):
                if b % 2 == 0:
                    dve.wait_ge(scalar_done, A.at(V, ("mqk", "c", b // 2)))
                o = qkT[:, b, :]
                ts(o, cin[:, b, 0:SEQ], convw[:, b, 0:1], convw[:, b, CONV:CONV + 1], ALU.mult, ALU.add).then_inc(vector_done, V.step())
                dve.wait_ge(vector_done, V.now())
                for j in range(1, CONV):
                    stt(o, cin[:, b, j:j + SEQ], convw[:, b, j:j + 1], o, ALU.mult, ALU.add).then_inc(vector_done, V.step("conv" if b == 3 and j == CONV - 1 else None))
                    dve.wait_ge(vector_done, V.now())

            def gate_sums():
                dve.wait_ge(scalar_done, A.at(V, "softplus"))
                tt(g4[:, 4, :], g4[:, 1, :], g4[:, 5, :], ALU.subtract).then_inc(vector_done, V.step())
                dve.wait_ge(vector_done, V.now())
                nc.vector.tensor_tensor_scan(g4[:, 1, :], ones[0:NR, 0:SEQ], g4[:, 4, :], 0.0, ALU.mult, ALU.add).then_inc(vector_done, V.step())
                dve.wait_ge(vector_done, V.now())
                tt(g4[:, 2, :], g4[:, 0, :], g4[:, 1, :], ALU.subtract).then_inc(vector_done, V.step())
                dve.wait_ge(vector_done, V.now())
                nc.vector.tensor_tensor_scan(g4[:, 3, :], g4[:, 2, :], g4[:, 2, :], 0.0, ALU.max, ALU.max).then_inc(vector_done, V.step())
                dve.wait_ge(vector_done, V.now())
                tt(g4[:, 4, :], g4[:, 1, :], g4[:, 3, :], ALU.add).then_inc(vector_done, V.step("bm"))
                dve.wait_ge(vector_done, V.now())


            for t in range(TT):
                rope_chunk("idx", t, NI + 1)
                scale_iw(t)
            for t in range(TT):
                rope_chunk("aq", t, NA)
            dve.wait_ge(tables_loaded, 16 * 4)
            top_k(0)
            for t in range(TT):
                rope_chunk("ak", t, NA)
            top_k(1)
            rope_chunk("rqk", 0, 2 * NR)
            att_in(0)
            att_in(1)
            rope_chunk("rqk", 1, 2 * NR)
            for s in range(len(ATT)):
                if s == 3:
                    gate_rows()
                if s == 4:
                    att_out(0)
                    ret_weights(0)
                    ret_weights(1)
                if s == 5:
                    ret_weights(2)
                    ret_weights(3)
                    conv(0)
                    conv(1)
                if s == 6:
                    dve.wait_ge(tensor_done, T.at(V, ("ret", "PV", NR - 1)))
                    nc.vector.tensor_copy(hn.rearrange("p h d -> p (h d)"), bank(V, ("ret", "O"))).then_inc(vector_done, V.step(("read", ("ret", "O"))))
                    dve.wait_ge(vector_done, V.now())
                    conv(2)
                    conv(3)
                if s == 7:
                    gate_sums()
                if s + 2 < len(ATT):
                    att_in(s + 2)
            att_out(1)
            head_variance("ret")

            def gate_row(c):
                for n in range(2):
                    dve.wait_ge(tensor_done, T.at(V, ("gate", c + n)))
                    ts(gb[:, n * N:(n + 1) * N], bank(V, ("gate", c + n)), 1.0, None, ALU.add).then_inc(vector_done, V.step(("read", ("gate", c + n))))
                    dve.wait_ge(vector_done, V.now())

            gate_row(4)
            dve.wait_ge(tensor_done, T.at(V, "gcol"))
            ps = bank(V, "gcol")
            nc.vector.tensor_copy(gcol, ps[:, 0:16]).then_inc(vector_done, V.step(("read", "gcol")))
            dve.wait_ge(vector_done, V.now())

            for h in range(NR):
                dve.wait_ge(tensor_done, T.at(V, ("ml", "M", h)))
                ps = bank(V, ("ml", "M", h))
                if h >= 2:
                    dve.wait_ge(tensor_done, T.at(V, ("ml", "PV", h - 2)))
                ca = cblock[:, C1["causal"]:C1["causal"] + SEQ]
                stt(wT[:, h % 2, 0:SEQ], ps[:, 0:SEQ], gcol[:, h:h + 1], ca, ALU.add, ALU.add).then_inc(vector_done, V.step())
                dve.wait_ge(vector_done, V.now())
                stt(wT[:, h % 2, SEQ:384], ps[:, P:SEQ], gcol[:, 8 + h:9 + h], ca[:, 0:P], ALU.add, ALU.add).then_inc(vector_done, V.step(("ml", "arg", h)))
                dve.wait_ge(vector_done, V.now())
                V.also(("read", ("ml", "M", h)))
                dve.wait_ge(tensor_done, T.at(V, ("ml", "S", h)))
                ps = bank(V, ("ml", "S", h))
                dve.wait_ge(scalar_done, A.at(V, ("ml", "exp", h)))
                stt(sT[:, h % 2, :], ps[:, 0:384], HD ** -0.5, wT[:, h % 2, :], ALU.mult, ALU.mult).then_inc(vector_done, V.step(("ml", "sT", h)))
                dve.wait_ge(vector_done, V.now())
                V.also(("read", ("ml", "S", h)))
            head_normed("ret")
            dve.wait_ge(scalar_done, A.at(V, "rg"))
            tt(o_cat[:, :, 512:768], sq.rearrange("p (t h) d -> p t (h d)", t=TT), rg, ALU.mult).then_inc(vector_done, V.step())
            dve.wait_ge(vector_done, V.now())
            dve.wait_ge(tensor_done, T.at(V, ("ml", "PV", NR - 1)))
            dve.wait_ge(scalar_done, A.at(V, "mo"))
            for t in range(TT):
                ps = bank(V, ("ml", "O", t))
                o = ps[:, 0:NR * (HD + 1)].rearrange("p (h d) -> p h d", h=NR)
                nc.vector.tensor_copy(den, o[:, :, HD:HD + 1]).then_inc(vector_done, V.step())
                dve.wait_ge(vector_done, V.now())
                stt(hv[:, 0:NR], den, -1.0, den, ALU.mult, ALU.max).then_inc(vector_done, V.step())
                dve.wait_ge(vector_done, V.now())
                tt(hv[:, 0:NR], hv[:, 0:NR], gcol[:, 8 * t + NR:8 * t + 2 * NR], ALU.max).then_inc(vector_done, V.step())
                dve.wait_ge(vector_done, V.now())
                nc.vector.reciprocal(hs[:, 0:NR], hv[:, 0:NR]).then_inc(vector_done, V.step())
                dve.wait_ge(vector_done, V.now())
                tt(hn[:, NR * t:NR * (t + 1), :], o[:, :, 0:HD], over(hs[:, 0:NR], NR, HD), ALU.mult).then_inc(vector_done, V.step(("read", ("ml", "O", t))))
                dve.wait_ge(vector_done, V.now())
            hflat = hn.rearrange("p (t h) d -> p t (h d)", t=TT)
            tt(hflat, hflat, mo, ALU.mult).then_inc(vector_done, V.step())
            dve.wait_ge(vector_done, V.now())
            head_variance("ml")
            head_normed("ml")
            nc.vector.tensor_copy(o_cat[:, :, 768:1024], sq.rearrange("p (t h) d -> p t (h d)", t=TT)).then_inc(vector_done, V.step("o_cat"))
            dve.wait_ge(vector_done, V.now())
            shift_columns(6, 2)
            shift_columns(8, 3)

            def residual(ps, t, h, read):
                o = x[:, t, h * N:(h + 1) * N]
                tt(tmp[:, 0, :], ps, gb[:, h * N:(h + 1) * N], ALU.mult).then_inc(vector_done, V.step(read))
                dve.wait_ge(vector_done, V.now())
                stt(o, o, ALPHA, tmp[:, 0, :], ALU.mult, ALU.add).then_inc(vector_done, V.step())
                dve.wait_ge(vector_done, V.now())

            dve.wait_ge(gains_loaded, gains_count(V))
            for t in range(TT):
                for h in range(2):
                    dve.wait_ge(tensor_done, T.at(V, ("wo", t, h)))
                    residual(bank(V, ("wo", t, h)), t, h, ("read", ("wo", t, h)))
                moments("ln1", t)
                if t:
                    layer_norm("ln1", 0)
            layer_norm("ln1", 1)
            V.also("ln1")
            gate_row(10)
            weights_rest(0, None, ("w_hi", 0), ("parts", 0))
            modulated("xT2", "hT2", mod[2], mod[3])
            input_rest("hT2")

            dve.wait_ge(scalar_done, A.at(V, "router"))
            v3 = lambda a, n: a.rearrange("p (t n) -> p t n", n=n)
            tt(v3(biased, NE), v3(scores, NE), br[:, :].unsqueeze(1).to_broadcast([P, TT, NE]), ALU.add).then_inc(vector_done, V.step())
            dve.wait_ge(vector_done, V.now())
            b4, pr = v3(biased, EG), v3(pairs, 6)
            tt(pr[:, :, 0:2], b4[:, :, 0:2], b4[:, :, 2:4], ALU.add).then_inc(vector_done, V.step())
            dve.wait_ge(vector_done, V.now())
            tt(pr[:, :, 2:4], b4[:, :, 0:4:2], b4[:, :, 1:4:2], ALU.add).then_inc(vector_done, V.step())
            dve.wait_ge(vector_done, V.now())
            tt(pr[:, :, 4:5], b4[:, :, 0:1], b4[:, :, 3:4], ALU.add).then_inc(vector_done, V.step())
            dve.wait_ge(vector_done, V.now())
            tt(pr[:, :, 5:6], b4[:, :, 1:2], b4[:, :, 2:3], ALU.add).then_inc(vector_done, V.step())
            dve.wait_ge(vector_done, V.now())
            vmax(gsum, pr).then_inc(vector_done, V.step())
            dve.wait_ge(vector_done, V.now())

            def first_best(o, src, key, n, weights):
                vmax(t2, v3(src, n)).then_inc(vector_done, V.step())
                dve.wait_ge(vector_done, V.now())
                tt(v3(key, n), v3(src, n), over(t2, TT, n), ALU.is_equal).then_inc(vector_done, V.step())
                dve.wait_ge(vector_done, V.now())
                tt(v3(key, n), v3(key, n), weights.unsqueeze(1).to_broadcast([P, TT, n]), ALU.mult).then_inc(vector_done, V.step())
                dve.wait_ge(vector_done, V.now())
                vmax(t2, v3(key, n)).then_inc(vector_done, V.step())
                dve.wait_ge(vector_done, V.now())
                tt(v3(o, n), v3(key, n), over(t2, TT, n), ALU.is_equal).then_inc(vector_done, V.step())
                dve.wait_ge(vector_done, V.now())

            first4 = cshared[:, CONST["first4"]:CONST["first4"] + NG]
            first16 = cshared[:, CONST["first16"]:CONST["first16"] + NE]
            first_best(gsum, gsum, key4, NG, first4)
            ts(gsum, gsum, -1.0, BIG, ALU.add, ALU.mult).then_inc(vector_done, V.step())
            dve.wait_ge(vector_done, V.now())
            tt(v3(bmask, EG), b4, over(gsum, 8, EG), ALU.add).then_inc(vector_done, V.step())
            dve.wait_ge(vector_done, V.now())
            first_best(sel, bmask, onehot, NE, first16)
            stt(bmask, sel, -BIG, bmask, ALU.mult, ALU.add).then_inc(vector_done, V.step())
            dve.wait_ge(vector_done, V.now())
            first_best(biased, bmask, onehot, NE, first16)
            tt(sel, sel, biased, ALU.add).then_inc(vector_done, V.step())
            dve.wait_ge(vector_done, V.now())
            tt(gate, sel, scores, ALU.mult).then_inc(vector_done, V.step())
            dve.wait_ge(vector_done, V.now())
            vsum(t2, v3(gate, NE)).then_inc(vector_done, V.step())
            dve.wait_ge(vector_done, V.now())
            nc.vector.reciprocal(t2, t2).then_inc(vector_done, V.step())
            dve.wait_ge(vector_done, V.now())
            tt(v3(gate, NE), v3(gate, NE), over(t2, TT, NE), ALU.mult).then_inc(vector_done, V.step())
            dve.wait_ge(vector_done, V.now())
            dve_experts(NE, True)
            dve.wait_ge(vector_done, V.now())
            dve.wait_ge(rows_loaded, rows_count(V))
            for t in range(TT):
                dve.wait_ge(tensor_done, T.at(V, ("dn0", NE - 1) if t == 0 else ("dn1", NE - 1)))
                for h in range(2):
                    residual(psum[:, 4 + 2 * t + h, :], t, h, None)
                moments("ln2", t)
                if t:
                    layer_norm("ln2", 0)
            layer_norm("ln2", 1)
            V.end()

        def rms(name):
            dve.wait_ge(scalar_done, A.at(V, (name, "ss")))
            ts(rstd[:, 0:TT], agg[:, 0:TT], 1.0 / D, RMS_EPS, ALU.mult, ALU.add).then_inc(vector_done, V.step((name, "var")))
            dve.wait_ge(vector_done, V.now())
            dve.wait_ge(scalar_done, A.at(V, (name, "sqrt")))
            nc.vector.reciprocal(rstd[:, TT:2 * TT], rstd[:, 0:TT]).then_inc(vector_done, V.step())
            dve.wait_ge(vector_done, V.now())

        def pre_norm(name):
            rms(("pre", name))
            for t in range(TT):
                ts(o_cat[:, t, :], x[:, t, :], rstd[:, TT + t:TT + t + 1], None, ALU.mult).then_inc(vector_done, V.step(("xn", name) if t else None))
                dve.wait_ge(vector_done, V.now())

        def gained(tag, name, gains):
            for g in range(KT // 2):
                dve.wait_ge(tensor_done, T.at(V, (tag, g)))
                ps = bank(V, (tag, g))
                for f in range(2):
                    k = 2 * g + f
                    ts(hT[:, k, :], ps[:, f * SEQ:(f + 1) * SEQ], gcols[:, gains + k:gains + k + 1], None, ALU.mult).then_inc(vector_done, V.step(("read", (tag, g)) if f else None))
                    dve.wait_ge(vector_done, V.now())
                V.also((name, g))

        def post_norm(name, row):
            rms(("post", name))
            for t in range(TT):
                stt(y2[:, t, :], y2[:, t, :], rstd[:, TT + t:TT + t + 1], rows[:, row, :], ALU.mult, ALU.mult).then_inc(vector_done, V.step())
                dve.wait_ge(vector_done, V.now())
                tt(x[:, t, :], x[:, t, :], y2[:, t, :], ALU.add).then_inc(vector_done, V.step(("x", name) if t else None))
                dve.wait_ge(vector_done, V.now())

        def dve_second(l):
            V.begin(1, l)
            dve.wait_ge(scalar_done, A.before(V))
            dve.wait_ge(tensor_done, T.before(V))
            dve.wait_ge(params_loaded, params_count(V))
            dve.wait_ge(const_loaded, 16)
            lq = lprod.rearrange("p (a d) -> p a d", a=2)
            tt(lq, lamrow[:, 0:2, :], lamrow[:, 2:4, :], ALU.mult).then_inc(vector_done, V.step())
            dve.wait_ge(vector_done, V.now())
            vsum(lsum, lq).then_inc(vector_done, V.step("lsum"))
            dve.wait_ge(vector_done, V.now())
            ts(subrow, subrow, lamc[:, 1:2], None, ALU.mult).then_inc(vector_done, V.step())
            dve.wait_ge(vector_done, V.now())
            dve.wait_ge(scalar_done, A.at(V, "lexp"))
            tt(lam, lsum[:, 0:1], lsum[:, 1:2], ALU.subtract).then_inc(vector_done, V.step())
            dve.wait_ge(vector_done, V.now())
            tt(lam, lam, lamc[:, 0:1], ALU.add).then_inc(vector_done, V.step())
            dve.wait_ge(vector_done, V.now())
            dve.wait_ge(tensor_done, T.at(V, "gains"))
            ps = bank(V, "gains")
            nc.vector.tensor_copy(gcols, ps[:, 0:3 * KT + GG]).then_inc(vector_done, V.step(("read", "gains")))
            dve.wait_ge(vector_done, V.now())
            pre_norm("mix")
            gained("xT", "hT", 0)

            for t in range(TT):
                dve.wait_ge(scalar_done, A.at(V, ("buv", "c", t)))
                nc.vector.bn_stats(st[:, 0:6], buv[:, t, GW:2 * GW]).then_inc(vector_done, V.step())
                dve.wait_ge(vector_done, V.now())
                dve.sem_inc(waited)
                nc.vector.bn_aggr(agg[:, 2 * t:2 * t + 2], st[:, 0:6]).then_inc(vector_done, V.step())
                dve.wait_ge(vector_done, V.now())
                ts(rstd[:, t:t + 1], agg[:, 2 * t + 1:2 * t + 2], RMS_EPS, None, ALU.add).then_inc(vector_done, V.step(("vn", "var") if t else None))
                dve.wait_ge(vector_done, V.now())
            dve.wait_ge(scalar_done, A.at(V, ("vn", "sqrt")))
            nc.vector.reciprocal(rstd[:, TT:2 * TT], rstd[:, 0:TT]).then_inc(vector_done, V.step())
            dve.wait_ge(vector_done, V.now())
            for t in range(TT):
                ts(vn[:, t, :], buv[:, t, GW:2 * GW], agg[:, 2 * t:2 * t + 1], rstd[:, TT + t:TT + t + 1], ALU.subtract, ALU.mult).then_inc(vector_done, V.step())
                dve.wait_ge(vector_done, V.now())
                tt(vn[:, t, :], vn[:, t, :], glnrow[:, 0, :], ALU.mult).then_inc(vector_done, V.step())
                dve.wait_ge(vector_done, V.now())
                tt(vn[:, t, :], vn[:, t, :], glnrow[:, 1, :], ALU.add).then_inc(vector_done, V.step(("vn", t)))
                dve.wait_ge(vector_done, V.now())

            scale = DQK ** -0.5

            def diff_in(s):
                t, h = DIFF[s]
                dve.wait_ge(tensor_done, T.at(V, ("diff", "S", s)))
                ps = bank(V, ("diff", "S", s))
                dist = cblock[:, t * SEQ:(t + 1) * SEQ].unsqueeze(1).to_broadcast([P, 2, SEQ])
                o = sm2[:, s % 2, :].rearrange("p (c k) -> p c k", c=2)
                stt(o, dist, -DIFF_SLOPES[h] / scale, ps[:, :, 0:SEQ], ALU.mult, ALU.add).then_inc(vector_done, V.step(("read", ("diff", "S", s))))
                dve.wait_ge(vector_done, V.now())
                n = ngm[:, 2 * (s % 2):2 * (s % 2) + 2]
                nc.vector.tensor_reduce(n, o, AX.X, ALU.max, negate=True).then_inc(vector_done, V.step())
                dve.wait_ge(vector_done, V.now())
                ts(n, n, scale, None, ALU.mult).then_inc(vector_done, V.step(("diff", "max", s)))
                dve.wait_ge(vector_done, V.now())

            def diff_out(s):
                dve.wait_ge(scalar_done, A.at(V, ("diff", "exp", s)))
                r = rsum[:, 2 * (s % 2):2 * (s % 2) + 2]
                nc.vector.reciprocal(r2, r).then_inc(vector_done, V.step())
                dve.wait_ge(vector_done, V.now())
                tt(r2[:, 1:2], r2[:, 1:2], lam, ALU.mult).then_inc(vector_done, V.step())
                dve.wait_ge(vector_done, V.now())
                p0, p1 = sm2[:, s % 2, 0:SEQ], sm2[:, s % 2, SEQ:2 * SEQ]
                ts(p1, p1, r2[:, 1:2], None, ALU.mult).then_inc(vector_done, V.step())
                dve.wait_ge(vector_done, V.now())
                if s >= 2:
                    dve.wait_ge(tensor_done, T.at(V, ("diff", "PT", s - 2)))
                stt(at2[:, s % 2, :], p0, r2[:, 0:1], p1, ALU.mult, ALU.subtract).then_inc(vector_done, V.step(("diff", "at", s)))
                dve.wait_ge(vector_done, V.now())

            diff_in(0)
            for s in range(len(DIFF)):
                if s + 1 < len(DIFF):
                    diff_in(s + 1)
                diff_out(s)

            def diff_norm(t):
                dve.wait_ge(tensor_done, T.at(V, ("diff", "PV", (t + 1) * DH - 1)))
                nc.vector.tensor_copy(hn2, bank(V, ("diff", "O", t))[:, 0:DH * HD].rearrange("p (h d) -> p h d", h=DH)).then_inc(vector_done, V.step(("read", ("diff", "O", t))))
                dve.wait_ge(vector_done, V.now())
                tt(sq2, hn2, hn2, ALU.mult).then_inc(vector_done, V.step())
                dve.wait_ge(vector_done, V.now())
                vsum(hv[:, 0:DH], sq2).then_inc(vector_done, V.step())
                dve.wait_ge(vector_done, V.now())
                ts(hv[:, 0:DH], hv[:, 0:DH], 1.0 / HD, RMS_EPS, ALU.mult, ALU.add).then_inc(vector_done, V.step(("diff", "var", t)))
                dve.wait_ge(vector_done, V.now())
                dve.wait_ge(scalar_done, A.at(V, ("diff", "sqrt", t)))
                nc.vector.reciprocal(hs[:, 0:DH], hv[:, 0:DH]).then_inc(vector_done, V.step())
                dve.wait_ge(vector_done, V.now())
                tt(hn2, hn2, over(hs[:, 0:DH], DH, HD), ALU.mult).then_inc(vector_done, V.step())
                dve.wait_ge(vector_done, V.now())
                tt(o_cat[:, t, 0:DH * HD].rearrange("p (h d) -> p h d", h=DH), hn2, subrow.unsqueeze(1).to_broadcast([P, DH, HD]), ALU.mult).then_inc(vector_done, V.step())
                dve.wait_ge(vector_done, V.now())

            diff_norm(0)
            diff_norm(1)

            dve.wait_ge(tensor_done, T.at(V, "mix"))
            ps = bank(V, "mix")
            for g in range(GG):
                stt(o_cat[:, :, 384 + g * HD:384 + (g + 1) * HD], ps[:, g * P:(g + 1) * P].rearrange("p (t d) -> p t d", t=TT), gcols[:, 3 * KT + g:3 * KT + g + 1], buv[:, :, g * HD:(g + 1) * HD], ALU.add, ALU.mult).then_inc(vector_done, V.step(("read", "mix") if g == GG - 1 else None))
                dve.wait_ge(vector_done, V.now())

            wscale = HD ** -0.5
            for s, (t, g) in enumerate(WIN):
                dve.wait_ge(tensor_done, T.at(V, ("win", "S", s)))
                ps = bank(V, ("win", "S", s))
                if s >= 2:
                    dve.wait_ge(tensor_done, T.at(V, ("win", "PT", s - 2)))
                wd = cblock[:, C2["wdist"] + t * SEQ:C2["wdist"] + (t + 1) * SEQ]
                for h in range(2):
                    stt(sm2[:, s % 2, h * SEQ:(h + 1) * SEQ], wd, -SWA_SLOPES[h * WG + g] / wscale, ps[:, h, 0:SEQ], ALU.mult, ALU.add).then_inc(vector_done, V.step(("read", ("win", "S", s)) if h else None))
                    dve.wait_ge(vector_done, V.now())
                vmax(nm2, sm2[:, s % 2, :].rearrange("p (h k) -> p h k", h=2)).then_inc(vector_done, V.step())
                dve.wait_ge(vector_done, V.now())
                sk = sinks[:, g:g + WG + 1:WG]
                stt(msink, nm2, wscale, sk, ALU.mult, ALU.max).then_inc(vector_done, V.step())
                dve.wait_ge(vector_done, V.now())
                c = t * WH + g
                tt(dsum[:, c:c + WG + 1:WG], sk, msink, ALU.subtract).then_inc(vector_done, V.step())
                dve.wait_ge(vector_done, V.now())
                ts(ngm[:, 2 * (s % 2):2 * (s % 2) + 2], msink, -1.0, None, ALU.mult).then_inc(vector_done, V.step(("win", "max", s)))
                dve.wait_ge(vector_done, V.now())

            def win_out(t):
                dve.wait_ge(scalar_done, A.at(V, ("win", "sink", t)))
                tt(rinv[:, 0:WH], dsum[:, t * WH:(t + 1) * WH], rsum[:, t * NA:t * NA + WH], ALU.add).then_inc(vector_done, V.step())
                dve.wait_ge(vector_done, V.now())
                nc.vector.reciprocal(rinv[:, WH:2 * WH], rinv[:, 0:WH]).then_inc(vector_done, V.step())
                dve.wait_ge(vector_done, V.now())
                dve.wait_ge(tensor_done, T.at(V, ("win", "PV", (t + 1) * WG - 1)))
                tt(o_cat[:, t, 640:1024].rearrange("p (h d) -> p h d", h=WH), bank(V, ("win", "O", t))[:, 0:WH * HD].rearrange("p (h d) -> p h d", h=WH), over(rinv[:, WH:2 * WH], WH, HD), ALU.mult).then_inc(vector_done, V.step(("read", ("win", "O", t))))
                dve.wait_ge(vector_done, V.now())

            win_out(0)
            win_out(1)
            V.also("o_cat")
            weights_rest(0, None, ("w_hi", 0), ("parts", 0))
            dve.wait_ge(gains_loaded, gains_count(V))
            post_norm("mix", 0)
            pre_norm("ffn")
            gained("xT2", "hT2", KT)
            input_rest("hT2")
            dve_experts(NF, False)
            dve.wait_ge(vector_done, V.now())
            post_norm("ffn", 1)
            pre_norm("ple")
            gained("xT3", "hT3", 2 * KT)
            for h in range(2):
                for t in range(TT):
                    dve.wait_ge(scalar_done, A.at(V, ("sig", t, h)))
                    o = y2[:, t, h * N:(h + 1) * N]
                    e = (e2 if t == 0 else e2b)[:, h * N:(h + 1) * N]
                    tt(o, o, e, ALU.mult).then_inc(vector_done, V.step("eg" if (h, t) == (1, 1) else None))
                    dve.wait_ge(vector_done, V.now())
            dve.wait_ge(rows_loaded, rows_count(V))
            post_norm("ple", 0)
            V.end()

        @block.vector
        def _(dve):
            nc.vector.memset(ones[:, :], 1.0).then_inc(vector_done, V.step())
            dve.wait_ge(vector_done, V.now())
            nc.vector.memset(zeros[:, :], 0.0).then_inc(vector_done, V.step())
            dve.wait_ge(vector_done, V.now())
            nc.vector.memset(cin, 0.0).then_inc(vector_done, V.step())
            dve.wait_ge(vector_done, V.now())
            nc.vector.memset(mv, 1.0).then_inc(vector_done, V.step())
            dve.wait_ge(vector_done, V.now())
            dve.wait_ge(start_loaded, 16 * 3)
            dve.wait_ge(scalar_done, A.at(V, "sigc"))
            tt(cact[:, :], cact[:, :], psum[:, 0, 0:KT], ALU.mult).then_inc(vector_done, V.step("cact"))
            dve.wait_ge(vector_done, V.now())
            nc.vector.tensor_copy(posf, posi[:, :]).then_inc(vector_done, V.step())
            dve.wait_ge(vector_done, V.now())
            invf = cshared[:, CONST["invf"]:CONST["invf"] + HALF]
            c1 = 6.28125
            c2 = float(np.float32(np.float16(TWO_PI - c1)))
            c3 = TWO_PI - c1 - c2
            for t in range(TT):
                ang, k, r = tmp[:, 0, 0:HALF], tmp[:, 0, HALF:HD], tmp[:, 1, 0:HALF]
                ts(ang, invf, posf[:, t:t + 1], None, ALU.mult).then_inc(vector_done, V.step())
                dve.wait_ge(vector_done, V.now())
                for cos in (0, 1):
                    ts(k, ang, 1.0 / TWO_PI, 0.25 * cos, ALU.mult, ALU.add).then_inc(vector_done, V.step())
                    dve.wait_ge(vector_done, V.now())
                    ts(k, k, ROUND, None, ALU.add).then_inc(vector_done, V.step())
                    dve.wait_ge(vector_done, V.now())
                    ts(k, k, -ROUND, None, ALU.add).then_inc(vector_done, V.step())
                    dve.wait_ge(vector_done, V.now())
                    stt(r, k, -c1, ang, ALU.mult, ALU.add).then_inc(vector_done, V.step())
                    dve.wait_ge(vector_done, V.now())
                    for c in (c2, c3):
                        stt(r, k, -c, r, ALU.mult, ALU.add).then_inc(vector_done, V.step())
                        dve.wait_ge(vector_done, V.now())
                    ts(r, r, np.pi / 2 * cos, None, ALU.add).then_inc(vector_done, V.step())
                    dve.wait_ge(vector_done, V.now())
                    o = (cosf if cos else sinf)[:, t, HALF:HD]
                    ts(o, r, -3.141592, 3.141592, ALU.max, ALU.min).then_inc(vector_done, V.step(("angle", t, cos)))
                    dve.wait_ge(vector_done, V.now())
            dve.wait_ge(scalar_done, A.at(V, "trig"))
            for t in range(TT):
                nc.vector.tensor_copy(cosf[:, t, 0:HALF], cosf[:, t, HALF:HD]).then_inc(vector_done, V.step())
                dve.wait_ge(vector_done, V.now())
                ts(sinf[:, t, 0:HALF], sinf[:, t, HALF:HD], -1.0, None, ALU.mult).then_inc(vector_done, V.step(("rope_tables") if t else None))
                dve.wait_ge(vector_done, V.now())
            with dve.Fori(0, DEPTH) as l:
                dve_first(l)
            with dve.Fori(0, DEPTH) as l:
                dve_second(l)

        def activate(o, a, f, **k):
            return nc.scalar.activation(o, a, f, **k)

        def copy(o, a):
            return nc.scalar.activation(o, a, ACT.Copy)

        def rounded_weights(e, i, more, name):
            act.wait_ge(G.sem(A, f"gu{e}"), G.level(A, f"gu{e}", more))
            w = gslot(A.block, f"gu{e}")
            for q in range(2):
                k = slice(q * KT // 2, (q + 1) * KT // 2)
                copy(w_hi[e % 2][:, k, :], w[:, k, 0:N]).then_inc(scalar_done, A.step(("w_hi", *name, q)))

        def rounded_input(name):
            for g in range(KT // 2):
                act.wait_ge(vector_done, V.at(A, (name, g)))
                copy(h_hi[A.block][:, 2 * g:2 * g + 2, :], hT[:, 2 * g:2 * g + 2, :]).then_inc(scalar_done, A.step((name, "hi", g)))

        def act_experts(ne):
            n = NIT[ne]

            def one(e, i, i0, more, gu0, gu1, step, following):
                act.wait_ge(tensor_done, T.at(A, gu0, i0))
                activate(sact[:, 0, :], psum[:, 0, 0:FE], ACT.Silu).then_inc(scalar_done, A.step(("silu", *step, 0)))
                if following is not None:
                    rounded_weights(e + 1, i, more, following)
                act.wait_ge(DN.sem(A, f"dn{e}"), DN.level(A, f"dn{e}", more))
                copy(d_hi[e % 2], dslot(A.block, f"dn{e}")).then_inc(scalar_done, A.step(("d_hi", *step)))
                act.wait_ge(tensor_done, T.at(A, gu1, i))
                activate(sact[:, 1, :], psum[:, 1, 0:FE], ACT.Silu).then_inc(scalar_done, A.step(("silu", *step, 1)))
                for t in range(TT):
                    act.wait_ge(tensor_done, T.at(A, ("tr", *step, t), i))
                    copy(hidT[:, t, :, :].rearrange("p f n -> p (f n)"), psum[:, 2 + t, 0:FE]).then_inc(scalar_done, A.step(("hidT", *step, t)))

            one(0, None, None, 0, ("gu0", 0), ("gu1", 0), (0,), (1,))
            with nc.scalar.Fori(0, n) as i:
                A.loop(f"act{A.block}", n)
                for j in range(4):
                    gu0, i0 = (("gu0", "loop", j - 1), i) if j else (("gu0", "loop", 3), i - 1)
                    one(1 + j, i, i0, i * 32, gu0, ("gu1", "loop", j), ("loop", j), ("loop", j))
                A.loop_end()
            for e in range(1 + 4 * n, ne):
                gu0, i0 = (("gu0", "loop", 3), n - 1) if e == 1 + 4 * n else (("gu0", e), None)
                one(e, None, i0, 0, gu0, ("gu1", e), (e,), (e + 1,) if e + 1 < ne else None)

        def root_of(name, var, *t):
            act.wait_ge(vector_done, V.at(A, (name, "var", *t)))
            activate(var, var, ACT.Sqrt).then_inc(scalar_done, A.step((name, "sqrt", *t)))
            act.wait_ge(scalar_done, A.now())

        def act_first(l):
            A.begin(0, l)

            def ada_copy(c):
                act.wait_ge(tensor_done, T.at(A, ("ada", c)))
                n = ADA_PAIRS.index(c // 2 * 2)
                if n:
                    act.wait_ge(tensor_done, T.at(A, ("arows_used", ADA_PAIRS[n - 1])))
                copy(arow[c % 2], bank(A, ("ada", c))[0:1, :]).then_inc(scalar_done, A.step(("arow", c)))
                A.also(("read", ("ada", c)))

            for c in (2, 3, 0, 1):
                ada_copy(c)
            act.wait_ge(vector_done, V.before(A))
            act.wait_ge(tensor_done, T.before(A))

            def rows_T(name, dst, blocks):
                for t in range(TT):
                    act.wait_ge(tensor_done, T.at(A, (name, "T", t)))
                    ps = bank(A, (name, "T", t))
                    copy(dst[:, 0:blocks, t * P:(t + 1) * P], ps[:, 0:blocks * P].rearrange("p (b n) -> p b n", b=blocks)).then_inc(scalar_done, A.step((name, "Tc", t)))
                    act.wait_ge(scalar_done, A.now())
                    A.also(("read", (name, "T", t)))

            rows_T("idx", idxT, 3)

            def relu(t):
                nk = (t + 1) * P
                if t:
                    act.wait_ge(vector_done, V.at(A, ("rel_read", t - 1)))
                act.wait_ge(tensor_done, T.at(A, ("idxS", t)))
                ps = bank(A, ("idxS", t))
                for h in range(2):
                    activate(rel[:, 2 * h:2 * h + 2, 0:nk], ps[:, h, :].rearrange("p (i k) -> p i k", i=2)[:, :, 0:nk], ACT.Relu).then_inc(scalar_done, A.step(("rel", t) if h else None))
                    act.wait_ge(scalar_done, A.now())
                A.also(("read", ("idxS", t)))

            def copied(name, dst, t):
                act.wait_ge(tensor_done, T.at(A, (name, t)))
                copy(dst, bank(A, (name, t))[:, 0:N]).then_inc(scalar_done, A.step((name, t)))
                act.wait_ge(scalar_done, A.now())
                A.also(("read", (name, t)))

            def copied_mvo(t):
                act.wait_ge(tensor_done, T.at(A, ("mvo", t)))
                ps = bank(A, ("mvo", t))
                copy(mv[:, t, :, 0:HD], ps[:, 0:256].rearrange("p (h d) -> p h d", h=NR)).then_inc(scalar_done, A.step(("mvo", t)))
                act.wait_ge(scalar_done, A.now())
                copy(mo[:, t, :], ps[:, 256:512]).then_inc(scalar_done, A.step(("read", ("mvo", t))))
                act.wait_ge(scalar_done, A.now())

            def copied_mqk(b):
                act.wait_ge(tensor_done, T.at(A, ("mqk", b)))
                ps = bank(A, ("mqk", b))
                copy(cin[:, 2 * b:2 * b + 2, CONV - 1:CONV - 1 + SEQ], ps.rearrange("p (b n) -> p b n", b=2)).then_inc(scalar_done, A.step(("mqk", "c", b)))
                act.wait_ge(scalar_done, A.now())
                A.also(("read", ("mqk", b)))

            def att_exp(s):
                t, i = ATT[s]
                nk = (t + 1) * P
                act.wait_ge(vector_done, V.at(A, ("att", "max", s)))
                for h in range(2):
                    o = sm[:, s % 2, h * nk:(h + 1) * nk]
                    c = t * NA + 2 * i + h
                    activate(o, o, ACT.Exp, bias=ngm[:, 2 * (s % 2) + h:2 * (s % 2) + h + 1], accum_out=rsum[:, c:c + 1]).then_inc(scalar_done, A.step(("att", "exp", s) if h else None))
                    act.wait_ge(scalar_done, A.now())

            def att_probs_T(s):
                t, i = ATT[s]
                act.wait_ge(tensor_done, T.at(A, ("att", "PT", s)))
                ps = bank(A, ("att", "PT", s))
                if s >= 2:
                    act.wait_ge(tensor_done, T.at(A, ("att", "PV", s - 2)))
                n = 2 * (t + 1) * P
                copy(pT[:, s % 2, 0:n], ps[:, 0:n]).then_inc(scalar_done, A.step(("att", "pT", s)))
                act.wait_ge(scalar_done, A.now())
                A.also(("read", ("att", "PT", s)))

            relu(0)
            rows_T("aq", aqT, 4)
            relu(1)
            for t in range(TT):
                copied("av", av[:, t, :], t)
            rows_T("ak", akT, 4)
            att_exp(0)
            att_exp(1)
            for s in range(len(ATT)):
                if s < 2:
                    copied("rvg", rvg[:, s, :], s)
                if s == 1:
                    rows_T("rqk", rrT, 4)
                if s in (2, 3):
                    copied_mvo(s - 2)
                if s in (4, 5):
                    copied_mqk(s - 4)
                if s == 4:
                    act.wait_ge(vector_done, V.at(A, "negabs"))
                    activate(grow[0:NR, 5, :], grow[0:NR, 5, :], ACT.Exp).then_inc(scalar_done, A.step())
                    act.wait_ge(scalar_done, A.now())
                    activate(grow[0:NR, 5, :], grow[0:NR, 5, :], ACT.Ln, bias=ones[0:NR, 0:1]).then_inc(scalar_done, A.step("softplus"))
                    act.wait_ge(scalar_done, A.now())
                if s >= 6:
                    ada_copy(s - 2)
                att_probs_T(s)
                if s + 2 < len(ATT):
                    att_exp(s + 2)
            act.wait_ge(vector_done, V.at(A, "bm"))
            activate(grow[0:NR, 5, :], grow[0:NR, 4, :], ACT.Exp, scale=-1.0).then_inc(scalar_done, A.step("erow"))
            act.wait_ge(scalar_done, A.now())
            act.wait_ge(vector_done, V.at(A, "conv"))
            activate(qkT, qkT, ACT.Silu).then_inc(scalar_done, A.step("conv"))
            activate(rg, rg, ACT.Silu).then_inc(scalar_done, A.step("rg"))
            activate(mo, mo, ACT.Sigmoid).then_inc(scalar_done, A.step("mo"))
            for h in range(NR):
                act.wait_ge(vector_done, V.at(A, ("ml", "arg", h)))
                activate(wT[:, h % 2, :], wT[:, h % 2, :], ACT.Exp).then_inc(scalar_done, A.step(("ml", "exp", h)))
                act.wait_ge(scalar_done, A.now())
                if h == 1:
                    ada_copy(6)
            root_of("ret", hv)
            ada_copy(7)
            root_of("ml", hv)
            ada_copy(8)
            ada_copy(9)
            for g in range(KT // 2):
                act.wait_ge(tensor_done, T.at(A, ("oT", g)))
                ps = bank(A, ("oT", g))
                copy(hT[:, 2 * g:2 * g + 2, :].rearrange("p f n -> p (f n)"), ps).then_inc(scalar_done, A.step(("oTc", g)))
                act.wait_ge(scalar_done, A.now())
                A.also(("read", ("oT", g)))
            for t in range(TT):
                root_of("ln1", rstd[:, t:t + 1], t)
            ada_copy(10)
            ada_copy(11)
            rounded_weights(0, None, 0, (0,))
            rounded_input("hT2")
            act.wait_ge(tensor_done, T.at(A, "router"))
            ps = psum[:, 3, :]
            activate(scores, ps[:, 0:TT * NE], ACT.Sigmoid).then_inc(scalar_done, A.step("router"))
            act.wait_ge(scalar_done, A.now())
            act_experts(NE)
            act.wait_ge(scalar_done, A.now())
            for t in range(TT):
                root_of("ln2", rstd[:, t:t + 1], t)
            A.end()

        def sum_squares(name, src):
            for t in range(TT):
                activate(junk, src[:, t, :], ACT.Square, accum_out=agg[:, t:t + 1]).then_inc(scalar_done, A.step((name, "ss") if t else None))
                act.wait_ge(scalar_done, A.now())
            root_of(name, rstd[:, 0:TT])

        def act_second(l):
            A.begin(1, l)
            act.wait_ge(vector_done, V.before(A))
            act.wait_ge(tensor_done, T.before(A))
            act.wait_ge(vector_done, V.at(A, "lsum"))
            activate(lsum, lsum, ACT.Exp).then_inc(scalar_done, A.step("lexp"))
            act.wait_ge(scalar_done, A.now())
            sum_squares(("pre", "mix"), x)
            act.wait_ge(tensor_done, T.at(A, "ws"))
            ps = bank(A, "ws")
            copy(wsT.rearrange("p g n -> p (g n)"), ps).then_inc(scalar_done, A.step("wsT"))
            act.wait_ge(scalar_done, A.now())
            A.also(("read", "ws"))
            act.wait_ge(tensor_done, T.at(A, "p"))
            ps = bank(A, "p")
            copy(pTT.rearrange("p k n -> p (k n)"), ps).then_inc(scalar_done, A.step("pT"))
            act.wait_ge(scalar_done, A.now())
            A.also(("read", "p"))

            def features(name, dst, blocks):
                for b in range(0, blocks, 2):
                    n = min(2, blocks - b)
                    act.wait_ge(tensor_done, T.at(A, (name, b // 2)))
                    ps = bank(A, (name, b // 2))
                    copy(dst[:, b:b + n, :].rearrange("p f n -> p (f n)"), ps[:, 0:n * SEQ]).then_inc(scalar_done, A.step((name, "c", b // 2)))
                    act.wait_ge(scalar_done, A.now())
                    A.also(("read", (name, b // 2)))

            def tokens(name, dst):
                for t in range(TT):
                    act.wait_ge(tensor_done, T.at(A, (name, t)))
                    ps = bank(A, (name, t))
                    copy(dst[:, t, :], ps).then_inc(scalar_done, A.step((name, "c", t)))
                    act.wait_ge(scalar_done, A.now())
                    A.also(("read", (name, t)))

            features("aq", qT2, 3)
            features("ak", kT2, 3)
            tokens("avcv", avcv)
            tokens("buv", buv)
            root_of("vn", rstd[:, 0:TT])
            features("cqk", cT2, 4)

            def probs_T(tag, s, n):
                act.wait_ge(tensor_done, T.at(A, (tag, "PT", s)))
                ps = bank(A, (tag, "PT", s))
                if s >= 2:
                    act.wait_ge(tensor_done, T.at(A, (tag, "PV", s - 2)))
                copy(pT2[:, s % 2, 0:n], ps[:, 0:n]).then_inc(scalar_done, A.step((tag, "pT", s)))
                act.wait_ge(scalar_done, A.now())
                A.also(("read", (tag, "PT", s)))

            def diff_exp(s):
                act.wait_ge(vector_done, V.at(A, ("diff", "max", s)))
                for c in range(2):
                    o = sm2[:, s % 2, c * SEQ:(c + 1) * SEQ]
                    k = 2 * (s % 2) + c
                    activate(o, o, ACT.Exp, bias=ngm[:, k:k + 1], scale=DQK ** -0.5, accum_out=rsum[:, k:k + 1]).then_inc(scalar_done, A.step(("diff", "exp", s) if c else None))
                    act.wait_ge(scalar_done, A.now())

            diff_exp(0)
            for s in range(len(DIFF)):
                if s + 1 < len(DIFF):
                    diff_exp(s + 1)
                probs_T("diff", s, SEQ)
            for t in range(TT):
                act.wait_ge(vector_done, V.at(A, ("diff", "var", t)))
                activate(hv[:, 0:DH], hv[:, 0:DH], ACT.Sqrt).then_inc(scalar_done, A.step(("diff", "sqrt", t)))
                act.wait_ge(scalar_done, A.now())
            for s, (t, g) in enumerate(WIN):
                act.wait_ge(vector_done, V.at(A, ("win", "max", s)))
                for h in range(2):
                    o = sm2[:, s % 2, h * SEQ:(h + 1) * SEQ]
                    k, c = 2 * (s % 2) + h, t * NA + h * WG + g
                    activate(o, o, ACT.Exp, bias=ngm[:, k:k + 1], scale=HD ** -0.5, accum_out=rsum[:, c:c + 1]).then_inc(scalar_done, A.step(("win", "exp", s) if h else None))
                    act.wait_ge(scalar_done, A.now())
                if g == WG - 1:
                    d = dsum[:, t * WH:(t + 1) * WH]
                    activate(d, d, ACT.Exp).then_inc(scalar_done, A.step(("win", "sink", t)))
                    act.wait_ge(scalar_done, A.now())
                probs_T("win", s, 2 * SEQ)
            for g in range(KT // 2):
                act.wait_ge(tensor_done, T.at(A, ("oT", g)))
                ps = bank(A, ("oT", g))
                copy(hT[:, 2 * g:2 * g + 2, :].rearrange("p f n -> p (f n)"), ps).then_inc(scalar_done, A.step(("oTc", g)))
                act.wait_ge(scalar_done, A.now())
                A.also(("read", ("oT", g)))
            rounded_weights(0, None, 0, (0,))
            for h in range(2):
                for t in range(TT):
                    act.wait_ge(tensor_done, T.at(A, ("wo", t, h)))
                    ps = bank(A, ("wo", t, h))
                    copy(y2[:, t, h * N:(h + 1) * N], ps).then_inc(scalar_done, A.step(("read", ("wo", t, h))))
                    act.wait_ge(scalar_done, A.now())
            sum_squares(("post", "mix"), y2)
            act.wait_ge(vector_done, V.at(A, ("x", "mix")))
            sum_squares(("pre", "ffn"), x)
            rounded_input("hT2")
            act_experts(NF)
            act.wait_ge(scalar_done, A.now())
            for t in range(TT):
                act.wait_ge(tensor_done, T.at(A, ("dn0", NF - 1) if t == 0 else ("dn1", NF - 1)))
                for h in range(2):
                    copy(y2[:, t, h * N:(h + 1) * N], psum[:, 4 + 2 * t + h, :]).then_inc(scalar_done, A.step(("read", ("acc", 2 * t + h))))
                    act.wait_ge(scalar_done, A.now())
            sum_squares(("post", "ffn"), y2)
            for t in range(TT):
                for h in range(2):
                    act.wait_ge(tensor_done, T.at(A, ("e", t, h)))
                    ps = bank(A, ("e", t, h))
                    copy((e2 if t == 0 else e2b)[:, h * N:(h + 1) * N], ps).then_inc(scalar_done, A.step(("read", ("e", t, h))))
                    act.wait_ge(scalar_done, A.now())
            act.wait_ge(vector_done, V.at(A, ("x", "ffn")))
            sum_squares(("pre", "ple"), x)
            for h in range(2):
                for t in range(TT):
                    act.wait_ge(tensor_done, T.at(A, ("pg", t, h)))
                    ps = bank(A, ("pg", t, h))
                    activate(y2[:, t, h * N:(h + 1) * N], ps, ACT.Sigmoid).then_inc(scalar_done, A.step(("sig", t, h)))
                    act.wait_ge(scalar_done, A.now())
                    A.also(("read", ("pg", t, h)))
            act.wait_ge(vector_done, V.at(A, "eg"))
            sum_squares(("post", "ple"), y2)
            A.end()

        @block.scalar
        def _(a):
            for dst, src in ((cblock[:, :], ins["c_first"]), (crows[:, :, :], ins["c_rows"]),
                             (wr[:, :, :], by_row(ins["w_router"])), (br[:, :], ins["b_router"].partition_broadcast(P))):
                nc.scalar.dma_start(dst, src).then_inc(tables_loaded, 16)
            act.wait_ge(tensor_done, T.at(A, "c"))
            activate(cact[:, :], psum[:, 0, 0:KT], ACT.Sigmoid).then_inc(scalar_done, A.step("sigc"))
            act.wait_ge(scalar_done, A.now())
            for t in range(TT):
                for cos in (0, 1):
                    o = (cosf if cos else sinf)[:, t, HALF:HD]
                    act.wait_ge(vector_done, V.at(A, ("angle", t, cos)))
                    activate(o, o, ACT.Sin).then_inc(scalar_done, A.step("trig" if (t, cos) == (TT - 1, 1) else None))
                    act.wait_ge(scalar_done, A.now())
            with a.Fori(0, DEPTH) as l:
                act_first(l)
            with a.Fori(0, DEPTH) as l:
                act_second(l)

        def load(dst, src, s):
            nc.sync.dma_start(dst, src).then_inc(s, 16)

        def experts_load(ne, gu_src, dn_src, freed_g, freed_d, then=lambda: None):
            n = NIT[ne]
            b = S.block

            def one(e, number, wait_g, wait_d):
                if wait_g is not None:
                    sp.wait_ge(wait_g[0].sem, wait_g[0].at(S, *wait_g[1:]))
                gate_w, up_w = gu_src(number)
                g = gslot(b, f"gu{e}")
                s = g_landed[G.slot[b, f"gu{e}"]]
                load(g[:, :, 0:FE], gate_w, s)
                load(g[:, :, FE:2 * FE], up_w, s)
                if wait_d is not None:
                    sp.wait_ge(wait_d[0].sem, wait_d[0].at(S, *wait_d[1:]))
                load(dslot(b, f"dn{e}"), dn_src(number), d_landed[DN.slot[b, f"dn{e}"]])

            def used_g(e):
                if e == 0:
                    return (T, ("gu1", 0))
                i, j = divmod(e - 1, 4)
                return (T, ("gu1", "loop", j), i) if i < n else (T, ("gu1", e))

            def used_d(e):
                i, j = divmod(e, 4)
                return (T, ("dn1", "loop", j), i) if i < n else (T, ("dn1", e))

            for e in range(5):
                if e == 4:
                    then()
                one(e, e, freed_g(e) if e < 4 else used_g(e - 4), freed_d(e) if e < 2 else used_d(e - 2))
            with nc.sync.Fori(0, n - 1) as i:
                for j in range(4):
                    e = 5 + j
                    one(e, i * 4 + e, (T, ("gu1", "loop", j), i),
                        (T, ("dn1", "loop", 3), i) if j == 0 else (T, ("dn1", "loop", j - 1), i + 1))
            for e in range(1 + 4 * n, ne):
                one(e, e, used_g(e - 4), used_d(e - 2))

        def used_first(name):
            if name.startswith("ada"):
                return (T, ("ada", int(name[3:])))
            if name == "mqk":
                return (T, ("mqk", 1))
            if name == "mvo":
                return (T, "gates")
            if name.startswith("wo"):
                return (T, ("wo", 1, int(name[2:])))
            return (T, (name, 1))

        def used_second(name):
            if name in ("aq", "ak", "cqk", "avcv", "buv"):
                return (T, (name, 1))
            if name.startswith("wo"):
                return (T, ("wo", 1, int(name[2:])))
            e = int(name[2:])
            n = NIT[NF]
            if e == 0:
                return (T, ("gu1", 0))
            i, j = divmod(e - 1, 4)
            return (T, ("gu1", "loop", j), i) if i < n else (T, ("gu1", e))

        def free_slot(b, name):
            c = ORDER[b].index(name)
            if c >= GS:
                sp.wait_ge((used_second if b else used_first)(ORDER[b][c - GS])[0].sem, (used_second if b else used_first)(ORDER[b][c - GS])[0].at(S, *(used_second if b else used_first)(ORDER[b][c - GS])[1:]))
                sp.sem_inc(waited)

        def sp_first(l):
            S.begin(0, l)
            w = layer("w_ada", l)

            def load_ada(c):
                if c >= 4:
                    free_slot(0, f"ada{c}")
                load(gslot(0, f"ada{c}")[:, :, 0:N], by_row(w[:, c * N:(c + 1) * N]), g_landed[G.slot[0, f"ada{c}"]])

            sp.wait_ge(tensor_done, T.last_pass(S, ("gu1", "loop", (NE - 5) % 4), NIT[NE] - 1))
            sp.sem_inc(waited)
            load(brow[0:ADA, :], layer("b_ada", l).rearrange("(c n) -> c n", n=N), bias_loaded)
            load_ada(2)
            for c, e in ((3, NE - 3), (0, NE - 2), (1, NE - 1)):
                sp.wait_ge(tensor_done, T.last_pass(S, ("gu1", e)))
                sp.sem_inc(waited)
                load_ada(c)
            load(ibias[0:NR], layer("i_bias", l).rearrange("(h a) -> h a", a=1), params_loaded)
            load(fbias[0:NR], layer("f_bias", l).rearrange("(h a) -> h a", a=1), params_loaded)
            cw = layer("conv_w", l).rearrange("j (b p) -> p b j", p=P)
            with nc.allow_non_contiguous_dma("one column of taps per channel"):
                for b in range(4):
                    load(convw[:, b, 0:CONV], cw[:, b, :], params_loaded)
                load(convw[:, :, CONV:CONV + 1], layer("conv_b", l).rearrange("(b p a) -> p b a", p=P, a=1), params_loaded)
            wi = layer("w_in", l)
            for name, (c0, c1) in CHUNKS1.items():
                free_slot(0, name)
                load(gslot(0, name)[:, :, 0:c1 - c0], by_row(wi[:, c0:c1]), g_landed[G.slot[0, name]])
            sp.wait_ge(vector_done, V.before(S))
            sp.sem_inc(waited)
            load(rows[:, 0, :], layer("ln_mix_g", l).partition_broadcast(P), gains_loaded)
            load(rows[:, 1, :], layer("ln_mix_b", l).partition_broadcast(P), gains_loaded)
            for c in range(4, 10):
                load_ada(c)
            wo = layer("w_out", l)
            for h in range(2):
                free_slot(0, f"wo{h}")
                load(gslot(0, f"wo{h}")[:, :, 0:N], by_row(wo[:, h * N:(h + 1) * N]), g_landed[G.slot[0, f"wo{h}"]])
            for c in range(10, ADA):
                load_ada(c)

            def gain_rows():
                sp.wait_ge(vector_done, V.at(S, "ln1"))
                sp.sem_inc(waited)
                load(rows[:, 0, :], layer("ln_ffn_g", l).partition_broadcast(P), rows_loaded)
                load(rows[:, 1, :], layer("ln_ffn_b", l).partition_broadcast(P), rows_loaded)

            def expert(name, e):
                a = ins[name][bass.ds(l, 1), bass.ds(e, 1)]
                return by_row(a.rearrange("a b c d -> (a b c) d"))

            experts_load(NE, lambda e: (expert("w_gate", e), expert("w_up", e)), lambda e: expert("w_down", e),
                         lambda e: used_first(ORDER[0][ORDER[0].index(f"gu{e}") - GS]), lambda e: None, gain_rows)
            S.end()

        def sp_second(l):
            S.begin(1, l)
            sp.wait_ge(tensor_done, T.before(S))
            sp.wait_ge(vector_done, V.before(S))
            sp.wait_ge(scalar_done, A.before(S))
            for n, name in enumerate(("g_pre_mix_2", "g_pre_ffn_2", "g_ple_gate_2")):
                load(grows[KT * n:KT * (n + 1), :], layer(name, l).rearrange("(k p) -> k p", p=P), params_loaded)
            load(grows[3 * KT:3 * KT + GG, :], layer("b_spatial_2", l), params_loaded)
            for n, name in enumerate(("lam_q1_2", "lam_q2_2", "lam_k1_2", "lam_k2_2")):
                load(lamrow[:, n, :], layer(name, l).partition_broadcast(P), params_loaded)
            load(lamc, layer("c_lam", l).partition_broadcast(P), params_loaded)
            load(subrow, layer("g_diff_sub_2", l).partition_broadcast(P), params_loaded)
            load(wsp, layer("w_spatial_2", l).rearrange("g t s -> t g s"), params_loaded)
            load(prow, token_major(layer("p_2", l).rearrange("a b c -> (a b) c")), params_loaded)
            load(rows[:, 0, :], layer("g_post_mix_2", l).partition_broadcast(P), gains_loaded)
            load(rows[:, 1, :], layer("g_post_ffn_2", l).partition_broadcast(P), gains_loaded)
            load(glnrow[:, 0, :], layer("gmlp_ln_g_2", l).partition_broadcast(P), params_loaded)
            load(glnrow[:, 1, :], layer("gmlp_ln_b_2", l).partition_broadcast(P), params_loaded)
            load(sinks, layer("swa_sinks_2", l).partition_broadcast(P), params_loaded)
            wi = layer("w_in_2", l)

            def load_g(name, parts):
                free_slot(1, name)
                for a, c0, n in parts:
                    load(gslot(1, name)[:, :, a:a + n], by_row(wi[:, c0:c0 + n]), g_landed[G.slot[1, name]])

            load_g("aq", [(0, 0, 384)])
            load_g("ak", [(0, 384, 384)])
            load_g("avcv", [(0, 768, 384), (384, IN2 - P, P)])
            load_g("buv", [(0, 1152, 512)])
            free_slot(1, "cqk")
            cq = gslot(1, "cqk")
            for g in range(WG):
                for h in range(2):
                    c0 = 1664 + (h * WG + g) * HD
                    load(cq[:, :, (2 * g + h) * HD:(2 * g + h + 1) * HD], by_row(wi[:, c0:c0 + HD]), g_landed[G.slot[1, "cqk"]])
            load(cq[:, :, 384:512], by_row(wi[:, 2048:2176]), g_landed[G.slot[1, "cqk"]])
            wo = layer("w_out_2", l)
            for h in range(2):
                free_slot(1, f"wo{h}")
                load(gslot(1, f"wo{h}")[:, :, 0:N], by_row(wo[:, h * N:(h + 1) * N]), g_landed[G.slot[1, f"wo{h}"]])
            wf, wd = layer("w_ffn_in_2", l), layer("w_ffn_out_2", l)

            def ffn(e):
                if isinstance(e, int):
                    return by_row(wf[:, e * FE:(e + 1) * FE]), by_row(wf[:, DFF + e * FE:DFF + (e + 1) * FE])
                return by_row(wf[:, bass.ds(e * FE, FE)]), by_row(wf[:, bass.ds(e * FE + DFF, FE)])

            def ffn_out(e):
                return by_row(wd[e * FE:(e + 1) * FE, :] if isinstance(e, int) else wd[bass.ds(e * FE, FE), :])

            experts_load(NF, ffn, ffn_out, lambda e: used_second(ORDER[1][ORDER[1].index(f"gu{e}") - GS]), lambda e: None)
            sp.wait_ge(tensor_done, T.at(S, ("dn1", NF - 2)))
            load(dslot(1, "up"), by_row(layer("w_ple_up_2", l)), d_landed[DN.slot[1, "up"]])
            wg = layer("w_ple_gate_2", l)
            for h in range(2):
                free_slot(1, f"pg{h}")
                load(gslot(1, f"pg{h}")[:, :, 0:N], by_row(wg[:, h * N:(h + 1) * N]), g_landed[G.slot[1, f"pg{h}"]])
            sp.wait_ge(vector_done, V.at(S, ("x", "mix")))
            load(rows[:, 0, :], layer("g_ple_post_2", l).partition_broadcast(P), rows_loaded)
            S.end()

        @block.sync
        def _(sp):
            load(c8, ins["c"].rearrange("a (k p) -> (a k) p", p=P), start_loaded)
            load(cshared[:, :], ins["c_shared"], start_loaded)
            with nc.allow_non_contiguous_dma("one position per partition"):
                load(posi[:, :], ins["positions"].rearrange("a (t p) -> p (a t)", p=P), start_loaded)
            load(x[:, :, :], token_major(ins["x"].rearrange("a b c -> (a b) c")), x_loaded)
            with sp.Fori(0, DEPTH) as l:
                sp_first(l)
            sp.wait_ge(vector_done, V.base(1))
            load(cblock[:, 0:C2_W], ins["c_second"], const_loaded)
            with sp.Fori(0, DEPTH) as l:
                sp_second(l)
            sp.wait_ge(vector_done, V.total())
            sp.dma_start(token_major(out), x[:, :, :]).then_inc(stored, 16)
            sp.wait_ge(stored, 16)

    return {"T": T.counted(), "V": V.counted(), "A": A.counted()}


_INS = ["x", "c", "positions", "w_ada", "b_ada", "w_in", "i_bias", "f_bias", "conv_w", "conv_b", "w_out", "ln_mix_g",
        "ln_mix_b", "w_router", "b_router", "w_gate", "w_up", "w_down", "ln_ffn_g", "ln_ffn_b", "p_2", "g_pre_mix_2",
        "w_in_2", "lam_q1_2", "lam_k1_2", "lam_q2_2", "lam_k2_2", "g_diff_sub_2", "gmlp_ln_g_2", "gmlp_ln_b_2",
        "w_spatial_2", "b_spatial_2", "swa_sinks_2", "w_out_2", "g_post_mix_2", "g_pre_ffn_2", "w_ffn_in_2",
        "w_ffn_out_2", "g_post_ffn_2", "w_ple_up_2", "w_ple_gate_2", "g_ple_gate_2", "g_ple_post_2"]


def kernel(**inputs):
    import concourse.bacc as _bacc
    from concourse.bass_utils import run_bass_kernel_spmd as _run

    arrays = {f"in_{n}": np.ascontiguousarray(inputs[n]) for n in _INS}
    arrays |= {f"in_{n}": a for n, a in constants().items()}

    def build(known):
        nc = _bacc.Bacc("TRN2", target_bir_lowering=False, num_devices=1)
        ins = {n[3:]: nc.dram_tensor(n, a.shape, mybir.dt.from_np(a.dtype), kind="ExternalInput").ap()
               for n, a in arrays.items()}
        out = nc.dram_tensor("out_x", (SEQ, D), F32, kind="ExternalOutput").ap()
        return nc, program(nc, ins, out, known)

    _, known = build(None)
    nc, _ = build(known)
    r = _run(nc, [arrays], core_ids=[0])
    return r.results[0]["out_x"].reshape(1, SEQ, D)
```

```python
from contextlib import ExitStack

import concourse.bass as bass
from concourse import mybir
import numpy as np

F32 = mybir.dt.float32
F32R = mybir.dt.float32r
I32 = mybir.dt.int32
ALU = mybir.AluOpType
ACT = mybir.ActivationFunctionType
AX = mybir.AxisListType

P = 128
D = 1024
SEQ = 256
TT = SEQ // P
KT = D // P
DEPTH = 2
HD = 64
HALF = HD // 2
N = 512
BIG = 1.0e30
TAKEN = -3.0e38
TOPK = min(256, SEQ // 4)
LN_EPS = 1e-5
RMS_EPS = 1e-6
ALPHA = (2.0 * DEPTH) ** 0.25
TWO_PI = 2.0 * np.pi
ROUND = 12582912.0

AQ, AK, AV, IQ, IK, IW, RQ, RK, RV, RG, MQ, MK, MV, MO, MI, MF = (
    0, 512, 1024, 1536, 1792, 1856, 1860, 2116, 2372, 2628, 2884, 3140, 3396, 3652, 3908, 3912)
IN1 = 3916
CHUNKS1 = {"idx": (IQ, RQ), "aq": (AQ, AK), "ak": (AK, AV), "av": (AV, IQ), "rqk": (RQ, RV),
           "rvg": (RV, MQ), "mvo": (MV, IN1), "mqk": (MQ, MV)}
NA = 8
NI = 4
NR = 4
NE = 16
NG = 4
EG = NE // NG
FE = 256
ADA = 6 * D // N
CONV = 4
DH = 6
DQK = 32
GG = 4
GW = 256
WH = 6
WG = 3
DFF = 2816
NF = DFF // FE
PLE = 256
IN2 = 2304
SLOPES = [2.0 ** (-8.0 * k / (DH + WH)) for k in range(1, DH + WH + 1)]
DIFF_SLOPES, SWA_SLOPES = SLOPES[WH:], SLOPES[:WH]

GS = 4
GW_MAX = 520
ARENA = 15400
SMALL = 640
DS = 2
ORDER = (
    "ada0 ada1 ada2 ada3 idx aq ada4 ak ada5 av rqk ada6 rvg ada7 mvo ada8 mqk ada9 wo0 wo1 ada10 ada11".split()
    + [f"gu{e}" for e in range(NE)],
    ["aq", "ak", "avcv", "buv", "cqk", "wo0", "wo1"] + [f"gu{e}" for e in range(NF)] + ["pg0", "pg1"],
)
ORDER_D = ([f"dn{e}" for e in range(NE)], [f"dn{e}" for e in range(NF)] + ["up"])
DMAS = ({f"ada{c}": 1 for c in range(ADA)} | {f"gu{e}": 2 for e in range(NE)},
        {f"gu{e}": 2 for e in range(NF)} | {"avcv": 2, "cqk": 7})
ROWS = (2, 1)
GAINS = (2, 2)
PARAMS = (7, 15)
ADA_PAIRS = (2, 0, 4, 6, 8, 10)
GATES = (4, 5, 10, 11)
AHEAD = 32

CONST = {}
_at = 0
for _name, _w in (("ident", P), ("invf", HALF), ("first4", NG), ("first16", NE), ("shared", 0)):
    CONST[_name] = _at
    _at += _w
C_SHARED = _at
C1 = {"decay": 0, "causal": NR * 384, "vis": NR * 384 + 256}
C1_W = NR * 384 + 256 + TT * SEQ
C2 = {"dist": 0, "wdist": TT * SEQ}
C2_W = 2 * TT * SEQ


def constants():
    p = np.arange(P)[:, None]
    j = np.arange(SEQ)[None, :]
    shared = np.zeros((P, C_SHARED), np.float32)
    shared[:, CONST["ident"]:CONST["ident"] + P] = np.eye(P)
    shared[:, CONST["invf"]:CONST["invf"] + HALF] = np.float32(10000.0) ** (
        -np.arange(HALF, dtype=np.float32) / np.float32(HALF))
    shared[:, CONST["first4"]:CONST["first4"] + NG] = np.arange(NG, 0, -1)
    shared[:, CONST["first16"]:CONST["first16"] + NE] = np.arange(NE, 0, -1)
    c1 = np.zeros((P, C1_W), np.float32)
    for h in range(NR):
        log_gamma = np.log1p(-(2.0 ** (-5.0 - h)))
        decay = np.where(j >= p, np.exp(np.maximum(j - p, 0) * log_gamma), 0.0) * HD ** -0.5
        c1[:, h * 384:h * 384 + 256] = decay
        c1[:, h * 384 + 256:h * 384 + 384] = decay[:, :P]
    c1[:, C1["causal"]:C1["causal"] + SEQ] = np.where(j >= p, 0.0, -BIG)
    c2 = np.zeros((P, C2_W), np.float32)
    for t in range(TT):
        q = t * P + p
        c1[:, C1["vis"] + t * SEQ:C1["vis"] + (t + 1) * SEQ] = np.where(j < (q // 64 + 1) * 64, 0.0, -BIG)
        dist = np.abs(q - j)
        c2[:, t * SEQ:(t + 1) * SEQ] = dist
        c2[:, C2["wdist"] + t * SEQ:C2["wdist"] + (t + 1) * SEQ] = np.where(dist <= 128, dist, BIG)
    rows = np.zeros((ADA, 8, P), np.float32)
    for n, c in enumerate(GATES):
        rows[c, NR + n, :] = 1.0
    for h in range(NR):
        rows[h, h, :] = -1.0
    lam = np.array([[0.8 - 0.6 * np.exp(-0.3 * l), 0.2 + 0.6 * np.exp(-0.3 * l)] for l in range(DEPTH)], np.float32)
    return {"c_shared": shared, "c_first": c1, "c_second": c2, "c_rows": rows, "c_lam": lam}


class Done:

    def __init__(self, sem, known):
        self.sem, self.known = sem, known
        self.block, self.l, self.n = None, None, 0
        self.marks, self.per, self.stride, self.first = {}, [0, 0], {}, 0
        self.inner, self.inner_n, self.inner_from = None, 0, 0

    def begin(self, block, l):
        if block == 0:
            self.first = self.n
        self.block, self.l, self.n = block, l, 0

    def end(self):
        self.per[self.block] = self.n

    def loop(self, name, n):
        self.inner, self.inner_n, self.inner_from = name, n, self.n

    def loop_end(self):
        step = self.n - self.inner_from
        self.stride[self.inner] = step
        self.n = self.inner_from + step * self.inner_n
        self.inner = None

    def step(self, name=None, by=1):
        self.n += by
        if name is not None:
            self.also(name)
        return by

    def also(self, name):
        assert (self.block, name) not in self.marks, name
        self.marks[self.block, name] = (self.n, self.inner)

    def base(self, block):
        k = self.known
        return k["first"] + (DEPTH * k["per"][0] if block else 0) if k else 1

    def before(self, by):
        return by.l * self.known["per"][by.block] + self.base(by.block) if self.known else 1

    def last_pass(self, by, name, i=None):
        if not self.known:
            return 1
        n, inner = self.known["marks"][0, name]
        n += i * self.known["stride"][inner] if inner else 0
        return by.l * self.known["per"][by.block] + (self.base(by.block) + n - self.known["per"][0])

    def at_last(self, name):
        return self.base(1) + (self.known["marks"][0, name][0] - self.known["per"][0]) if self.known else 1

    def now(self):
        if self.block is None:
            return self.n
        return self.l * self.known["per"][self.block] + (self.base(self.block) + self.n) if self.known else 1

    def total(self):
        return self.base(1) + DEPTH * self.known["per"][1] if self.known else 1

    def at(self, by, name, i=None):
        if not self.known:
            return 1
        n, inner = self.known["marks"][by.block, name]
        if by.block is None:
            return n
        v = by.l * self.known["per"][by.block] + (self.base(by.block) + n)
        return v if inner is None else v + i * self.known["stride"][inner]

    def counted(self):
        return {"marks": self.marks, "per": self.per, "stride": self.stride, "first": self.first}


class Ring:

    def __init__(self, sems, slots, orders, dmas):
        self.sems, self.slot, self.count, self.per = sems, {}, {}, []
        for b, order in enumerate(orders):
            total = [0] * slots
            for c, name in enumerate(order):
                s = c % slots
                total[s] += 16 * dmas[b].get(name, 1)
                self.slot[b, name], self.count[b, name] = s, total[s]
            self.per.append(total)

    def sem(self, by, name):
        return self.sems[self.slot[by.block, name]]

    def level(self, by, name, more=0):
        b, s = by.block, self.slot[by.block, name]
        first = DEPTH * self.per[0][s] if b else 0
        return by.l * self.per[b][s] + (first + self.count[b, name]) + more


def program(nc, ins, out, known):
    ctx = ExitStack()
    with ctx:
        def sb(name, shape, dt=F32):
            return ctx.enter_context(nc.sbuf_tensor(name, shape, dt))

        def sb_parts(name, shape):
            with nc.sbuf_tensor(name, shape, F32) as whole:
                pass
            return whole, ctx.enter_context(nc.sbuf_tensor(f"{name}_parts", shape, F32R))

        def sem(name):
            return ctx.enter_context(nc.semaphore(name))

        pe, dve, act, sp = nc.tensor, nc.vector, nc.scalar, nc.sync

        gring, gring_rest = sb_parts("gring", [P, GS, KT, GW_MAX])
        dring, dring_rest = sb_parts("dring", [P, DS, FE // P, D])
        x = sb("x", [P, TT, D])
        hT, hT_parts = sb_parts("hT", [P, KT, SEQ])
        o_cat, o_cat_parts = sb_parts("o_cat", [P, TT, D])
        cshared = sb("cshared", [P, C_SHARED])
        cblock = sb("cblock", [P, C1_W])
        crows = sb("crows", [ADA, 8, P])
        rows = sb("rows", [P, 2, D])
        gb = sb("gb", [P, D])
        ones = sb("ones", [P, SEQ])
        zeros = sb("zeros", [P, P])
        cosf = sb("cosf", [P, TT, HD])
        sinf = sb("sinf", [P, TT, HD])
        cact = sb("cact", [P, KT])
        wr = sb("wr", [P, KT, NE])
        br = sb("br", [P, NE])
        ex, ex_parts = sb_parts("ex", [P, 3, TT * FE])
        sact = ex[:, 0, :].rearrange("p (t f) -> p t f", t=TT)
        hid = ex[:, 1, :].rearrange("p (t f) -> p t f", t=TT)
        hidT = ex_parts[:, 2, :].rearrange("p (t f n) -> p t f n", t=TT, f=FE // P)
        small = sb("small", [P, SMALL])
        tmp = sb("tmp", [P, 2, N])
        arena, arena_parts = sb_parts("arena", [P, ARENA])
        ident = cshared[:, 0:P]

        used = [0]

        def restart():
            used[0] = 0

        def buf(*shape, of=arena):
            size = int(np.prod(shape))
            a = of[:, used[0]:used[0] + size]
            used[0] += size
            assert used[0] <= ARENA, used[0]
            if len(shape) == 2:
                a = a.rearrange("p (a b) -> p a b", a=shape[0])
            elif len(shape) == 3:
                a = a.rearrange("p (a b c) -> p a b c", a=shape[0], b=shape[1])
            return a

        s_used = [0]

        def sc(n):
            a = small[:, s_used[0]:s_used[0] + n]
            s_used[0] += n
            assert s_used[0] <= SMALL
            return a

        psum = ctx.enter_context(nc.psum_tensor("psum", [P, 8, N], F32))

        tensor_done, vector_done, scalar_done = sem("tensor_done"), sem("vector_done"), sem("scalar_done")
        g_landed = [sem(f"g_landed{i}") for i in range(GS)]
        d_landed = [sem(f"d_landed{i}") for i in range(DS)]
        start_loaded, x_loaded, tables_loaded = sem("start_loaded"), sem("x_loaded"), sem("tables_loaded")
        bias_loaded, params_loaded = sem("bias_loaded"), sem("params_loaded")
        gains_loaded, rows_loaded = sem("gains_loaded"), sem("rows_loaded")
        const_loaded, stored, waited = sem("const_loaded"), sem("stored"), sem("waited")

        known = known or {}
        T = Done(tensor_done, known.get("T"))
        V = Done(vector_done, known.get("V"))
        A = Done(scalar_done, known.get("A"))
        S = Done(None, known.get("S"))
        G = Ring(g_landed, GS, ORDER, DMAS)
        DN = Ring(d_landed, DS, ORDER_D, ({}, {}))

        def gslot(block, name):
            return gring[:, G.slot[block, name]]

        def dslot(block, name):
            return dring[:, DN.slot[block, name]]

        def g_rest(block, name):
            return gring_rest[:, G.slot[block, name]]

        def d_rest(block, name):
            return dring_rest[:, DN.slot[block, name]]

        def params_count(by):
            b = by.block
            return by.l * (16 * PARAMS[b]) + (16 * PARAMS[b] + (DEPTH * 16 * PARAMS[0] if b else 0))

        def bias_count(by):
            return by.l * 16 + 16

        def gains_count(by):
            b = by.block
            return by.l * (16 * GAINS[b]) + (16 * GAINS[b] + (DEPTH * 16 * GAINS[0] if b else 0))

        def rows_count(by):
            b = by.block
            return by.l * (16 * ROWS[b]) + (16 * ROWS[b] + (DEPTH * 16 * ROWS[0] if b else 0))

        bank_of, on_bank = {}, {}
        turn = [0]

        def take(name, reader, bank=None, pair=False):
            if bank is None:
                bank = turn[0] + (turn[0] % 2 if pair else 0)
                bank %= 6
                turn[0] = (bank + (2 if pair else 1)) % 6
            banks = (bank, bank + 1) if pair else (bank,)
            for last in dict.fromkeys(on_bank[b] for b in banks if b in on_bank):
                pe.wait_ge(last[0].sem, last[0].at(T, *last[1:]))
                if pair:
                    pe.sem_inc(waited)
            for b in banks:
                on_bank[b] = (reader, ("read", name))
            bank_of[T.block, name] = (bank, pair)
            return psum[:, bank:bank + 2, :] if pair else psum[:, bank, :]

        def bank(E, name):
            b, pair = bank_of[E.block, name]
            return psum[:, b:b + 2, :] if pair else psum[:, b, :]

        roped = buf(3, N)
        idxT, aqT, akT, rrT = buf(3, SEQ), buf(4, SEQ), buf(4, SEQ), buf(4, SEQ)
        av, rvg = buf(TT, N), buf(TT, N)
        rv, rg = rvg[:, :, 0:256], rvg[:, :, 256:512]
        qkT, mo = buf(4, SEQ), buf(TT, 256)
        rel, bias = buf(NI, SEQ), buf(TT, SEQ)
        score = buf(SEQ)
        sm, pT = buf(2, N), buf(2, N)
        tail = used[0]
        cin, mv = buf(4, SEQ + CONV - 1), buf(TT, NR, HD + 1)
        brow = buf(N)
        arow = [sm[0:1, n, :] for n in range(2)]
        acc = tmp
        convw = buf(4, CONV + 1)
        sT = roped.rearrange("p a n -> p (a n)")[:, 0:768].rearrange("p (a n) -> p a n", a=2)
        wT = roped.rearrange("p a n -> p (a n)")[:, 768:1536].rearrange("p (a n) -> p a n", a=2)
        rel2 = rel.rearrange("p (a b) n -> p a (b n)", a=2)
        hn = rel.rearrange("p a n -> p (a n)")[:, 0:N].rearrange("p (h d) -> p h d", h=8)
        sq = rel.rearrange("p a n -> p (a n)")[:, N:2 * N].rearrange("p (h d) -> p h d", h=8)
        grow = ex.rearrange("p a n -> p (a n)").rearrange("p (r n) -> p r n", r=6)
        restart()
        prow, wsp = buf(TT, PLE), buf(GG, P)
        grows, glnrow, subrow = buf(P), buf(2, GW), buf(HD)
        lamrow = buf(4, DQK)
        e2, e2b = gb[:, :], arena[:, used[0]:used[0] + D]
        qT2, kT2, at2 = buf(3, SEQ), buf(3, SEQ), buf(2, SEQ)
        cT2 = buf(4, SEQ)
        avcv, buv, vn, wsT = buf(TT, N), buf(TT, N), buf(TT, GW), buf(GG, P)
        pT2 = buf(2, N)
        hn2, sq2 = buf(TT * DH, HD), buf(TT * DH, HD)
        sm2 = buf(3, N)
        junk = sm2[:, 0:2, :].rearrange("p a n -> p (a n)")
        restart()
        w_hi = [buf(KT, N, of=arena_parts) for _ in range(2)]
        d_hi = [buf(FE // P, D, of=arena_parts) for _ in range(2)]
        hidT_lo = buf(TT, FE // P, P, of=arena_parts)
        assert used[0] <= tail, (used[0], tail)
        used[0] = tail
        y2, pTT = buf(TT, D), buf(PLE // P, SEQ)
        used[0] = tail
        h_hi = (o_cat_parts[:, :, :].rearrange("p t n -> p (t n)").rearrange("p (k n) -> p k n", k=KT),
                buf(KT, SEQ, of=arena_parts))
        h_lo = hT_parts

        mod = [sc(KT) for _ in range(4)]
        iw, ngm, rsum = sc(TT * NI), sc(3 * 2), sc(TT * NA)
        rinv, top8 = sc(TT * NA), sc(8)
        st, agg, rstd = sc(12), sc(2 * TT), sc(2 * TT)
        hs, hv = sc(8), sc(8)
        hs2, hv2 = sc(TT * DH), sc(TT * DH)
        gcol, den = sc(16), sc(NR)
        ibias, fbias = sc(1), sc(1)
        scores, biased, bmask, onehot, sel, gate = (sc(TT * NE) for _ in range(6))
        pairs, gsum, key4, t2 = sc(8 * 6), sc(8), sc(8), sc(TT)
        posf = sc(TT)
        gcols = sc(3 * KT + GG)
        lamc, lam, lsum = sc(2), sc(1), sc(2)
        r2, nm2, sinks, msink, dsum = sc(2), sc(2), sc(WH), sc(2), sc(TT * WH)
        lprod = sc(2 * DQK)
        c8 = ex[0:KT, 0, 0:P]
        posi = sb("posi", [P, TT], I32)

        block = ctx.enter_context(nc.Block())

        def token_major(ap):
            return ap.rearrange("(t p) n -> p t n", p=P)

        def by_row(ap):
            return ap.rearrange("(k p) n -> p k n", p=P)

        def layer(name, l):
            a = ins[name][bass.ds(l, 1)]
            return a.rearrange("a b c d -> (a b) c d") if len(a.shape) == 4 else a.rearrange(
                "a b c -> (a b) c") if len(a.shape) == 3 else a.rearrange("a b -> (a b)")

        NIT = {NE: (NE - 2) // 4, NF: (NF - 2) // 4}

        def transposed_x(tag, src, reader, gs=range(KT // 2), ready=None):
            banks = {}
            for g in gs:
                banks[g] = take((tag, g), (V, A)[g % 2] if reader is None else reader)
                pe.sem_inc(waited)
            for t in range(TT):
                if ready is not None:
                    pe.wait_ge(vector_done, V.at(T, ready(t)))
                for g in gs:
                    for f in (2 * g, 2 * g + 1):
                        last = nc.tensor.transpose(banks[g][:, (f % 2) * SEQ + t * P:(f % 2) * SEQ + (t + 1) * P],
                                                   src[:, t, f * P:(f + 1) * P], ident)
                    if t == TT - 1:
                        last.then_inc(tensor_done, T.step((tag, g)))

        def token_product(ps, t, w, n, ks=range(KT)):
            for k in ks:
                last = nc.tensor.matmul(ps[:, 0:n], hT[:, k, t * P:(t + 1) * P], w[:, k, 0:n],
                                        start=k == 0, stop=k == KT - 1)
            return last

        def split_product(ps, hi, lo, w, w_rest, start, stop):
            nc.tensor.matmul(ps, hi, w, start=start, stop=False)
            nc.tensor.matmul(ps, hi, w_rest, start=False, stop=False)
            return nc.tensor.matmul(ps, lo, w, start=False, stop=stop)

        def feature_product(ps, w, c0, m, at):
            for k in range(KT):
                last = nc.tensor.matmul(ps[0:m, at:at + SEQ], w[:, k, c0:c0 + m], hT[:, k, :],
                                        start=k == 0, stop=k == KT - 1)
            return last

        def pe_experts(ne, start, block_no, routed=None):
            n = NIT[ne]

            def gu(e, t, i, name, before):
                if before is not None:
                    pe.wait_ge(vector_done, V.at(T, *before))
                w, w_rest = w_hi[e % 2], g_rest(block_no, f"gu{e}")
                for k in range(KT):
                    last = split_product(psum[:, t, :], h_hi[block_no][:, k, t * P:(t + 1) * P], h_lo[:, k, t * P:(t + 1) * P],
                                         w[:, k, :], w_rest[:, k, 0:N], k == 0, k == KT - 1)
                last.then_inc(tensor_done, T.step(name))

            def tr(t, i, name, hid_name):
                pe.wait_ge(vector_done, V.at(T, hid_name, i))
                for f in range(FE // P):
                    last = nc.tensor.transpose(psum[:, 2 + t, f * P:(f + 1) * P], hid[:, t, f * P:(f + 1) * P], ident)
                last.then_inc(tensor_done, T.step(name))

            def dn(e, t, i, name, copied, first=False, final=False):
                pe.wait_ge(vector_done, V.at(T, *copied))
                w, w_rest = d_hi[e % 2], d_rest(block_no, f"dn{e}")
                for f in range(FE // P):
                    for h in range(2):
                        last = split_product(psum[:, 4 + 2 * t + h, :], hidT[:, t, f, :], hidT_lo[:, t, f, :],
                                             w[:, f, h * N:(h + 1) * N], w_rest[:, f, h * N:(h + 1) * N],
                                             first and f == 0, final and f == FE // P - 1)
                last.then_inc(tensor_done, T.step(name))

            for b in range(8):
                if b in on_bank:
                    pe.wait_ge(on_bank[b][0].sem, on_bank[b][0].at(T, *on_bank[b][1:]))
                    pe.sem_inc(waited)
                    del on_bank[b]
            pe.wait_ge(start[0].sem, start[0].at(T, *start[1:]))
            for h in range(2):
                nc.tensor.matmul(psum[:, 6 + h, :], zeros[0:1, :], crows[0:1, 0:NR, :].rearrange("r h p -> r (h p)"), start=True, stop=False)
            gu(0, 0, None, ("gu0", 0), (("parts", 0), None))
            if routed is not None:
                routed()
            gu(0, 1, None, ("gu1", 0), None)
            tr(0, None, ("tr", 0, 0), ("hid", 0, 0))
            gu(1, 0, None, ("gu0", 1), (("parts", 1), None))
            tr(1, None, ("tr", 0, 1), ("hid", 0, 1))
            dn(0, 0, None, ("dn0", 0), (("hidT", 0, 0), None), first=True)
            with nc.tensor.Fori(0, n) as i:
                T.loop(f"pe{block_no}", n)
                for j in range(4):
                    e = 1 + j
                    before = (("hid", "loop", j - 1, 1), i) if j else (("hid", "loop", 3, 1), i - 1)
                    gu(e, 1, i, ("gu1", "loop", j), before)
                    tr(0, i, ("tr", "loop", j, 0), ("hid", "loop", j, 0))
                    copied = (("hidT", "loop", j - 1, 1), i) if j else (("hidT", "loop", 3, 1), i - 1)
                    dn(e - 1, 1, i, ("dn1", "loop", j), copied)
                    gu(e + 1, 0, i, ("gu0", "loop", j), (("parts", "loop", j), i))
                    tr(1, i, ("tr", "loop", j, 1), ("hid", "loop", j, 1))
                    dn(e, 0, i, ("dn0", "loop", j), (("hidT", "loop", j, 0), i))
                T.loop_end()
            for e in range(1 + 4 * n, ne):
                prev = ("loop", 3) if e == 1 + 4 * n else (e - 1,)
                it = n - 1 if e == 1 + 4 * n else None
                gu(e, 1, None, ("gu1", e), (("hid", *prev, 1), it))
                tr(0, None, ("tr", e, 0), ("hid", e, 0))
                dn(e - 1, 1, None, ("dn1", e - 1), (("hidT", *prev, 1), it))
                if e + 1 < ne:
                    gu(e + 1, 0, None, ("gu0", e + 1), (("parts", e + 1), None))
                tr(1, None, ("tr", e, 1), ("hid", e, 1))
                dn(e, 0, None, ("dn0", e), (("hidT", e, 0), None), final=e == ne - 1)
            dn(ne - 1, 1, None, ("dn1", ne - 1), (("hidT", ne - 1, 1), None), final=True)

        def pe_attention(tag, steps, ahead, scores_of, widths, values_of, probs_src, probs_T, outs, between):
            n = len(steps)

            def score_step(s):
                ps = take((tag, "S", s), V, pair=True)
                scores_of(ps, s).then_inc(tensor_done, T.step((tag, "S", s)))

            for s in range(ahead):
                score_step(s)
            for s in range(n):
                between(s)
                if s + ahead < n:
                    score_step(s + ahead)
                pe.wait_ge(probs_src(s)[0].sem, probs_src(s)[0].at(T, *probs_src(s)[1:]))
                ps = take((tag, "PT", s), A)
                src, blocks = widths(s)
                for b in range(blocks):
                    last = nc.tensor.transpose(ps[:, b * P:(b + 1) * P], src[:, b * P:(b + 1) * P], ident)
                last.then_inc(tensor_done, T.step((tag, "PT", s)))
                if s in outs:
                    name, reader, b = outs[s]
                    take(name, reader, b)
                pe.wait_ge(scalar_done, A.at(T, (tag, "pT", s)))
                values_of(s).then_inc(tensor_done, T.step((tag, "PV", s)))

        ATT = [(t, i) for t in range(TT) for i in range(NA // 2)]

        def pe_first(l):
            T.begin(0, l)
            on_bank.clear()
            turn[0] = 0

            def ada_row(c, bank_no):
                ps = take(("ada", c), A, bank_no)
                pe.wait_ge(G.sem(T, f"ada{c}"), G.level(T, f"ada{c}"))
                if c == ADA_PAIRS[0]:
                    pe.wait_ge(bias_loaded, bias_count(T))
                for k in range(KT):
                    nc.tensor.matmul(ps[0:1, :], cact[:, k:k + 1], gslot(0, f"ada{c}")[:, k, 0:N], start=k == 0, stop=False)
                nc.tensor.matmul(ps[0:1, :], ident[0:ADA, c:c + 1], brow[0:ADA, :], start=False, stop=True).then_inc(tensor_done, T.step(("ada", c)))

            def row_columns(c, bank_no):
                ps = take(("columns", c), V, bank_no)
                pe.wait_ge(scalar_done, A.at(T, ("arow", c + 1)))
                pe.sem_inc(waited)
                for n in range(2):
                    for j in range(N // P):
                        last = nc.tensor.matmul(ps[:, 4 * n + j:4 * n + j + 1], arow[n][:, j * P:(j + 1) * P], ones[0:1, 0:1],
                                                start=True, stop=True)
                last.then_inc(tensor_done, T.step(("sums_used", c)))

            def sum_columns(c, bank_no=None):
                ps = take(("columns", c), V, bank_no)
                pe.wait_ge(vector_done, V.at(T, ("acc", c + 1)))
                pe.sem_inc(waited)
                for n in range(2):
                    for j in range(N // P):
                        o = ps[:, 4 * n + j:4 * n + j + 1]
                        nc.tensor.matmul(o, acc[:, n, j * P:(j + 1) * P], ones[:, 0:1], start=True, stop=False)
                        last = nc.tensor.matmul(o, brow[0:ADA, j * P:(j + 1) * P], ident[0:ADA, c + n:c + n + 1],
                                                start=False, stop=True)
                last.then_inc(tensor_done, T.step(("sums_used", c)))

            def sum_gates(c):
                for n in range(2):
                    ps = take(("gate", c + n), V)
                    pe.wait_ge(vector_done, V.at(T, ("acc", c + n)))
                    pe.sem_inc(waited)
                    nc.tensor.matmul(ps, ones[:, 0:P], acc[:, n, :], start=True, stop=False)
                    nc.tensor.matmul(ps, crows[:, NR + GATES.index(c + n), :], brow[0:ADA, :], start=False, stop=True).then_inc(tensor_done, T.step(("gate", c + n)))
                T.also(("sums_used", c))

            ada_row(2, 0)
            ada_row(3, 1)
            row_columns(2, 2)
            sum_columns(0, 3)
            pe.wait_ge(vector_done, V.before(T))
            pe.wait_ge(scalar_done, A.before(T))
            pe.wait_ge(x_loaded, 16)
            transposed_x("xT", x, None)
            pe.wait_ge(vector_done, V.at(T, ("hT", KT // 2 - 2)))
            pe.wait_ge(scalar_done, A.at(T, ("hT", KT // 2 - 1)))

            def in_proj(name, t):
                if t == 0:
                    pe.wait_ge(G.sem(T, name), G.level(T, name))
                c0, c1 = CHUNKS1[name]
                ps = take((name, t), V if name in ("idx", "aq", "ak", "rqk") else A)
                token_product(ps, t, gslot(0, name), min(N, c1 - c0)).then_inc(tensor_done, T.step((name, t)))

            rope_slot = {n: i for i, n in enumerate([(c, t) for c in ("idx", "aq", "ak", "rqk") for t in range(TT)])}

            def transposed_rope(name, t, blocks):
                pe.wait_ge(vector_done, V.at(T, ("rope", name, t)))
                ps = take((name, "T", t), A)
                src = roped[:, rope_slot[name, t] % 3, :]
                for b in range(blocks):
                    last = nc.tensor.transpose(ps[:, b * P:(b + 1) * P], src[:, b * P:(b + 1) * P], ident)
                last.then_inc(tensor_done, T.step((name, "T", t)))

            def index_scores(t):
                nk = (t + 1) * P
                ps = take(("idxS", t), A, pair=True)
                if t == 0:
                    pe.sem_inc(waited)
                    pe.wait_ge(scalar_done, A.at(T, ("idx", "Tc", 1)))
                for p in range(2):
                    for h in (0, 1):
                        last = nc.tensor.matmul(ps[:, h, p * SEQ:p * SEQ + nk],
                                                idxT[h * HD:(h + 1) * HD, p, t * P:(t + 1) * P],
                                                idxT[h * HD:(h + 1) * HD, 2, 0:nk], start=True, stop=True)
                last.then_inc(tensor_done, T.step(("idxS", t)))

            def mqk(b):
                if b == 0:
                    pe.wait_ge(G.sem(T, "mqk"), G.level(T, "mqk"))
                ps = take(("mqk", b), A)
                for f in range(2):
                    last = feature_product(ps, gslot(0, "mqk"), (2 * b + f) * P, P, f * SEQ)
                last.then_inc(tensor_done, T.step(("mqk", b)))

            def gates():
                ps = take("gates", V)
                for f in range(2):
                    last = feature_product(ps, gslot(0, "mvo"), N + NR * f, NR, f * SEQ)
                last.then_inc(tensor_done, T.step("gates"))

            in_proj("idx", 0)
            in_proj("idx", 1)
            in_proj("aq", 0)
            transposed_rope("idx", 0, 3)
            transposed_rope("idx", 1, 3)
            in_proj("aq", 1)
            index_scores(0)
            index_scores(1)
            in_proj("ak", 0)
            transposed_rope("aq", 0, 4)
            transposed_rope("aq", 1, 4)
            in_proj("ak", 1)
            in_proj("av", 0)
            in_proj("av", 1)
            transposed_rope("ak", 0, 4)
            transposed_rope("ak", 1, 4)
            in_proj("rqk", 0)

            def att_scores(ps, s):
                t, i = ATT[s]
                nk = (t + 1) * P
                if s == 0:
                    pe.wait_ge(scalar_done, A.at(T, ("aq", "Tc", 1)))
                    pe.wait_ge(scalar_done, A.at(T, ("ak", "Tc", 1)))
                for h in (0, 1):
                    last = nc.tensor.matmul(ps[:, h, 0:nk], aqT[h * HD:(h + 1) * HD, i, t * P:(t + 1) * P],
                                            akT[h * HD:(h + 1) * HD, i, 0:nk], start=True, stop=True)
                return last

            def att_values(s):
                t, i = ATT[s]
                if s == 0:
                    pe.wait_ge(scalar_done, A.at(T, ("av", 1)))
                for h in (0, 1):
                    c = (2 * i + h) * HD
                    for k in range(t + 1):
                        last = nc.tensor.matmul(psum[:, 6 + t, c:c + HD], pT[:, s % 2, (h * (t + 1) + k) * P:(h * (t + 1) + k + 1) * P],
                                                av[:, k, c:c + HD], start=k == 0, stop=k == t)
                return last

            def transposed_scores(ps, qk, h):
                r, b = (h % 2) * HD, h // 2
                nc.tensor.matmul(ps[:, 0:SEQ], qk[r:r + HD, 2 + b, 0:P], qk[r:r + HD, b, :], start=True, stop=True)
                return nc.tensor.matmul(ps[:, SEQ:SEQ + P], qk[r:r + HD, 2 + b, P:SEQ], qk[r:r + HD, b, P:SEQ],
                                        start=True, stop=True)

            def ret_scores(h):
                ps = take(("ret", "S", h), V)
                if h == 0:
                    pe.wait_ge(scalar_done, A.at(T, ("rqk", "Tc", 1)))
                transposed_scores(ps, rrT, h).then_inc(tensor_done, T.step(("ret", "S", h)))

            def ret_values(h):
                if h == 0:
                    take(("ret", "O"), V, 6)
                    pe.wait_ge(scalar_done, A.at(T, ("rvg", 1)))
                ps = bank(T, ("ret", "O"))
                pe.wait_ge(vector_done, V.at(T, ("ret", "sT", h)))
                c = h * HD
                nc.tensor.matmul(ps[:, c:c + HD], sT[:, h % 2, 0:P], rv[:, 0, c:c + HD], start=True, stop=True)
                nc.tensor.matmul(ps[:, 256 + c:256 + c + HD], sT[:, h % 2, P:SEQ], rv[:, 0, c:c + HD], start=True, stop=False)
                nc.tensor.matmul(ps[:, 256 + c:256 + c + HD], sT[:, h % 2, SEQ:384], rv[:, 1, c:c + HD], start=False, stop=True).then_inc(tensor_done, T.step(("ret", "PV", h)))

            def between(s):
                if s == 0:
                    in_proj("rqk", 1)
                    sum_gates(4)
                    in_proj("rvg", 0)
                if s == 1:
                    in_proj("rvg", 1)
                    transposed_rope("rqk", 0, 4)
                    transposed_rope("rqk", 1, 4)
                if s == 2:
                    sum_columns(6)
                    in_proj("mvo", 0)
                if s == 3:
                    in_proj("mvo", 1)
                    gates()
                if s == 4:
                    ret_scores(0)
                    ret_scores(1)
                    mqk(0)
                if s == 5:
                    ret_values(0)
                    ret_values(1)
                    ret_scores(2)
                    ret_scores(3)
                    mqk(1)
                    sum_columns(8)
                if s == 6:
                    ret_values(2)
                    ret_values(3)

            pe_attention("att", ATT, 2, att_scores, lambda s: (sm[:, s % 2, :], 2 * (ATT[s][0] + 1)), att_values,
                         lambda s: (A, ("att", "exp", s)), pT,
                         {0: (("att", "O", 0), V, 6), NA // 2: (("att", "O", 1), V, 7)}, between)

            ps = take("gcol", V)
            pe.wait_ge(scalar_done, A.at(T, "erow"))
            for t in range(TT):
                for n, r in ((0, 2), (1, 5)):
                    last = nc.tensor.matmul(ps[:, 8 * t + 4 * n:8 * t + 4 * n + NR], grow[0:NR, r, t * P:(t + 1) * P],
                                            ident[0:NR, 0:NR], start=True, stop=True)
            last.then_inc(tensor_done, T.step("gcol"))

            def ml_scores(h):
                ps = take(("ml", "M", h), V)
                if h == 0:
                    pe.wait_ge(tables_loaded, 16 * 4)
                    pe.wait_ge(scalar_done, A.at(T, "conv"))
                nc.tensor.matmul(ps[:, 0:SEQ], crows[0:NR, h, :], grow[0:NR, 3, :], start=True, stop=True).then_inc(tensor_done, T.step(("ml", "M", h)))
                ps = take(("ml", "S", h), V)
                transposed_scores(ps, qkT, h).then_inc(tensor_done, T.step(("ml", "S", h)))

            ml_scores(0)
            ml_scores(1)
            o0, o1 = take(("ml", "O", 0), V, 7), take(("ml", "O", 1), V, 6)
            for h in range(NR):
                pe.wait_ge(vector_done, V.at(T, ("ml", "sT", h)))
                if h == 0:
                    pe.wait_ge(scalar_done, A.at(T, ("mvo", 1)))
                c = h * (HD + 1)
                nc.tensor.matmul(o0[:, c:c + HD + 1], sT[:, h % 2, 0:P], mv[:, 0, h, :], start=True, stop=True)
                nc.tensor.matmul(o1[:, c:c + HD + 1], sT[:, h % 2, P:SEQ], mv[:, 0, h, :], start=True, stop=False)
                nc.tensor.matmul(o1[:, c:c + HD + 1], sT[:, h % 2, SEQ:384], mv[:, 1, h, :], start=False, stop=True).then_inc(tensor_done, T.step(("ml", "PV", h)))
                if h + 2 < NR:
                    ml_scores(h + 2)

            pe.wait_ge(vector_done, V.at(T, ("read", ("att", "O", 1))))
            transposed_x("oT", o_cat, A, range(2))
            pe.wait_ge(scalar_done, A.at(T, ("oTc", 1)))
            for t in range(TT):
                for h in range(2):
                    if t == 0:
                        pe.wait_ge(G.sem(T, f"wo{h}"), G.level(T, f"wo{h}"))
                    token_product(take(("wo", t, h), V), t, gslot(0, f"wo{h}"), N, range(4))
            pe.wait_ge(vector_done, V.at(T, "o_cat"))
            transposed_x("oT", o_cat, A, range(2, 4))
            pe.wait_ge(scalar_done, A.at(T, ("oTc", 3)))
            for t in range(TT):
                for h in range(2):
                    token_product(bank(T, ("wo", t, h)), t, gslot(0, f"wo{h}"), N, range(4, KT)).then_inc(tensor_done, T.step(("wo", t, h)))
            sum_gates(10)
            transposed_x("xT2", x, None, ready=lambda t: ("ln1", t))

            def router():
                ps = psum[:, 3, :]
                for t in range(TT):
                    for k in range(KT):
                        for n, part in enumerate((h_hi[0].bitcast(F32), h_lo[:, :, :].bitcast(F32))):
                            last = nc.tensor.matmul(ps[:, t * NE:(t + 1) * NE], part[:, k, t * P:(t + 1) * P], wr[:, k, :],
                                                    start=k == 0 and n == 0, stop=k == KT - 1 and n == 1)
                last.then_inc(tensor_done, T.step("router"))

            pe_experts(NE, (V, ("hT2", "parts")), 0, router)
            T.end()

        DIFF = [(t, h) for t in range(TT) for h in range(DH)]
        WIN = [(t, g) for t in range(TT) for g in range(WG)]

        def pe_second(l):
            T.begin(1, l)
            on_bank.clear()
            turn[0] = 0
            pe.wait_ge(scalar_done, A.before(T))
            pe.wait_ge(params_loaded, params_count(T))
            ps = take("gains", V)
            pe.sem_inc(waited)
            nc.tensor.transpose(ps[:, 0:3 * KT + GG], grows[0:3 * KT + GG, :], ident[0:3 * KT + GG, 0:3 * KT + GG]).then_inc(tensor_done, T.step("gains"))
            ps = take("ws", A)
            for g in range(GG):
                last = nc.tensor.transpose(ps[:, g * P:(g + 1) * P], wsp[:, g, :], ident)
            last.then_inc(tensor_done, T.step("ws"))
            ps = take("p", A)
            for t in range(TT):
                for k in range(PLE // P):
                    last = nc.tensor.transpose(ps[:, k * SEQ + t * P:k * SEQ + (t + 1) * P], prow[:, t, k * P:(k + 1) * P], ident)
            last.then_inc(tensor_done, T.step("p"))
            transposed_x("xT", o_cat, None, ready=lambda t: ("xn", "mix", t))
            pe.wait_ge(vector_done, V.at(T, ("hT", KT // 2 - 2)))
            pe.wait_ge(scalar_done, A.at(T, ("hT", KT // 2 - 1)))

            def features(name, b, blocks):
                if b == 0:
                    pe.wait_ge(G.sem(T, name), G.level(T, name))
                ps = take((name, b), A)
                for f in range(blocks):
                    last = feature_product(ps, gslot(1, name), (2 * b + f) * P, P, f * SEQ)
                last.then_inc(tensor_done, T.step((name, b)))

            def tokens(name, t):
                if t == 0:
                    pe.wait_ge(G.sem(T, name), G.level(T, name))
                ps = take((name, t), A)
                token_product(ps, t, gslot(1, name), N).then_inc(tensor_done, T.step((name, t)))

            for name in ("aq", "ak"):
                features(name, 0, 2)
                features(name, 1, 1)
            tokens("avcv", 0)
            tokens("avcv", 1)

            def diff_scores(ps, s):
                t, h = DIFF[s]
                if s == 0:
                    pe.wait_ge(scalar_done, A.at(T, ("ak", "c", 1)))
                for c in range(2):
                    r = (h % 2) * HD + c * DQK
                    last = nc.tensor.matmul(ps[:, c, 0:SEQ], qT2[r:r + DQK, h // 2, t * P:(t + 1) * P],
                                            kT2[r:r + DQK, h // 2, :], start=True, stop=True)
                return last

            def diff_values(s):
                t, h = DIFF[s]
                if s == 0:
                    pe.wait_ge(scalar_done, A.at(T, ("avcv", "c", 1)))
                for k in range(TT):
                    last = nc.tensor.matmul(psum[:, 6 + t, h * HD:(h + 1) * HD], pT2[:, s % 2, k * P:(k + 1) * P],
                                            avcv[:, k, h * HD:(h + 1) * HD], start=k == 0, stop=k == TT - 1)
                return last

            def between_diff(s):
                if s < 2:
                    tokens("buv", s)
                elif s < 4:
                    features("cqk", s - 2, 2)

            pe_attention("diff", DIFF, 3, diff_scores, lambda s: (at2[:, s % 2, :], TT), diff_values,
                         lambda s: (V, ("diff", "at", s)), pT2,
                         {0: (("diff", "O", 0), V, 6), DH: (("diff", "O", 1), V, 7)}, between_diff)

            def win_scores(ps, s):
                t, g = WIN[s]
                if s == 0:
                    pe.wait_ge(scalar_done, A.at(T, ("cqk", "c", 1)))
                for h in range(2):
                    last = nc.tensor.matmul(ps[:, h, 0:SEQ], cT2[h * HD:(h + 1) * HD, g, t * P:(t + 1) * P],
                                            cT2[h * HD:(h + 1) * HD, WG, :], start=True, stop=True)
                return last

            def win_values(s):
                t, g = WIN[s]
                for h in range(2):
                    c = (h * WG + g) * HD
                    for k in range(TT):
                        last = nc.tensor.matmul(psum[:, 6 + t, c:c + HD], pT2[:, s % 2, (h * TT + k) * P:(h * TT + k + 1) * P],
                                                avcv[:, k, 384 + h * HD:384 + (h + 1) * HD], start=k == 0, stop=k == TT - 1)
                return last

            def between_win(s):
                if s == 0:
                    pe.wait_ge(vector_done, V.at(T, ("vn", 1)))
                    pe.wait_ge(scalar_done, A.at(T, "wsT"))
                    pe.sem_inc(waited)
                    ps = take("mix", V)
                    for g in range(GG):
                        last = nc.tensor.matmul(ps[:, g * P:(g + 1) * P], wsT[:, g, :], vn[:, :, g * HD:(g + 1) * HD],
                                                start=True, stop=True)
                    last.then_inc(tensor_done, T.step("mix"))

            pe_attention("win", WIN, 3, win_scores, lambda s: (sm2[:, s % 3, :], 2 * TT), win_values,
                         lambda s: (A, ("win", "exp", s)), pT2,
                         {0: (("win", "O", 0), V, 6), WG: (("win", "O", 1), V, 7)}, between_win)

            pe.wait_ge(vector_done, V.at(T, "o_cat"))
            transposed_x("oT", o_cat, A)
            pe.wait_ge(scalar_done, A.at(T, ("oTc", KT // 2 - 1)))
            for t in range(TT):
                for h in range(2):
                    if t == 0:
                        pe.wait_ge(G.sem(T, f"wo{h}"), G.level(T, f"wo{h}"))
                    ps = take(("wo", t, h), V)
                    token_product(ps, t, gslot(1, f"wo{h}"), N).then_inc(tensor_done, T.step(("wo", t, h)))
            transposed_x("xT2", o_cat, None, ready=lambda t: ("xn", "ffn", t))
            pe_experts(NF, (V, ("hT2", "parts")), 1)
            for b in range(4):
                on_bank[4 + b] = (V, ("read", ("acc", b)))
            for t in range(TT):
                on_bank[t], on_bank[2 + t] = (V, ("hid", NF - 1, t)), (V, ("hidT", NF - 1, t))
            pe.wait_ge(DN.sem(T, "up"), DN.level(T, "up"))
            pe.wait_ge(scalar_done, A.at(T, "pT"))
            for t in range(TT):
                for h in range(2):
                    ps = take(("e", t, h), A)
                    for k in range(PLE // P):
                        last = nc.tensor.matmul(ps, pTT[:, k, t * P:(t + 1) * P], dslot(1, "up")[:, k, h * N:(h + 1) * N],
                                                start=k == 0, stop=k == PLE // P - 1)
                    last.then_inc(tensor_done, T.step(("e", t, h)))
            transposed_x("xT3", o_cat, None, ready=lambda t: ("xn", "ple", t))
            pe.wait_ge(vector_done, V.at(T, ("hT3", KT // 2 - 2)))
            pe.wait_ge(scalar_done, A.at(T, ("hT3", KT // 2 - 1)))
            for t in range(TT):
                for h in range(2):
                    if t == 0:
                        pe.wait_ge(G.sem(T, f"pg{h}"), G.level(T, f"pg{h}"))
                    ps = take(("pg", t, h), A)
                    token_product(ps, t, gslot(1, f"pg{h}"), N).then_inc(tensor_done, T.step(("pg", t, h)))
            T.end()

        @block.tensor
        def _(pe):
            pe.sem_inc(tensor_done, T.step(by=AHEAD))
            pe.wait_ge(start_loaded, 16 * 3)
            nc.tensor.transpose(psum[:, 0, 0:KT], c8, ident[0:KT, 0:KT]).then_inc(tensor_done, T.step("c"))
            pe.wait_ge(vector_done, V.at(T, "cact"))
            with pe.Fori(0, DEPTH) as l:
                pe_first(l)
            with pe.Fori(0, DEPTH) as l:
                pe_second(l)

        def ts(o, a, s1, s2, op0, op1=None):
            if op1 is None:
                return nc.vector.tensor_scalar(o, a, s1, None, op0)
            return nc.vector.tensor_scalar(o, a, s1, s2, op0, op1)

        def tt(o, a, b, op):
            return nc.vector.tensor_tensor(o, a, b, op)

        def stt(o, a, s, b, op0, op1):
            return nc.vector.scalar_tensor_tensor(o, a, s, b, op0, op1)

        def vmax(o, a):
            return nc.vector.tensor_reduce(o, a, AX.X, ALU.max)

        def vsum(o, a):
            return nc.vector.tensor_reduce(o, a, AX.X, ALU.add)

        def over(col, *shape):
            return col.unsqueeze(2).to_broadcast([P, *shape])

        def ada(c):
            dve.wait_ge(G.sem(V, f"ada{c}"), G.level(V, f"ada{c}"))
            n = ADA_PAIRS.index(c // 2 * 2)
            if c % 2 == 0 and n > 1:
                dve.wait_ge(tensor_done, T.at(V, ("sums_used", ADA_PAIRS[n - 1])))
            w, a = gslot(0, f"ada{c}"), acc[:, c % 2, :]
            ts(a, w[:, 0, 0:N], cact[:, 0:1], None, ALU.mult).then_inc(vector_done, V.step())
            dve.wait_ge(vector_done, V.now())
            for k in range(1, KT):
                stt(a, w[:, k, 0:N], cact[:, k:k + 1], a, ALU.mult, ALU.add).then_inc(vector_done, V.step(("acc", c) if k == KT - 1 else None))
                dve.wait_ge(vector_done, V.now())

        def rope(ps, nh, t, o, name, last_read, space):
            heads = ps[:, 0:nh * HD].rearrange("p (h d) -> p h d", h=nh)
            a = space[:, 0, 0:nh * HD].rearrange("p (h d) -> p h d", h=nh)
            b = space[:, 1, 0:nh * HD].rearrange("p (h d) -> p h d", h=nh)
            cs = cosf[:, t, :].unsqueeze(1).to_broadcast([P, nh, HD])
            tt(a, heads, cs, ALU.mult).then_inc(vector_done, V.step())
            dve.wait_ge(vector_done, V.now())
            for h, g in ((0, 1), (1, 0)):
                sn = sinf[:, t, h * HALF:(h + 1) * HALF].unsqueeze(1).to_broadcast([P, nh, HALF])
                tt(b[:, :, h * HALF:(h + 1) * HALF], heads[:, :, g * HALF:(g + 1) * HALF], sn, ALU.mult).then_inc(vector_done, V.step(last_read if h else None))
                dve.wait_ge(vector_done, V.now())
            tt(o.rearrange("p (h d) -> p h d", h=nh), a, b, ALU.add).then_inc(vector_done, V.step(name))
            dve.wait_ge(vector_done, V.now())

        def head_variance(name):
            vsum(hs, hn).then_inc(vector_done, V.step())
            dve.wait_ge(vector_done, V.now())
            ts(hs, hs, 1.0 / HD, None, ALU.mult).then_inc(vector_done, V.step())
            dve.wait_ge(vector_done, V.now())
            tt(hn, hn, over(hs, 8, HD), ALU.subtract).then_inc(vector_done, V.step())
            dve.wait_ge(vector_done, V.now())
            tt(sq, hn, hn, ALU.mult).then_inc(vector_done, V.step())
            dve.wait_ge(vector_done, V.now())
            vsum(hv, sq).then_inc(vector_done, V.step())
            dve.wait_ge(vector_done, V.now())
            ts(hv, hv, 1.0 / HD, LN_EPS, ALU.mult, ALU.add).then_inc(vector_done, V.step((name, "var")))
            dve.wait_ge(vector_done, V.now())

        def head_normed(name):
            dve.wait_ge(scalar_done, A.at(V, (name, "sqrt")))
            nc.vector.reciprocal(hs, hv).then_inc(vector_done, V.step())
            dve.wait_ge(vector_done, V.now())
            tt(sq, hn, over(hs, 8, HD), ALU.mult).then_inc(vector_done, V.step())
            dve.wait_ge(vector_done, V.now())

        def moments(name, t):
            for h in range(2):
                nc.vector.bn_stats(st[:, 6 * h:6 * h + 6], x[:, t, h * N:(h + 1) * N]).then_inc(vector_done, V.step())
                dve.wait_ge(vector_done, V.now())
            dve.sem_inc(waited)
            nc.vector.bn_aggr(agg[:, 2 * t:2 * t + 2], st).then_inc(vector_done, V.step())
            dve.wait_ge(vector_done, V.now())
            ts(rstd[:, t:t + 1], agg[:, 2 * t + 1:2 * t + 2], LN_EPS, None, ALU.add).then_inc(vector_done, V.step((name, "var", t)))
            dve.wait_ge(vector_done, V.now())

        def layer_norm(name, t):
            dve.wait_ge(scalar_done, A.at(V, (name, "sqrt", t)))
            nc.vector.reciprocal(rstd[:, TT + t:TT + t + 1], rstd[:, t:t + 1]).then_inc(vector_done, V.step())
            dve.wait_ge(vector_done, V.now())
            ts(x[:, t, :], x[:, t, :], agg[:, 2 * t:2 * t + 1], rstd[:, TT + t:TT + t + 1], ALU.subtract, ALU.mult).then_inc(vector_done, V.step())
            dve.wait_ge(vector_done, V.now())
            tt(x[:, t, :], x[:, t, :], rows[:, 0, :], ALU.mult).then_inc(vector_done, V.step())
            dve.wait_ge(vector_done, V.now())
            tt(x[:, t, :], x[:, t, :], rows[:, 1, :], ALU.add).then_inc(vector_done, V.step((name, t)))
            dve.wait_ge(vector_done, V.now())

        def modulated(tag, name, scale, shift=None, parts=False):
            for g in range(0, KT // 2, 2):
                dve.wait_ge(tensor_done, T.at(V, (tag, g)))
                ps = bank(V, (tag, g))
                for f in range(2):
                    k = 2 * g + f
                    if shift is None:
                        ts(hT[:, k, :], ps[:, f * SEQ:(f + 1) * SEQ], scale[:, k:k + 1], None, ALU.mult).then_inc(vector_done, V.step((name, g) if f else None))
                    else:
                        ts(hT[:, k, :], ps[:, f * SEQ:(f + 1) * SEQ], scale[:, k:k + 1], shift[:, k:k + 1], ALU.mult, ALU.add).then_inc(vector_done, V.step((name, g) if f else None))
                V.also(("read", (tag, g)))
            if parts:
                dve.wait_ge(vector_done, V.now())
                for g in range(KT // 2):
                    dve.wait_ge(scalar_done, A.at(V, (name, "hi", g)))
                    tt(h_lo[:, 2 * g:2 * g + 2, :], hT[:, 2 * g:2 * g + 2, :], h_hi[V.block][:, 2 * g:2 * g + 2, :], ALU.subtract).then_inc(vector_done, V.step((name, "parts") if g == KT // 2 - 1 else None))

        def weights_rest(e, i, rounded, name):
            w, w_rest, hi = gslot(V.block, f"gu{e}"), g_rest(V.block, f"gu{e}"), w_hi[e % 2]
            for q in range(2):
                k = slice(q * KT // 2, (q + 1) * KT // 2)
                dve.wait_ge(scalar_done, A.at(V, (*rounded, q), i))
                tt(w_rest[:, k, 0:N], w[:, k, 0:N], hi[:, k, :], ALU.subtract).then_inc(vector_done, V.step(name if q else None))

        def dve_experts(ne, gated):
            n = NIT[ne]

            def one(e, i, step, name, column, following):
                for t in range(TT):
                    dve.wait_ge(scalar_done, A.at(V, ("silu", *step, t), i))
                    up = psum[:, t, FE:2 * FE]
                    if gated:
                        stt(hid[:, t, :], up, column(t), sact[:, t, :], ALU.mult, ALU.mult).then_inc(vector_done, V.step((*name, t)))
                    else:
                        tt(hid[:, t, :], up, sact[:, t, :], ALU.mult).then_inc(vector_done, V.step((*name, t)))
                    if t == 0:
                        if following is not None:
                            weights_rest(e + 1, i, ("w_hi", *following), ("parts", *following))
                        dve.wait_ge(scalar_done, A.at(V, ("d_hi", *step), i))
                        d = dslot(V.block, f"dn{e}")
                        tt(d_rest(V.block, f"dn{e}"), d, d_hi[e % 2], ALU.subtract).then_inc(vector_done, V.step())
                for t in range(TT):
                    dve.wait_ge(scalar_done, A.at(V, ("hidT", *step, t), i))
                    tt(hidT_lo[:, t, :, :].rearrange("p f n -> p (f n)"), psum[:, 2 + t, 0:FE],
                       hidT[:, t, :, :].rearrange("p f n -> p (f n)"), ALU.subtract).then_inc(vector_done, V.step(("hidT", *step, t)))

            def static_column(e):
                return lambda t: gate[:, t * NE + e:t * NE + e + 1]

            one(0, None, (0,), ("hid", 0), static_column(0), (1,))
            with nc.vector.Fori(0, n) as i:
                V.loop(f"dve{V.block}", n)
                for j in range(4):
                    one(1 + j, i, ("loop", j), ("hid", "loop", j),
                        lambda t, j=j: gate[:, bass.ds(i * 4 + (t * NE + 1 + j), 1)], ("loop", j))
                V.loop_end()
            for e in range(1 + 4 * n, ne):
                one(e, None, (e,), ("hid", e), static_column(e), (e + 1,) if e + 1 < ne else None)

        def dve_first(l):
            V.begin(0, l)
            dve.wait_ge(scalar_done, A.before(V))
            dve.wait_ge(tensor_done, T.before(V))

            def shift_columns(c, i):
                dve.wait_ge(tensor_done, T.at(V, ("sums_used", c)))
                ts(mod[i], bank(V, ("columns", c))[:, 0:KT], float(i % 2), None, ALU.add).then_inc(vector_done, V.step(("read", ("columns", c))))
                dve.wait_ge(vector_done, V.now())

            ada(0)
            ada(1)
            shift_columns(2, 1)
            shift_columns(0, 0)
            modulated("xT", "hT", mod[1], mod[0])

            slots = {}

            def rope_chunk(name, t, nh):
                i = len(slots)
                slots[i] = (name, t)
                dve.wait_ge(tensor_done, T.at(V, (name, t)))
                ps = bank(V, (name, t))
                if i >= 3:
                    dve.wait_ge(tensor_done, T.at(V, (slots[i - 3][0], "T", slots[i - 3][1])))
                o = roped[:, i % 3, :]
                if name == "idx":
                    nc.vector.tensor_copy(iw[:, t * NI:(t + 1) * NI], ps[:, IW - IQ:RQ - IQ]).then_inc(vector_done, V.step())
                    dve.wait_ge(vector_done, V.now())
                    rope(ps, nh, t, o[:, 0:nh * HD], None, ("read", (name, t)), sm)
                    nc.vector.tensor_copy(o[:, nh * HD:(nh + 1) * HD], o[:, (nh - 1) * HD:nh * HD]).then_inc(vector_done, V.step(("rope", name, t)))
                    dve.wait_ge(vector_done, V.now())
                else:
                    rope(ps, nh, t, o, ("rope", name, t), ("read", (name, t)), rel2 if name == "rqk" else sm)

            def top_k(t):
                nk = (t + 1) * P
                w = score[:, 0:nk]
                dve.wait_ge(scalar_done, A.at(V, ("rel", t)))
                for h in range(NI):
                    prev = cblock[:, C1["vis"] + t * SEQ:C1["vis"] + t * SEQ + nk] if h == 0 else w
                    stt(w, rel[:, (h % 2) * 2 + h // 2, 0:nk], iw[:, t * NI + h:t * NI + h + 1], prev, ALU.mult, ALU.add).then_inc(vector_done, V.step(("rel_read", t) if h == NI - 1 else None))
                    dve.wait_ge(vector_done, V.now())
                for r in range(TOPK // 8):
                    dve.sem_inc(waited)
                    nc.vector.max(top8, w).then_inc(vector_done, V.step())
                    dve.wait_ge(vector_done, V.now())
                    dve.sem_inc(waited)
                    nc.vector.match_replace(w, top8, w, TAKEN).then_inc(vector_done, V.step())
                    dve.wait_ge(vector_done, V.now())
                ts(bias[:, t, 0:nk], w, -2.0e38, -BIG, ALU.is_gt, ALU.mult).then_inc(vector_done, V.step())
                dve.wait_ge(vector_done, V.now())

            def scale_iw(t):
                ts(iw[:, t * NI:(t + 1) * NI], iw[:, t * NI:(t + 1) * NI], (NI * HD) ** -0.5, None, ALU.mult).then_inc(vector_done, V.step())
                dve.wait_ge(vector_done, V.now())

            def att_in(s):
                t, i = ATT[s]
                nk = (t + 1) * P
                dve.wait_ge(tensor_done, T.at(V, ("att", "S", s)))
                ps = bank(V, ("att", "S", s))
                if s >= 2:
                    dve.wait_ge(tensor_done, T.at(V, ("att", "PT", s - 2)))
                o = sm[:, s % 2, 0:2 * nk].rearrange("p (h k) -> p h k", h=2)
                bb = bias[:, t, 0:nk].unsqueeze(1).to_broadcast([P, 2, nk])
                stt(o, ps[:, :, 0:nk], HD ** -0.5, bb, ALU.mult, ALU.add).then_inc(vector_done, V.step(("read", ("att", "S", s))))
                dve.wait_ge(vector_done, V.now())
                nc.vector.tensor_reduce(ngm[:, 2 * (s % 2):2 * (s % 2) + 2], o, AX.X, ALU.max, negate=True).then_inc(vector_done, V.step(("att", "max", s)))
                dve.wait_ge(vector_done, V.now())

            def att_out(t):
                dve.wait_ge(scalar_done, A.at(V, ("att", "exp", (t + 1) * (NA // 2) - 1)))
                nc.vector.reciprocal(rinv[:, t * NA:(t + 1) * NA], rsum[:, t * NA:(t + 1) * NA]).then_inc(vector_done, V.step())
                dve.wait_ge(vector_done, V.now())
                dve.wait_ge(tensor_done, T.at(V, ("att", "PV", (t + 1) * (NA // 2) - 1)))
                tt(o_cat[:, t, 0:N].rearrange("p (h d) -> p h d", h=NA), bank(V, ("att", "O", t)).rearrange("p (h d) -> p h d", h=NA), over(rinv[:, t * NA:(t + 1) * NA], NA, HD), ALU.mult).then_inc(vector_done, V.step(("read", ("att", "O", t))))
                dve.wait_ge(vector_done, V.now())

            def ret_weights(h):
                dve.wait_ge(tensor_done, T.at(V, ("ret", "S", h)))
                ps = bank(V, ("ret", "S", h))
                if h >= 2:
                    dve.wait_ge(tensor_done, T.at(V, ("ret", "PV", h - 2)))
                tt(sT[:, h % 2, :], ps[:, 0:384], cblock[:, h * 384:(h + 1) * 384], ALU.mult).then_inc(vector_done, V.step(("ret", "sT", h)))
                dve.wait_ge(vector_done, V.now())
                V.also(("read", ("ret", "S", h)))

            g4 = grow[0:NR]

            def gate_row(c):
                for n in range(2):
                    dve.wait_ge(tensor_done, T.at(V, ("gate", c + n)))
                    ts(gb[:, n * N:(n + 1) * N], bank(V, ("gate", c + n)), 1.0, None, ALU.add).then_inc(vector_done, V.step(("read", ("gate", c + n))))
                    dve.wait_ge(vector_done, V.now())

            def gate_rows():
                dve.wait_ge(tensor_done, T.at(V, "gates"))
                ps = bank(V, "gates")
                dve.wait_ge(params_loaded, params_count(V))
                ts(g4[:, 0, :], ps[0:NR, 0:SEQ], ibias[0:NR], None, ALU.add).then_inc(vector_done, V.step())
                dve.wait_ge(vector_done, V.now())
                ts(g4[:, 1, :], ps[0:NR, SEQ:2 * SEQ], fbias[0:NR], None, ALU.add).then_inc(vector_done, V.step(("read", "gates")))
                dve.wait_ge(vector_done, V.now())
                stt(g4[:, 5, :], g4[:, 1, :], -1.0, g4[:, 1, :], ALU.mult, ALU.min).then_inc(vector_done, V.step("negabs"))
                dve.wait_ge(vector_done, V.now())
                ts(g4[:, 1, :], g4[:, 1, :], 0.0, None, ALU.min).then_inc(vector_done, V.step())
                dve.wait_ge(vector_done, V.now())

            def conv(b):
                if b % 2 == 0:
                    dve.wait_ge(scalar_done, A.at(V, ("mqk", "c", b // 2)))
                o = qkT[:, b, :]
                ts(o, cin[:, b, 0:SEQ], convw[:, b, 0:1], convw[:, b, CONV:CONV + 1], ALU.mult, ALU.add).then_inc(vector_done, V.step())
                dve.wait_ge(vector_done, V.now())
                for j in range(1, CONV):
                    stt(o, cin[:, b, j:j + SEQ], convw[:, b, j:j + 1], o, ALU.mult, ALU.add).then_inc(vector_done, V.step("conv" if b == 3 and j == CONV - 1 else None))
                    dve.wait_ge(vector_done, V.now())

            def gate_sums():
                dve.wait_ge(scalar_done, A.at(V, "softplus"))
                tt(g4[:, 4, :], g4[:, 1, :], g4[:, 5, :], ALU.subtract).then_inc(vector_done, V.step())
                dve.wait_ge(vector_done, V.now())
                nc.vector.tensor_tensor_scan(g4[:, 1, :], ones[0:NR, 0:SEQ], g4[:, 4, :], 0.0, ALU.mult, ALU.add).then_inc(vector_done, V.step())
                dve.wait_ge(vector_done, V.now())
                tt(g4[:, 2, :], g4[:, 0, :], g4[:, 1, :], ALU.subtract).then_inc(vector_done, V.step())
                dve.wait_ge(vector_done, V.now())
                nc.vector.tensor_tensor_scan(g4[:, 3, :], g4[:, 2, :], g4[:, 2, :], 0.0, ALU.max, ALU.max).then_inc(vector_done, V.step())
                dve.wait_ge(vector_done, V.now())
                tt(g4[:, 4, :], g4[:, 1, :], g4[:, 3, :], ALU.add).then_inc(vector_done, V.step("bm"))
                dve.wait_ge(vector_done, V.now())


            for t in range(TT):
                rope_chunk("idx", t, NI + 1)
                scale_iw(t)
            for t in range(TT):
                rope_chunk("aq", t, NA)
            ada(4)
            dve.wait_ge(tables_loaded, 16 * 4)
            top_k(0)
            for t in range(TT):
                rope_chunk("ak", t, NA)
            ada(5)
            top_k(1)
            rope_chunk("rqk", 0, 2 * NR)
            att_in(0)
            att_in(1)
            rope_chunk("rqk", 1, 2 * NR)
            for s in range(len(ATT)):
                if s == 0:
                    gate_row(4)
                if s < 2:
                    ada(6 + s)
                if s == 2:
                    shift_columns(6, 2)
                    ada(8)
                if s == 3:
                    gate_rows()
                    ada(9)
                if s == 4:
                    att_out(0)
                    ret_weights(0)
                    ret_weights(1)
                if s == 5:
                    ret_weights(2)
                    ret_weights(3)
                    conv(0)
                    conv(1)
                    shift_columns(8, 3)
                if s == 6:
                    dve.wait_ge(tensor_done, T.at(V, ("ret", "PV", NR - 1)))
                    nc.vector.tensor_copy(hn.rearrange("p h d -> p (h d)"), bank(V, ("ret", "O"))).then_inc(vector_done, V.step(("read", ("ret", "O"))))
                    dve.wait_ge(vector_done, V.now())
                    conv(2)
                    conv(3)
                if s == 7:
                    gate_sums()
                if s + 2 < len(ATT):
                    att_in(s + 2)
            att_out(1)
            head_variance("ret")

            dve.wait_ge(tensor_done, T.at(V, "gcol"))
            ps = bank(V, "gcol")
            nc.vector.tensor_copy(gcol, ps[:, 0:16]).then_inc(vector_done, V.step(("read", "gcol")))
            dve.wait_ge(vector_done, V.now())

            for h in range(NR):
                dve.wait_ge(tensor_done, T.at(V, ("ml", "M", h)))
                ps = bank(V, ("ml", "M", h))
                if h >= 2:
                    dve.wait_ge(tensor_done, T.at(V, ("ml", "PV", h - 2)))
                ca = cblock[:, C1["causal"]:C1["causal"] + SEQ]
                stt(wT[:, h % 2, 0:SEQ], ps[:, 0:SEQ], gcol[:, h:h + 1], ca, ALU.add, ALU.add).then_inc(vector_done, V.step())
                dve.wait_ge(vector_done, V.now())
                stt(wT[:, h % 2, SEQ:384], ps[:, P:SEQ], gcol[:, 8 + h:9 + h], ca[:, 0:P], ALU.add, ALU.add).then_inc(vector_done, V.step(("ml", "arg", h)))
                dve.wait_ge(vector_done, V.now())
                V.also(("read", ("ml", "M", h)))
                dve.wait_ge(tensor_done, T.at(V, ("ml", "S", h)))
                ps = bank(V, ("ml", "S", h))
                dve.wait_ge(scalar_done, A.at(V, ("ml", "exp", h)))
                stt(sT[:, h % 2, :], ps[:, 0:384], HD ** -0.5, wT[:, h % 2, :], ALU.mult, ALU.mult).then_inc(vector_done, V.step(("ml", "sT", h)))
                dve.wait_ge(vector_done, V.now())
                V.also(("read", ("ml", "S", h)))
            head_normed("ret")
            dve.wait_ge(scalar_done, A.at(V, "rg"))
            tt(o_cat[:, :, 512:768], sq.rearrange("p (t h) d -> p t (h d)", t=TT), rg, ALU.mult).then_inc(vector_done, V.step())
            dve.wait_ge(vector_done, V.now())
            dve.wait_ge(tensor_done, T.at(V, ("ml", "PV", NR - 1)))
            dve.wait_ge(scalar_done, A.at(V, "mo"))
            for t in range(TT):
                ps = bank(V, ("ml", "O", t))
                o = ps[:, 0:NR * (HD + 1)].rearrange("p (h d) -> p h d", h=NR)
                nc.vector.tensor_copy(den, o[:, :, HD:HD + 1]).then_inc(vector_done, V.step())
                dve.wait_ge(vector_done, V.now())
                stt(hv[:, 0:NR], den, -1.0, den, ALU.mult, ALU.max).then_inc(vector_done, V.step())
                dve.wait_ge(vector_done, V.now())
                tt(hv[:, 0:NR], hv[:, 0:NR], gcol[:, 8 * t + NR:8 * t + 2 * NR], ALU.max).then_inc(vector_done, V.step())
                dve.wait_ge(vector_done, V.now())
                nc.vector.reciprocal(hs[:, 0:NR], hv[:, 0:NR]).then_inc(vector_done, V.step())
                dve.wait_ge(vector_done, V.now())
                tt(hn[:, NR * t:NR * (t + 1), :], o[:, :, 0:HD], over(hs[:, 0:NR], NR, HD), ALU.mult).then_inc(vector_done, V.step(("read", ("ml", "O", t))))
                dve.wait_ge(vector_done, V.now())
            hflat = hn.rearrange("p (t h) d -> p t (h d)", t=TT)
            tt(hflat, hflat, mo, ALU.mult).then_inc(vector_done, V.step())
            dve.wait_ge(vector_done, V.now())
            head_variance("ml")
            head_normed("ml")
            nc.vector.tensor_copy(o_cat[:, :, 768:1024], sq.rearrange("p (t h) d -> p t (h d)", t=TT)).then_inc(vector_done, V.step("o_cat"))
            dve.wait_ge(vector_done, V.now())
            ada(10)

            def residual(ps, t, h, read, gated):
                o = x[:, t, h * N:(h + 1) * N]
                tt(gated, ps, gb[:, h * N:(h + 1) * N], ALU.mult).then_inc(vector_done, V.step(read))
                dve.wait_ge(vector_done, V.now())
                stt(o, o, ALPHA, gated, ALU.mult, ALU.add).then_inc(vector_done, V.step())
                dve.wait_ge(vector_done, V.now())

            dve.wait_ge(gains_loaded, gains_count(V))
            for t in range(TT):
                for h in range(2):
                    dve.wait_ge(tensor_done, T.at(V, ("wo", t, h)))
                    residual(bank(V, ("wo", t, h)), t, h, ("read", ("wo", t, h)), hn.rearrange("p h d -> p (h d)"))
                moments("ln1", t)
                if t == 0:
                    ada(11)
                layer_norm("ln1", t)
            V.also("ln1")
            gate_row(10)
            weights_rest(0, None, ("w_hi", 0), ("parts", 0))
            modulated("xT2", "hT2", mod[3], mod[2], parts=True)

            dve.wait_ge(scalar_done, A.at(V, "router"))
            v3 = lambda a, n: a.rearrange("p (t n) -> p t n", n=n)
            tt(v3(biased, NE), v3(scores, NE), br[:, :].unsqueeze(1).to_broadcast([P, TT, NE]), ALU.add).then_inc(vector_done, V.step())
            dve.wait_ge(vector_done, V.now())
            b4, pr = v3(biased, EG), v3(pairs, 6)
            tt(pr[:, :, 0:2], b4[:, :, 0:2], b4[:, :, 2:4], ALU.add).then_inc(vector_done, V.step())
            dve.wait_ge(vector_done, V.now())
            tt(pr[:, :, 2:4], b4[:, :, 0:4:2], b4[:, :, 1:4:2], ALU.add).then_inc(vector_done, V.step())
            dve.wait_ge(vector_done, V.now())
            tt(pr[:, :, 4:5], b4[:, :, 0:1], b4[:, :, 3:4], ALU.add).then_inc(vector_done, V.step())
            dve.wait_ge(vector_done, V.now())
            tt(pr[:, :, 5:6], b4[:, :, 1:2], b4[:, :, 2:3], ALU.add).then_inc(vector_done, V.step())
            dve.wait_ge(vector_done, V.now())
            vmax(gsum, pr).then_inc(vector_done, V.step())
            dve.wait_ge(vector_done, V.now())

            def first_best(o, src, key, n, weights):
                vmax(t2, v3(src, n)).then_inc(vector_done, V.step())
                dve.wait_ge(vector_done, V.now())
                tt(v3(key, n), v3(src, n), over(t2, TT, n), ALU.is_equal).then_inc(vector_done, V.step())
                dve.wait_ge(vector_done, V.now())
                tt(v3(key, n), v3(key, n), weights.unsqueeze(1).to_broadcast([P, TT, n]), ALU.mult).then_inc(vector_done, V.step())
                dve.wait_ge(vector_done, V.now())
                vmax(t2, v3(key, n)).then_inc(vector_done, V.step())
                dve.wait_ge(vector_done, V.now())
                tt(v3(o, n), v3(key, n), over(t2, TT, n), ALU.is_equal).then_inc(vector_done, V.step())
                dve.wait_ge(vector_done, V.now())

            first4 = cshared[:, CONST["first4"]:CONST["first4"] + NG]
            first16 = cshared[:, CONST["first16"]:CONST["first16"] + NE]
            first_best(gsum, gsum, key4, NG, first4)
            ts(gsum, gsum, -1.0, BIG, ALU.add, ALU.mult).then_inc(vector_done, V.step())
            dve.wait_ge(vector_done, V.now())
            tt(v3(bmask, EG), b4, over(gsum, 8, EG), ALU.add).then_inc(vector_done, V.step())
            dve.wait_ge(vector_done, V.now())
            first_best(sel, bmask, onehot, NE, first16)
            stt(bmask, sel, -BIG, bmask, ALU.mult, ALU.add).then_inc(vector_done, V.step())
            dve.wait_ge(vector_done, V.now())
            first_best(biased, bmask, onehot, NE, first16)
            tt(sel, sel, biased, ALU.add).then_inc(vector_done, V.step())
            dve.wait_ge(vector_done, V.now())
            tt(gate, sel, scores, ALU.mult).then_inc(vector_done, V.step())
            dve.wait_ge(vector_done, V.now())
            vsum(t2, v3(gate, NE)).then_inc(vector_done, V.step())
            dve.wait_ge(vector_done, V.now())
            nc.vector.reciprocal(t2, t2).then_inc(vector_done, V.step())
            dve.wait_ge(vector_done, V.now())
            tt(v3(gate, NE), v3(gate, NE), over(t2, TT, NE), ALU.mult).then_inc(vector_done, V.step())
            dve.wait_ge(vector_done, V.now())
            dve_experts(NE, True)
            dve.wait_ge(vector_done, V.now())
            dve.wait_ge(rows_loaded, rows_count(V))
            for t in range(TT):
                dve.wait_ge(tensor_done, T.at(V, ("dn0", NE - 1) if t == 0 else ("dn1", NE - 1)))
                for h in range(2):
                    residual(psum[:, 4 + 2 * t + h, :], t, h, None, tmp[:, h, :])
                moments("ln2", t)
                if t:
                    layer_norm("ln2", 0)
            layer_norm("ln2", 1)
            V.end()

        def rms(name, t, halves):
            dve.wait_ge(scalar_done, A.at(V, (name, "ss", t)))
            total = agg[:, 2 * t:2 * t + 1]
            if halves:
                tt(total, total, agg[:, 2 * t + 1:2 * t + 2], ALU.add).then_inc(vector_done, V.step())
                dve.wait_ge(vector_done, V.now())
            ts(rstd[:, t:t + 1], total, 1.0 / D, RMS_EPS, ALU.mult, ALU.add).then_inc(vector_done, V.step((name, "var", t)))
            dve.wait_ge(vector_done, V.now())
            dve.wait_ge(scalar_done, A.at(V, (name, "sqrt", t)))
            nc.vector.reciprocal(rstd[:, TT + t:TT + t + 1], rstd[:, t:t + 1]).then_inc(vector_done, V.step())
            dve.wait_ge(vector_done, V.now())

        def pre_norm(name):
            for t in range(TT):
                rms(("pre", name), t, False)
                ts(o_cat[:, t, :], x[:, t, :], rstd[:, TT + t:TT + t + 1], None, ALU.mult).then_inc(vector_done, V.step(("xn", name, t)))
                dve.wait_ge(vector_done, V.now())

        def post_norm(name, row, banks):
            for t in range(TT):
                rms(("post", name), t, True)
                for h in range(2):
                    ps, read = banks(t, h)
                    stt(y2[:, t, h * N:(h + 1) * N], ps, rstd[:, TT + t:TT + t + 1], rows[:, row, h * N:(h + 1) * N], ALU.mult, ALU.mult).then_inc(vector_done, V.step(read))
                dve.wait_ge(vector_done, V.now())
                tt(x[:, t, :], x[:, t, :], y2[:, t, :], ALU.add).then_inc(vector_done, V.step(("x", name, t)))
                dve.wait_ge(vector_done, V.now())

        def dve_second(l):
            V.begin(1, l)
            dve.wait_ge(scalar_done, A.before(V))
            dve.wait_ge(tensor_done, T.before(V))
            pre_norm("mix")
            dve.wait_ge(tensor_done, T.at(V, "gains"))
            ps = bank(V, "gains")
            nc.vector.tensor_copy(gcols, ps[:, 0:3 * KT + GG]).then_inc(vector_done, V.step(("read", "gains")))
            dve.wait_ge(vector_done, V.now())
            modulated("xT", "hT", gcols)
            dve.wait_ge(params_loaded, params_count(V))
            dve.wait_ge(const_loaded, 16)
            lq = lprod.rearrange("p (a d) -> p a d", a=2)
            tt(lq, lamrow[:, 0:2, :], lamrow[:, 2:4, :], ALU.mult).then_inc(vector_done, V.step())
            dve.wait_ge(vector_done, V.now())
            vsum(lsum, lq).then_inc(vector_done, V.step("lsum"))
            dve.wait_ge(vector_done, V.now())
            ts(subrow, subrow, lamc[:, 1:2], None, ALU.mult).then_inc(vector_done, V.step())
            dve.wait_ge(vector_done, V.now())
            dve.wait_ge(scalar_done, A.at(V, "lexp"))
            tt(lam, lsum[:, 0:1], lsum[:, 1:2], ALU.subtract).then_inc(vector_done, V.step())
            dve.wait_ge(vector_done, V.now())
            tt(lam, lam, lamc[:, 0:1], ALU.add).then_inc(vector_done, V.step())
            dve.wait_ge(vector_done, V.now())
            def gate_moments():
                for t in range(TT):
                    dve.wait_ge(scalar_done, A.at(V, ("buv", "c", t)))
                    nc.vector.bn_stats(st[:, 0:6], buv[:, t, GW:2 * GW]).then_inc(vector_done, V.step())
                    dve.wait_ge(vector_done, V.now())
                    dve.sem_inc(waited)
                    nc.vector.bn_aggr(agg[:, 2 * t:2 * t + 2], st[:, 0:6]).then_inc(vector_done, V.step())
                    dve.wait_ge(vector_done, V.now())
                    ts(rstd[:, t:t + 1], agg[:, 2 * t + 1:2 * t + 2], RMS_EPS, None, ALU.add).then_inc(vector_done, V.step(("vn", "var") if t else None))
                    dve.wait_ge(vector_done, V.now())

            def gate_norm():
                dve.wait_ge(scalar_done, A.at(V, ("vn", "sqrt")))
                nc.vector.reciprocal(rstd[:, TT:2 * TT], rstd[:, 0:TT]).then_inc(vector_done, V.step())
                dve.wait_ge(vector_done, V.now())
                for t in range(TT):
                    ts(vn[:, t, :], buv[:, t, GW:2 * GW], agg[:, 2 * t:2 * t + 1], rstd[:, TT + t:TT + t + 1], ALU.subtract, ALU.mult).then_inc(vector_done, V.step())
                    dve.wait_ge(vector_done, V.now())
                    tt(vn[:, t, :], vn[:, t, :], glnrow[:, 0, :], ALU.mult).then_inc(vector_done, V.step())
                    dve.wait_ge(vector_done, V.now())
                    tt(vn[:, t, :], vn[:, t, :], glnrow[:, 1, :], ALU.add).then_inc(vector_done, V.step(("vn", t)))
                    dve.wait_ge(vector_done, V.now())

            def diff_in(s):
                t, h = DIFF[s]
                dve.wait_ge(tensor_done, T.at(V, ("diff", "S", s)))
                ps = bank(V, ("diff", "S", s))
                dist = cblock[:, t * SEQ:(t + 1) * SEQ].unsqueeze(1).to_broadcast([P, 2, SEQ])
                o = sm2[:, s % 3, :].rearrange("p (c k) -> p c k", c=2)
                stt(o, dist, -DIFF_SLOPES[h], ps[:, :, 0:SEQ], ALU.mult, ALU.add).then_inc(vector_done, V.step(("read", ("diff", "S", s))))
                dve.wait_ge(vector_done, V.now())
                nc.vector.tensor_reduce(ngm[:, 2 * (s % 3):2 * (s % 3) + 2], o, AX.X, ALU.max, negate=True).then_inc(vector_done, V.step(("diff", "max", s)))

            def diff_out(s):
                dve.wait_ge(scalar_done, A.at(V, ("diff", "exp", s)))
                r = rsum[:, 2 * (s % 3):2 * (s % 3) + 2]
                nc.vector.reciprocal(r2, r).then_inc(vector_done, V.step())
                dve.wait_ge(vector_done, V.now())
                tt(r2[:, 1:2], r2[:, 1:2], lam, ALU.mult).then_inc(vector_done, V.step())
                dve.wait_ge(vector_done, V.now())
                p0, p1 = sm2[:, s % 3, 0:SEQ], sm2[:, s % 3, SEQ:2 * SEQ]
                ts(p1, p1, r2[:, 1:2], None, ALU.mult).then_inc(vector_done, V.step())
                dve.wait_ge(vector_done, V.now())
                if s >= 2:
                    dve.wait_ge(tensor_done, T.at(V, ("diff", "PT", s - 2)))
                stt(at2[:, s % 2, :], p0, r2[:, 0:1], p1, ALU.mult, ALU.subtract).then_inc(vector_done, V.step(("diff", "at", s)))
                dve.wait_ge(vector_done, V.now())

            for s in range(3):
                diff_in(s)
            dve.wait_ge(vector_done, V.now())
            for s in range(len(DIFF)):
                if s == 4:
                    gate_moments()
                if s == 6:
                    gate_norm()
                diff_out(s)
                if s + 3 < len(DIFF):
                    diff_in(s + 3)
                    dve.wait_ge(vector_done, V.now())

            def diff_norm():
                for t in range(TT):
                    dve.wait_ge(tensor_done, T.at(V, ("diff", "PV", (t + 1) * DH - 1)))
                    nc.vector.tensor_copy(hn2[:, t * DH:(t + 1) * DH, :], bank(V, ("diff", "O", t))[:, 0:DH * HD].rearrange("p (h d) -> p h d", h=DH)).then_inc(vector_done, V.step(("read", ("diff", "O", t))))
                dve.wait_ge(vector_done, V.now())
                tt(sq2, hn2, hn2, ALU.mult).then_inc(vector_done, V.step())
                dve.wait_ge(vector_done, V.now())
                vsum(hv2, sq2).then_inc(vector_done, V.step())
                dve.wait_ge(vector_done, V.now())
                ts(hv2, hv2, 1.0 / HD, RMS_EPS, ALU.mult, ALU.add).then_inc(vector_done, V.step(("diff", "var")))
                dve.wait_ge(vector_done, V.now())
                dve.wait_ge(scalar_done, A.at(V, ("diff", "sqrt")))
                nc.vector.reciprocal(hs2, hv2).then_inc(vector_done, V.step())
                dve.wait_ge(vector_done, V.now())
                tt(hn2, hn2, over(hs2, TT * DH, HD), ALU.mult).then_inc(vector_done, V.step())
                dve.wait_ge(vector_done, V.now())
                for t in range(TT):
                    tt(o_cat[:, t, 0:DH * HD].rearrange("p (h d) -> p h d", h=DH), hn2[:, t * DH:(t + 1) * DH, :], subrow.unsqueeze(1).to_broadcast([P, DH, HD]), ALU.mult).then_inc(vector_done, V.step())
                dve.wait_ge(vector_done, V.now())

            wscale = HD ** -0.5

            def win_in(s):
                t, g = WIN[s]
                dve.wait_ge(tensor_done, T.at(V, ("win", "S", s)))
                ps = bank(V, ("win", "S", s))
                if s >= 3:
                    dve.wait_ge(tensor_done, T.at(V, ("win", "PT", s - 3)))
                wd = cblock[:, C2["wdist"] + t * SEQ:C2["wdist"] + (t + 1) * SEQ]
                for h in range(2):
                    stt(sm2[:, s % 3, h * SEQ:(h + 1) * SEQ], wd, -SWA_SLOPES[h * WG + g] / wscale, ps[:, h, 0:SEQ], ALU.mult, ALU.add).then_inc(vector_done, V.step(("read", ("win", "S", s)) if h else None))
                    dve.wait_ge(vector_done, V.now())
                vmax(nm2, sm2[:, s % 3, :].rearrange("p (h k) -> p h k", h=2)).then_inc(vector_done, V.step())
                dve.wait_ge(vector_done, V.now())
                sk = sinks[:, g:g + WG + 1:WG]
                stt(msink, nm2, wscale, sk, ALU.mult, ALU.max).then_inc(vector_done, V.step())
                dve.wait_ge(vector_done, V.now())
                c = t * WH + g
                tt(dsum[:, c:c + WG + 1:WG], sk, msink, ALU.subtract).then_inc(vector_done, V.step())
                dve.wait_ge(vector_done, V.now())
                ts(ngm[:, 2 * (s % 3):2 * (s % 3) + 2], msink, -1.0, None, ALU.mult).then_inc(vector_done, V.step(("win", "max", s)))
                dve.wait_ge(vector_done, V.now())

            for s in range(3):
                win_in(s)
            diff_norm()
            dve.wait_ge(tensor_done, T.at(V, "mix"))
            ps = bank(V, "mix")
            for g in range(GG):
                stt(o_cat[:, :, 384 + g * HD:384 + (g + 1) * HD], ps[:, g * P:(g + 1) * P].rearrange("p (t d) -> p t d", t=TT), gcols[:, 3 * KT + g:3 * KT + g + 1], buv[:, :, g * HD:(g + 1) * HD], ALU.add, ALU.mult).then_inc(vector_done, V.step(("read", "mix") if g == GG - 1 else None))
                dve.wait_ge(vector_done, V.now())

            for s in range(3, len(WIN)):
                win_in(s)

            def win_out(t):
                dve.wait_ge(scalar_done, A.at(V, ("win", "sink", t)))
                tt(rinv[:, 0:WH], dsum[:, t * WH:(t + 1) * WH], rsum[:, t * NA:t * NA + WH], ALU.add).then_inc(vector_done, V.step())
                dve.wait_ge(vector_done, V.now())
                nc.vector.reciprocal(rinv[:, WH:2 * WH], rinv[:, 0:WH]).then_inc(vector_done, V.step())
                dve.wait_ge(vector_done, V.now())
                dve.wait_ge(tensor_done, T.at(V, ("win", "PV", (t + 1) * WG - 1)))
                tt(o_cat[:, t, 640:1024].rearrange("p (h d) -> p h d", h=WH), bank(V, ("win", "O", t))[:, 0:WH * HD].rearrange("p (h d) -> p h d", h=WH), over(rinv[:, WH:2 * WH], WH, HD), ALU.mult).then_inc(vector_done, V.step(("read", ("win", "O", t))))
                dve.wait_ge(vector_done, V.now())

            win_out(0)
            win_out(1)
            V.also("o_cat")
            weights_rest(0, None, ("w_hi", 0), ("parts", 0))
            dve.wait_ge(gains_loaded, gains_count(V))
            post_norm("mix", 0, lambda t, h: (bank(V, ("wo", t, h)), ("read", ("wo", t, h))))
            pre_norm("ffn")
            modulated("xT2", "hT2", gcols[:, KT:2 * KT], parts=True)
            dve_experts(NF, False)
            dve.wait_ge(vector_done, V.now())
            post_norm("ffn", 1, lambda t, h: (psum[:, 4 + 2 * t + h, :], ("read", ("acc", 2 * t + h))))
            pre_norm("ple")
            modulated("xT3", "hT3", gcols[:, 2 * KT:3 * KT])
            for t in range(TT):
                for h in range(2):
                    dve.wait_ge(scalar_done, A.at(V, ("sig", t, h)))
                    o = y2[:, t, h * N:(h + 1) * N]
                    e = (e2 if t == 0 else e2b)[:, h * N:(h + 1) * N]
                    tt(o, o, e, ALU.mult).then_inc(vector_done, V.step(("eg", t) if h else None))
            dve.wait_ge(vector_done, V.now())
            dve.wait_ge(rows_loaded, rows_count(V))
            for t in range(TT):
                rms(("post", "ple"), t, False)
                stt(y2[:, t, :], y2[:, t, :], rstd[:, TT + t:TT + t + 1], rows[:, 0, :], ALU.mult, ALU.mult).then_inc(vector_done, V.step())
                dve.wait_ge(vector_done, V.now())
                tt(x[:, t, :], x[:, t, :], y2[:, t, :], ALU.add).then_inc(vector_done, V.step())
                dve.wait_ge(vector_done, V.now())
            V.end()

        @block.vector
        def _(dve):
            nc.vector.memset(ones[:, :], 1.0).then_inc(vector_done, V.step())
            dve.wait_ge(vector_done, V.now())
            nc.vector.memset(zeros[:, :], 0.0).then_inc(vector_done, V.step())
            dve.wait_ge(vector_done, V.now())
            nc.vector.memset(cin, 0.0).then_inc(vector_done, V.step())
            dve.wait_ge(vector_done, V.now())
            nc.vector.memset(mv, 1.0).then_inc(vector_done, V.step())
            dve.wait_ge(vector_done, V.now())
            dve.wait_ge(start_loaded, 16 * 3)
            dve.wait_ge(scalar_done, A.at(V, "sigc"))
            tt(cact[:, :], cact[:, :], psum[:, 0, 0:KT], ALU.mult).then_inc(vector_done, V.step("cact"))
            dve.wait_ge(vector_done, V.now())
            nc.vector.tensor_copy(posf, posi[:, :]).then_inc(vector_done, V.step())
            dve.wait_ge(vector_done, V.now())
            invf = cshared[:, CONST["invf"]:CONST["invf"] + HALF]
            c1 = 6.28125
            c2 = float(np.float32(np.float16(TWO_PI - c1)))
            c3 = TWO_PI - c1 - c2
            for t in range(TT):
                ang, k, r = tmp[:, 0, 0:HALF], tmp[:, 0, HALF:HD], tmp[:, 1, 0:HALF]
                ts(ang, invf, posf[:, t:t + 1], None, ALU.mult).then_inc(vector_done, V.step())
                dve.wait_ge(vector_done, V.now())
                for cos in (0, 1):
                    ts(k, ang, 1.0 / TWO_PI, 0.25 * cos, ALU.mult, ALU.add).then_inc(vector_done, V.step())
                    dve.wait_ge(vector_done, V.now())
                    ts(k, k, ROUND, None, ALU.add).then_inc(vector_done, V.step())
                    dve.wait_ge(vector_done, V.now())
                    ts(k, k, -ROUND, None, ALU.add).then_inc(vector_done, V.step())
                    dve.wait_ge(vector_done, V.now())
                    stt(r, k, -c1, ang, ALU.mult, ALU.add).then_inc(vector_done, V.step())
                    dve.wait_ge(vector_done, V.now())
                    for c in (c2, c3):
                        stt(r, k, -c, r, ALU.mult, ALU.add).then_inc(vector_done, V.step())
                        dve.wait_ge(vector_done, V.now())
                    ts(r, r, np.pi / 2 * cos, None, ALU.add).then_inc(vector_done, V.step())
                    dve.wait_ge(vector_done, V.now())
                    o = (cosf if cos else sinf)[:, t, HALF:HD]
                    ts(o, r, -3.141592, 3.141592, ALU.max, ALU.min).then_inc(vector_done, V.step(("angle", t, cos)))
                    dve.wait_ge(vector_done, V.now())
            dve.wait_ge(scalar_done, A.at(V, "trig"))
            for t in range(TT):
                nc.vector.tensor_copy(cosf[:, t, 0:HALF], cosf[:, t, HALF:HD]).then_inc(vector_done, V.step())
                dve.wait_ge(vector_done, V.now())
                ts(sinf[:, t, 0:HALF], sinf[:, t, HALF:HD], -1.0, None, ALU.mult).then_inc(vector_done, V.step(("rope_tables") if t else None))
                dve.wait_ge(vector_done, V.now())
            with dve.Fori(0, DEPTH) as l:
                dve_first(l)
            with dve.Fori(0, DEPTH) as l:
                dve_second(l)

        def activate(o, a, f, **k):
            return nc.scalar.activation(o, a, f, **k)

        def copy(o, a):
            return nc.scalar.activation(o, a, ACT.Copy)

        def rounded_weights(e, i, more, name):
            act.wait_ge(G.sem(A, f"gu{e}"), G.level(A, f"gu{e}", more))
            w = gslot(A.block, f"gu{e}")
            for q in range(2):
                k = slice(q * KT // 2, (q + 1) * KT // 2)
                copy(w_hi[e % 2][:, k, :], w[:, k, 0:N]).then_inc(scalar_done, A.step(("w_hi", *name, q)))

        def modulated_T(tag, name, scale, shift=None, parts=False):
            for g in range(KT // 2):
                if g % 2:
                    act.wait_ge(tensor_done, T.at(A, (tag, g)))
                    for f in range(2):
                        k = 2 * g + f
                        ps = bank(A, (tag, g))[:, f * SEQ:(f + 1) * SEQ]
                        if shift is None:
                            activate(hT[:, k, :], ps, ACT.Copy, scale=scale[:, k:k + 1]).then_inc(scalar_done, A.step((name, g) if f else None))
                        else:
                            activate(hT[:, k, :], ps, ACT.Identity, scale=scale[:, k:k + 1], bias=shift[:, k:k + 1]).then_inc(scalar_done, A.step((name, g) if f else None))
                    A.also(("read", (tag, g)))
                if parts:
                    if g % 2:
                        act.wait_ge(scalar_done, A.now())
                    else:
                        act.wait_ge(vector_done, V.at(A, (name, g)))
                    copy(h_hi[A.block][:, 2 * g:2 * g + 2, :], hT[:, 2 * g:2 * g + 2, :]).then_inc(scalar_done, A.step((name, "hi", g)))

        def act_experts(ne):
            n = NIT[ne]

            def one(e, i, i0, more, gu0, gu1, step, following):
                act.wait_ge(tensor_done, T.at(A, gu0, i0))
                activate(sact[:, 0, :], psum[:, 0, 0:FE], ACT.Silu).then_inc(scalar_done, A.step(("silu", *step, 0)))
                if following is not None:
                    rounded_weights(e + 1, i, more, following)
                act.wait_ge(DN.sem(A, f"dn{e}"), DN.level(A, f"dn{e}", more))
                copy(d_hi[e % 2], dslot(A.block, f"dn{e}")).then_inc(scalar_done, A.step(("d_hi", *step)))
                act.wait_ge(tensor_done, T.at(A, gu1, i))
                activate(sact[:, 1, :], psum[:, 1, 0:FE], ACT.Silu).then_inc(scalar_done, A.step(("silu", *step, 1)))
                for t in range(TT):
                    act.wait_ge(tensor_done, T.at(A, ("tr", *step, t), i))
                    copy(hidT[:, t, :, :].rearrange("p f n -> p (f n)"), psum[:, 2 + t, 0:FE]).then_inc(scalar_done, A.step(("hidT", *step, t)))

            one(0, None, None, 0, ("gu0", 0), ("gu1", 0), (0,), (1,))
            with nc.scalar.Fori(0, n) as i:
                A.loop(f"act{A.block}", n)
                for j in range(4):
                    gu0, i0 = (("gu0", "loop", j - 1), i) if j else (("gu0", "loop", 3), i - 1)
                    one(1 + j, i, i0, i * 32, gu0, ("gu1", "loop", j), ("loop", j), ("loop", j))
                A.loop_end()
            for e in range(1 + 4 * n, ne):
                gu0, i0 = (("gu0", "loop", 3), n - 1) if e == 1 + 4 * n else (("gu0", e), None)
                one(e, None, i0, 0, gu0, ("gu1", e), (e,), (e + 1,) if e + 1 < ne else None)

        def root_of(name, var, *t):
            act.wait_ge(vector_done, V.at(A, (name, "var", *t)))
            activate(var, var, ACT.Sqrt).then_inc(scalar_done, A.step((name, "sqrt", *t)))
            act.wait_ge(scalar_done, A.now())

        def act_first(l):
            A.begin(0, l)

            def ada_copy(c):
                act.wait_ge(tensor_done, T.at(A, ("ada", c)))
                copy(arow[c % 2], bank(A, ("ada", c))[0:1, :]).then_inc(scalar_done, A.step(("arow", c)))
                A.also(("read", ("ada", c)))

            ada_copy(2)
            ada_copy(3)
            act.wait_ge(vector_done, V.at(A, ("read", ("columns", 0))))
            modulated_T("xT", "hT", mod[1], mod[0])

            def rows_T(name, dst, blocks):
                for t in range(TT):
                    act.wait_ge(tensor_done, T.at(A, (name, "T", t)))
                    ps = bank(A, (name, "T", t))
                    copy(dst[:, 0:blocks, t * P:(t + 1) * P], ps[:, 0:blocks * P].rearrange("p (b n) -> p b n", b=blocks)).then_inc(scalar_done, A.step((name, "Tc", t)))
                    act.wait_ge(scalar_done, A.now())
                    A.also(("read", (name, "T", t)))

            rows_T("idx", idxT, 3)

            def relu(t):
                nk = (t + 1) * P
                if t:
                    act.wait_ge(vector_done, V.at(A, ("rel_read", t - 1)))
                act.wait_ge(tensor_done, T.at(A, ("idxS", t)))
                ps = bank(A, ("idxS", t))
                for h in range(2):
                    activate(rel[:, 2 * h:2 * h + 2, 0:nk], ps[:, h, :].rearrange("p (i k) -> p i k", i=2)[:, :, 0:nk], ACT.Relu).then_inc(scalar_done, A.step(("rel", t) if h else None))
                    act.wait_ge(scalar_done, A.now())
                A.also(("read", ("idxS", t)))

            def copied(name, dst, t):
                act.wait_ge(tensor_done, T.at(A, (name, t)))
                copy(dst, bank(A, (name, t))[:, 0:N]).then_inc(scalar_done, A.step((name, t)))
                act.wait_ge(scalar_done, A.now())
                A.also(("read", (name, t)))

            def copied_mvo(t):
                act.wait_ge(tensor_done, T.at(A, ("mvo", t)))
                ps = bank(A, ("mvo", t))
                copy(mv[:, t, :, 0:HD], ps[:, 0:256].rearrange("p (h d) -> p h d", h=NR)).then_inc(scalar_done, A.step(("mvo", t)))
                act.wait_ge(scalar_done, A.now())
                copy(mo[:, t, :], ps[:, 256:512]).then_inc(scalar_done, A.step(("read", ("mvo", t))))
                act.wait_ge(scalar_done, A.now())

            def copied_mqk(b):
                act.wait_ge(tensor_done, T.at(A, ("mqk", b)))
                ps = bank(A, ("mqk", b))
                copy(cin[:, 2 * b:2 * b + 2, CONV - 1:CONV - 1 + SEQ], ps.rearrange("p (b n) -> p b n", b=2)).then_inc(scalar_done, A.step(("mqk", "c", b)))
                act.wait_ge(scalar_done, A.now())
                A.also(("read", ("mqk", b)))

            def att_exp(s):
                t, i = ATT[s]
                nk = (t + 1) * P
                act.wait_ge(vector_done, V.at(A, ("att", "max", s)))
                for h in range(2):
                    o = sm[:, s % 2, h * nk:(h + 1) * nk]
                    c = t * NA + 2 * i + h
                    activate(o, o, ACT.Exp, bias=ngm[:, 2 * (s % 2) + h:2 * (s % 2) + h + 1], accum_out=rsum[:, c:c + 1]).then_inc(scalar_done, A.step(("att", "exp", s) if h else None))
                    act.wait_ge(scalar_done, A.now())

            def att_probs_T(s):
                t, i = ATT[s]
                act.wait_ge(tensor_done, T.at(A, ("att", "PT", s)))
                ps = bank(A, ("att", "PT", s))
                if s >= 2:
                    act.wait_ge(tensor_done, T.at(A, ("att", "PV", s - 2)))
                n = 2 * (t + 1) * P
                copy(pT[:, s % 2, 0:n], ps[:, 0:n]).then_inc(scalar_done, A.step(("att", "pT", s)))
                act.wait_ge(scalar_done, A.now())
                A.also(("read", ("att", "PT", s)))

            relu(0)
            rows_T("aq", aqT, 4)
            relu(1)
            for t in range(TT):
                copied("av", av[:, t, :], t)
            rows_T("ak", akT, 4)
            att_exp(0)
            att_exp(1)
            for s in range(len(ATT)):
                if s < 2:
                    copied("rvg", rvg[:, s, :], s)
                if s == 1:
                    rows_T("rqk", rrT, 4)
                if s in (2, 3):
                    copied_mvo(s - 2)
                if s in (4, 5):
                    copied_mqk(s - 4)
                if s == 4:
                    act.wait_ge(vector_done, V.at(A, "negabs"))
                    activate(grow[0:NR, 5, :], grow[0:NR, 5, :], ACT.Exp).then_inc(scalar_done, A.step())
                    act.wait_ge(scalar_done, A.now())
                    activate(grow[0:NR, 5, :], grow[0:NR, 5, :], ACT.Ln, bias=ones[0:NR, 0:1]).then_inc(scalar_done, A.step("softplus"))
                    act.wait_ge(scalar_done, A.now())
                att_probs_T(s)
                if s + 2 < len(ATT):
                    att_exp(s + 2)
            act.wait_ge(vector_done, V.at(A, "bm"))
            activate(grow[0:NR, 5, :], grow[0:NR, 4, :], ACT.Exp, scale=-1.0).then_inc(scalar_done, A.step("erow"))
            act.wait_ge(scalar_done, A.now())
            act.wait_ge(vector_done, V.at(A, "conv"))
            activate(qkT, qkT, ACT.Silu).then_inc(scalar_done, A.step("conv"))
            activate(rg, rg, ACT.Silu).then_inc(scalar_done, A.step("rg"))
            activate(mo, mo, ACT.Sigmoid).then_inc(scalar_done, A.step("mo"))
            for h in range(NR):
                act.wait_ge(vector_done, V.at(A, ("ml", "arg", h)))
                activate(wT[:, h % 2, :], wT[:, h % 2, :], ACT.Exp).then_inc(scalar_done, A.step(("ml", "exp", h)))
                act.wait_ge(scalar_done, A.now())

            def copied_oT(g):
                act.wait_ge(tensor_done, T.at(A, ("oT", g)))
                copy(hT[:, 2 * g:2 * g + 2, :].rearrange("p f n -> p (f n)"), bank(A, ("oT", g))).then_inc(scalar_done, A.step(("oTc", g)))
                act.wait_ge(scalar_done, A.now())
                A.also(("read", ("oT", g)))

            root_of("ret", hv)
            copied_oT(0)
            copied_oT(1)
            root_of("ml", hv)
            for g in range(2, KT // 2):
                copied_oT(g)
            for t in range(TT):
                root_of("ln1", rstd[:, t:t + 1], t)
            rounded_weights(0, None, 0, (0,))
            act.wait_ge(vector_done, V.at(A, ("read", ("columns", 8))))
            modulated_T("xT2", "hT2", mod[3], mod[2], parts=True)
            act.wait_ge(tensor_done, T.at(A, "router"))
            ps = psum[:, 3, :]
            activate(scores, ps[:, 0:TT * NE], ACT.Sigmoid).then_inc(scalar_done, A.step("router"))
            act.wait_ge(scalar_done, A.now())
            act_experts(NE)
            act.wait_ge(scalar_done, A.now())
            for t in range(TT):
                root_of("ln2", rstd[:, t:t + 1], t)
            A.end()

        def sum_squares(name, t, src):
            activate(junk, src[:, t, :], ACT.Square, accum_out=agg[:, 2 * t:2 * t + 1]).then_inc(scalar_done, A.step((name, "ss", t)))
            act.wait_ge(scalar_done, A.now())
            root_of(name, rstd[:, t:t + 1], t)

        def sum_squares_of_banks(name, t, ready, banks):
            for h in range(2):
                act.wait_ge(tensor_done, T.at(A, ready(t, h)))
                activate(junk[:, h * N:(h + 1) * N], banks(t, h), ACT.Square, accum_out=agg[:, 2 * t + h:2 * t + h + 1]).then_inc(scalar_done, A.step((name, "ss", t) if h else None))
            act.wait_ge(scalar_done, A.now())
            root_of(name, rstd[:, t:t + 1], t)

        def act_second(l):
            A.begin(1, l)
            act.wait_ge(vector_done, V.before(A))
            act.wait_ge(tensor_done, T.before(A))
            for t in range(TT):
                sum_squares(("pre", "mix"), t, x)
            act.wait_ge(tensor_done, T.at(A, "ws"))
            ps = bank(A, "ws")
            copy(wsT.rearrange("p g n -> p (g n)"), ps).then_inc(scalar_done, A.step("wsT"))
            act.wait_ge(scalar_done, A.now())
            A.also(("read", "ws"))
            act.wait_ge(tensor_done, T.at(A, "p"))
            ps = bank(A, "p")
            copy(pTT.rearrange("p k n -> p (k n)"), ps).then_inc(scalar_done, A.step("pT"))
            act.wait_ge(scalar_done, A.now())
            A.also(("read", "p"))

            def features(name, dst, b, n, scale=1.0):
                act.wait_ge(tensor_done, T.at(A, (name, b)))
                ps = bank(A, (name, b))
                activate(dst[:, 2 * b:2 * b + n, :].rearrange("p f n -> p (f n)"), ps[:, 0:n * SEQ], ACT.Copy, scale=scale).then_inc(scalar_done, A.step((name, "c", b)))
                act.wait_ge(scalar_done, A.now())
                A.also(("read", (name, b)))

            def tokens(name, dst, t):
                act.wait_ge(tensor_done, T.at(A, (name, t)))
                ps = bank(A, (name, t))
                copy(dst[:, t, :], ps).then_inc(scalar_done, A.step((name, "c", t)))
                act.wait_ge(scalar_done, A.now())
                A.also(("read", (name, t)))

            act.wait_ge(vector_done, V.at(A, ("read", "gains")))
            modulated_T("xT", "hT", gcols)
            for b in range(2):
                features("aq", qT2, b, 2 - b, DQK ** -0.5)
            for b in range(2):
                features("ak", kT2, b, 2 - b)
            act.wait_ge(vector_done, V.at(A, "lsum"))
            activate(lsum, lsum, ACT.Exp).then_inc(scalar_done, A.step("lexp"))
            act.wait_ge(scalar_done, A.now())
            for t in range(TT):
                tokens("avcv", avcv, t)

            def probs_T(tag, s, n):
                act.wait_ge(tensor_done, T.at(A, (tag, "PT", s)))
                ps = bank(A, (tag, "PT", s))
                if s >= 2:
                    act.wait_ge(tensor_done, T.at(A, (tag, "PV", s - 2)))
                copy(pT2[:, s % 2, 0:n], ps[:, 0:n]).then_inc(scalar_done, A.step((tag, "pT", s)))
                act.wait_ge(scalar_done, A.now())
                A.also(("read", (tag, "PT", s)))

            def diff_exp(s):
                act.wait_ge(vector_done, V.at(A, ("diff", "max", s)))
                for c in range(2):
                    o = sm2[:, s % 3, c * SEQ:(c + 1) * SEQ]
                    k = 2 * (s % 3) + c
                    activate(o, o, ACT.Exp, bias=ngm[:, k:k + 1], accum_out=rsum[:, k:k + 1]).then_inc(scalar_done, A.step(("diff", "exp", s) if c else None))
                act.wait_ge(scalar_done, A.now())

            def win_exp(s):
                t, g = WIN[s]
                act.wait_ge(vector_done, V.at(A, ("win", "max", s)))
                for h in range(2):
                    o = sm2[:, s % 3, h * SEQ:(h + 1) * SEQ]
                    k, c = 2 * (s % 3) + h, t * NA + h * WG + g
                    activate(o, o, ACT.Exp, bias=ngm[:, k:k + 1], scale=HD ** -0.5, accum_out=rsum[:, c:c + 1]).then_inc(scalar_done, A.step(("win", "exp", s) if h else None))
                act.wait_ge(scalar_done, A.now())
                if g == WG - 1:
                    d = dsum[:, t * WH:(t + 1) * WH]
                    activate(d, d, ACT.Exp).then_inc(scalar_done, A.step(("win", "sink", t)))
                    act.wait_ge(scalar_done, A.now())

            for s in range(3):
                diff_exp(s)
            for s in range(len(DIFF)):
                if s < 2:
                    tokens("buv", buv, s)
                elif s < 4:
                    features("cqk", cT2, s - 2, 2)
                if s == 5:
                    root_of("vn", rstd[:, 0:TT])
                probs_T("diff", s, SEQ)
                if s + 3 < len(DIFF):
                    diff_exp(s + 3)
            win_exp(0)
            win_exp(1)
            root_of("diff", hv2)
            for s in range(len(WIN)):
                probs_T("win", s, 2 * SEQ)
                if s + 2 < len(WIN):
                    win_exp(s + 2)
            for g in range(KT // 2):
                act.wait_ge(tensor_done, T.at(A, ("oT", g)))
                ps = bank(A, ("oT", g))
                copy(hT[:, 2 * g:2 * g + 2, :].rearrange("p f n -> p (f n)"), ps).then_inc(scalar_done, A.step(("oTc", g)))
                act.wait_ge(scalar_done, A.now())
                A.also(("read", ("oT", g)))
            rounded_weights(0, None, 0, (0,))
            for t in range(TT):
                sum_squares_of_banks(("post", "mix"), t, lambda t, h: ("wo", t, h), lambda t, h: bank(A, ("wo", t, h)))
            for t in range(TT):
                act.wait_ge(vector_done, V.at(A, ("x", "mix", t)))
                sum_squares(("pre", "ffn"), t, x)
            modulated_T("xT2", "hT2", gcols[:, KT:2 * KT], parts=True)
            act_experts(NF)
            act.wait_ge(scalar_done, A.now())
            for t in range(TT):
                sum_squares_of_banks(("post", "ffn"), t, lambda t, h: (f"dn{t}", NF - 1), lambda t, h: psum[:, 4 + 2 * t + h, :])
            for t in range(TT):
                for h in range(2):
                    act.wait_ge(tensor_done, T.at(A, ("e", t, h)))
                    ps = bank(A, ("e", t, h))
                    copy((e2 if t == 0 else e2b)[:, h * N:(h + 1) * N], ps).then_inc(scalar_done, A.step(("read", ("e", t, h))))
            for t in range(TT):
                act.wait_ge(vector_done, V.at(A, ("x", "ffn", t)))
                sum_squares(("pre", "ple"), t, x)
            modulated_T("xT3", "hT3", gcols[:, 2 * KT:3 * KT])
            for t in range(TT):
                for h in range(2):
                    act.wait_ge(tensor_done, T.at(A, ("pg", t, h)))
                    ps = bank(A, ("pg", t, h))
                    activate(y2[:, t, h * N:(h + 1) * N], ps, ACT.Sigmoid).then_inc(scalar_done, A.step(("sig", t, h)))
                    A.also(("read", ("pg", t, h)))
            for t in range(TT):
                act.wait_ge(vector_done, V.at(A, ("eg", t)))
                sum_squares(("post", "ple"), t, y2)
            A.end()

        @block.scalar
        def _(a):
            act.wait_ge(tensor_done, T.at(A, "c"))
            activate(cact[:, :], psum[:, 0, 0:KT], ACT.Sigmoid).then_inc(scalar_done, A.step("sigc"))
            act.wait_ge(scalar_done, A.now())
            nc.scalar.dma_start(x[:, :, :], token_major(ins["x"].rearrange("a b c -> (a b) c"))).then_inc(x_loaded, 16)
            for dst, src in ((cblock[:, :], ins["c_first"]), (crows[:, :, :], ins["c_rows"]),
                             (wr[:, :, :], by_row(ins["w_router"])), (br[:, :], ins["b_router"].partition_broadcast(P))):
                nc.scalar.dma_start(dst, src).then_inc(tables_loaded, 16)
            for t in range(TT):
                for cos in (0, 1):
                    o = (cosf if cos else sinf)[:, t, HALF:HD]
                    act.wait_ge(vector_done, V.at(A, ("angle", t, cos)))
                    activate(o, o, ACT.Sin).then_inc(scalar_done, A.step("trig" if (t, cos) == (TT - 1, 1) else None))
                    act.wait_ge(scalar_done, A.now())
            with a.Fori(0, DEPTH) as l:
                act_first(l)
            with a.Fori(0, DEPTH) as l:
                act_second(l)

        def load(dst, src, s):
            nc.sync.dma_start(dst, src).then_inc(s, 16)

        def experts_load(ne, gu_src, dn_src, freed_g, then=lambda: None):
            n = NIT[ne]
            b = S.block

            def gu(e, number, wait):
                if wait is not None:
                    sp.wait_ge(wait[0].sem, wait[0].at(S, *wait[1:]))
                gate_w, up_w = gu_src(number)
                g = gslot(b, f"gu{e}")
                s = g_landed[G.slot[b, f"gu{e}"]]
                load(g[:, :, 0:FE], gate_w, s)
                load(g[:, :, FE:2 * FE], up_w, s)

            def dn(e, number, wait):
                if wait is not None:
                    sp.wait_ge(wait[0].sem, wait[0].at(S, *wait[1:]))
                load(dslot(b, f"dn{e}"), dn_src(number), d_landed[DN.slot[b, f"dn{e}"]])

            def used_g(e):
                if e == 0:
                    return (T, ("gu1", 0))
                i, j = divmod(e - 1, 4)
                return (T, ("gu1", "loop", j), i) if i < n else (T, ("gu1", e))

            def used_d(e):
                i, j = divmod(e, 4)
                return (T, ("dn1", "loop", j), i) if i < n else (T, ("dn1", e))

            for e in range(5):
                if e == 4:
                    then()
                gu(e, e, freed_g(e) if e < 4 else used_g(e - 4))
                if e >= 2:
                    dn(e - 2, e - 2, used_d(e - 4) if e >= 4 else None)
            with nc.sync.Fori(0, n - 1) as i:
                for j in range(4):
                    e = 5 + j
                    gu(e, i * 4 + e, (T, ("gu1", "loop", j), i))
                    dn(e - 2, i * 4 + (e - 2), (T, ("dn1", "loop", 0), i + 1) if j == 3 else (T, ("dn1", "loop", j + 1), i))
            for e in range(1 + 4 * n, ne + 2):
                if e < ne:
                    gu(e, e, used_g(e - 4))
                dn(e - 2, e - 2, used_d(e - 4))

        def used_first(name):
            if name.startswith("ada"):
                return (T, (name[:3], int(name[3:]))) if name in ("ada2", "ada3") else (V, ("acc", int(name[3:])))
            if name == "mqk":
                return (T, ("mqk", 1))
            if name == "mvo":
                return (T, "gates")
            if name.startswith("wo"):
                return (T, ("wo", 1, int(name[2:])))
            return (T, (name, 1))

        def used_second(name):
            if name in ("aq", "ak", "cqk", "avcv", "buv"):
                return (T, (name, 1))
            if name.startswith("wo"):
                return (T, ("wo", 1, int(name[2:])))
            e = int(name[2:])
            n = NIT[NF]
            if e == 0:
                return (T, ("gu1", 0))
            i, j = divmod(e - 1, 4)
            return (T, ("gu1", "loop", j), i) if i < n else (T, ("gu1", e))

        def free_slot(b, name):
            c = ORDER[b].index(name)
            if c >= GS:
                sp.wait_ge((used_second if b else used_first)(ORDER[b][c - GS])[0].sem, (used_second if b else used_first)(ORDER[b][c - GS])[0].at(S, *(used_second if b else used_first)(ORDER[b][c - GS])[1:]))
                sp.sem_inc(waited)

        def sp_first(l):
            S.begin(0, l)
            w = layer("w_ada", l)

            def load_ada(c):
                if c >= 4:
                    free_slot(0, f"ada{c}")
                load(gslot(0, f"ada{c}")[:, :, 0:N], by_row(w[:, c * N:(c + 1) * N]), g_landed[G.slot[0, f"ada{c}"]])

            sp.wait_ge(tensor_done, T.last_pass(S, ("gu1", "loop", (NE - 5) % 4), NIT[NE] - 1))
            sp.sem_inc(waited)
            load(brow[0:ADA, :], layer("b_ada", l).rearrange("(c n) -> c n", n=N), bias_loaded)
            load_ada(2)
            for c, e in ((3, NE - 3), (0, NE - 2), (1, NE - 1)):
                sp.wait_ge(tensor_done, T.last_pass(S, ("gu1", e)))
                sp.sem_inc(waited)
                load_ada(c)
            load(ibias[0:NR], layer("i_bias", l).rearrange("(h a) -> h a", a=1), params_loaded)
            load(fbias[0:NR], layer("f_bias", l).rearrange("(h a) -> h a", a=1), params_loaded)
            cw = layer("conv_w", l).rearrange("j (b p) -> p b j", p=P)
            with nc.allow_non_contiguous_dma("one column of taps per channel"):
                for b in range(4):
                    load(convw[:, b, 0:CONV], cw[:, b, :], params_loaded)
                load(convw[:, :, CONV:CONV + 1], layer("conv_b", l).rearrange("(b p a) -> p b a", p=P, a=1), params_loaded)
            wi = layer("w_in", l)
            wo = layer("w_out", l)
            for name in ORDER[0][GS:ORDER[0].index("gu0")]:
                if name == "wo0":
                    sp.wait_ge(vector_done, V.before(S))
                    sp.sem_inc(waited)
                    load(rows[:, 0, :], layer("ln_mix_g", l).partition_broadcast(P), gains_loaded)
                    load(rows[:, 1, :], layer("ln_mix_b", l).partition_broadcast(P), gains_loaded)
                if name in CHUNKS1:
                    free_slot(0, name)
                    c0, c1 = CHUNKS1[name]
                    load(gslot(0, name)[:, :, 0:c1 - c0], by_row(wi[:, c0:c1]), g_landed[G.slot[0, name]])
                elif name.startswith("wo"):
                    free_slot(0, name)
                    h = int(name[2:])
                    load(gslot(0, name)[:, :, 0:N], by_row(wo[:, h * N:(h + 1) * N]), g_landed[G.slot[0, name]])
                else:
                    load_ada(int(name[3:]))

            def gain_rows():
                sp.wait_ge(vector_done, V.at(S, "ln1"))
                sp.sem_inc(waited)
                load(rows[:, 0, :], layer("ln_ffn_g", l).partition_broadcast(P), rows_loaded)
                load(rows[:, 1, :], layer("ln_ffn_b", l).partition_broadcast(P), rows_loaded)

            def expert(name, e):
                a = ins[name][bass.ds(l, 1), bass.ds(e, 1)]
                return by_row(a.rearrange("a b c d -> (a b c) d"))

            experts_load(NE, lambda e: (expert("w_gate", e), expert("w_up", e)), lambda e: expert("w_down", e),
                         lambda e: used_first(ORDER[0][ORDER[0].index(f"gu{e}") - GS]), gain_rows)
            S.end()

        def sp_second(l):
            S.begin(1, l)
            sp.wait_ge(tensor_done, T.before(S) - 3)
            sp.sem_inc(waited)
            for n, name in enumerate(("g_pre_mix_2", "g_pre_ffn_2", "g_ple_gate_2")):
                load(grows[KT * n:KT * (n + 1), :], layer(name, l).rearrange("(k p) -> k p", p=P), params_loaded)
            load(grows[3 * KT:3 * KT + GG, :], layer("b_spatial_2", l), params_loaded)
            for n, name in enumerate(("lam_q1_2", "lam_q2_2", "lam_k1_2", "lam_k2_2")):
                load(lamrow[:, n, :], layer(name, l).partition_broadcast(P), params_loaded)
            load(lamc, layer("c_lam", l).partition_broadcast(P), params_loaded)
            load(subrow, layer("g_diff_sub_2", l).partition_broadcast(P), params_loaded)
            load(wsp, layer("w_spatial_2", l).rearrange("g t s -> t g s"), params_loaded)
            load(prow, token_major(layer("p_2", l).rearrange("a b c -> (a b) c")), params_loaded)
            load(glnrow[:, 0, :], layer("gmlp_ln_g_2", l).partition_broadcast(P), params_loaded)
            load(glnrow[:, 1, :], layer("gmlp_ln_b_2", l).partition_broadcast(P), params_loaded)
            load(sinks, layer("swa_sinks_2", l).partition_broadcast(P), params_loaded)
            wi = layer("w_in_2", l)

            def load_g(name, parts):
                free_slot(1, name)
                for a, c0, n in parts:
                    load(gslot(1, name)[:, :, a:a + n], by_row(wi[:, c0:c0 + n]), g_landed[G.slot[1, name]])

            load_g("aq", [(0, 0, 384)])
            load_g("ak", [(0, 384, 384)])
            sp.wait_ge(tensor_done, T.before(S))
            sp.sem_inc(waited)
            load_g("avcv", [(0, 768, 384), (384, IN2 - P, P)])
            load_g("buv", [(0, 1152, 512)])
            sp.wait_ge(vector_done, V.before(S))
            sp.sem_inc(waited)
            load(rows[:, 0, :], layer("g_post_mix_2", l).partition_broadcast(P), gains_loaded)
            load(rows[:, 1, :], layer("g_post_ffn_2", l).partition_broadcast(P), gains_loaded)
            free_slot(1, "cqk")
            cq = gslot(1, "cqk")
            for g in range(WG):
                for h in range(2):
                    c0 = 1664 + (h * WG + g) * HD
                    load(cq[:, :, (2 * g + h) * HD:(2 * g + h + 1) * HD], by_row(wi[:, c0:c0 + HD]), g_landed[G.slot[1, "cqk"]])
            load(cq[:, :, 384:512], by_row(wi[:, 2048:2176]), g_landed[G.slot[1, "cqk"]])
            wo = layer("w_out_2", l)
            for h in range(2):
                free_slot(1, f"wo{h}")
                load(gslot(1, f"wo{h}")[:, :, 0:N], by_row(wo[:, h * N:(h + 1) * N]), g_landed[G.slot[1, f"wo{h}"]])
            wf, wd = layer("w_ffn_in_2", l), layer("w_ffn_out_2", l)

            def ffn(e):
                if isinstance(e, int):
                    return by_row(wf[:, e * FE:(e + 1) * FE]), by_row(wf[:, DFF + e * FE:DFF + (e + 1) * FE])
                return by_row(wf[:, bass.ds(e * FE, FE)]), by_row(wf[:, bass.ds(e * FE + DFF, FE)])

            def ffn_out(e):
                return by_row(wd[e * FE:(e + 1) * FE, :] if isinstance(e, int) else wd[bass.ds(e * FE, FE), :])

            experts_load(NF, ffn, ffn_out, lambda e: used_second(ORDER[1][ORDER[1].index(f"gu{e}") - GS]))
            sp.wait_ge(tensor_done, T.at(S, ("dn1", NF - 2)))
            load(dslot(1, "up"), by_row(layer("w_ple_up_2", l)), d_landed[DN.slot[1, "up"]])
            wg = layer("w_ple_gate_2", l)
            for h in range(2):
                free_slot(1, f"pg{h}")
                load(gslot(1, f"pg{h}")[:, :, 0:N], by_row(wg[:, h * N:(h + 1) * N]), g_landed[G.slot[1, f"pg{h}"]])
            sp.wait_ge(vector_done, V.at(S, ("x", "mix", TT - 1)))
            load(rows[:, 0, :], layer("g_ple_post_2", l).partition_broadcast(P), rows_loaded)
            S.end()

        @block.sync
        def _(sp):
            load(c8, ins["c"].rearrange("a (k p) -> (a k) p", p=P), start_loaded)
            load(cshared[:, :], ins["c_shared"], start_loaded)
            with nc.allow_non_contiguous_dma("one position per partition"):
                load(posi[:, :], ins["positions"].rearrange("a (t p) -> p (a t)", p=P), start_loaded)
            with sp.Fori(0, DEPTH) as l:
                sp_first(l)
            sp.wait_ge(vector_done, V.at_last("o_cat"))
            load(cblock[:, 0:C2_W], ins["c_second"], const_loaded)
            with sp.Fori(0, DEPTH) as l:
                sp_second(l)
            sp.wait_ge(vector_done, V.total())
            sp.dma_start(token_major(out), x[:, :, :]).then_inc(stored, 16)
            sp.wait_ge(stored, 16)

    return {"T": T.counted(), "V": V.counted(), "A": A.counted()}


_INS = ["x", "c", "positions", "w_ada", "b_ada", "w_in", "i_bias", "f_bias", "conv_w", "conv_b", "w_out", "ln_mix_g",
        "ln_mix_b", "w_router", "b_router", "w_gate", "w_up", "w_down", "ln_ffn_g", "ln_ffn_b", "p_2", "g_pre_mix_2",
        "w_in_2", "lam_q1_2", "lam_k1_2", "lam_q2_2", "lam_k2_2", "g_diff_sub_2", "gmlp_ln_g_2", "gmlp_ln_b_2",
        "w_spatial_2", "b_spatial_2", "swa_sinks_2", "w_out_2", "g_post_mix_2", "g_pre_ffn_2", "w_ffn_in_2",
        "w_ffn_out_2", "g_post_ffn_2", "w_ple_up_2", "w_ple_gate_2", "g_ple_gate_2", "g_ple_post_2"]


def kernel(**inputs):
    import concourse.bacc as _bacc
    from concourse.bass_utils import run_bass_kernel_spmd as _run

    arrays = {f"in_{n}": np.ascontiguousarray(inputs[n]) for n in _INS}
    arrays |= {f"in_{n}": a for n, a in constants().items()}

    def build(known):
        nc = _bacc.Bacc("TRN2", target_bir_lowering=False, num_devices=1)
        ins = {n[3:]: nc.dram_tensor(n, a.shape, mybir.dt.from_np(a.dtype), kind="ExternalInput").ap()
               for n, a in arrays.items()}
        out = nc.dram_tensor("out_x", (SEQ, D), F32, kind="ExternalOutput").ap()
        return nc, program(nc, ins, out, known)

    _, known = build(None)
    nc, _ = build(known)
    r = _run(nc, [arrays], core_ids=[0])
    return r.results[0]["out_x"].reshape(1, SEQ, D)
```
